# Optimizing a Trainium2 kernel written in Bass

```python
import math
import jax, jax.numpy as jnp
from jax import lax
import numpy as np

D_MODEL = 1024
BATCH = 1
SEQ = 512
DEPTH = 2

N_MEM = 256
N_MIXERS = 2
N_A = (DEPTH + 1) // 2
N_B = DEPTH // 2
MIX_WIDTH = D_MODEL
MEM_HEADS = 4
MEM_HEAD_DIM = MIX_WIDTH // 4 // MEM_HEADS
MEM_WIDTH = MEM_HEADS * MEM_HEAD_DIM
MIXER_WIDTH = MIX_WIDTH - MEM_WIDTH

GLA_HEADS = 4
GLA_DV = MIXER_WIDTH // GLA_HEADS
GLA_DK = GLA_DV // 2
GLA_HK = GLA_HEADS * GLA_DK
GLA_GATE_RANK = 16
GLA_GATE_TAU = 16.0
GLA_CHUNK = 64
GLA_IN = 2 * GLA_HK + MIXER_WIDTH + GLA_GATE_RANK + MEM_WIDTH + MIX_WIDTH

DIL_GROUPS = ((128, 1), (512, 4), (2048, 16))
DIL_HEADS = 6
DIL_HEAD_DIM = MIXER_WIDTH // DIL_HEADS
DIL_IN = len(DIL_GROUPS) * 3 * MIXER_WIDTH + MEM_WIDTH + MIX_WIDTH

ROPE_THETA = 500000.0
ROPE_DIM = DIL_HEAD_DIM // 4
NORM_EPS = 1e-6


def rmsnorm(x, w):
    xf = x.astype(jnp.float32)
    y = xf * lax.rsqrt(jnp.mean(xf * xf, axis=-1, keepdims=True) + NORM_EPS)
    return (y * w.astype(jnp.float32)).astype(x.dtype)

def partial_rope(x, pos):
    half = ROPE_DIM // 2
    inv = ROPE_THETA ** (-jnp.arange(half, dtype=jnp.float32) / half)
    ang = pos.astype(jnp.float32)[:, None] * inv[None, :]
    cos = jnp.cos(ang)[None, :, None, :]
    sin = jnp.sin(ang)[None, :, None, :]
    xr = x[..., :ROPE_DIM].astype(jnp.float32)
    x1, x2 = xr[..., :half], xr[..., half:]
    rot = jnp.concatenate([x1 * cos - x2 * sin, x1 * sin + x2 * cos], axis=-1).astype(x.dtype)
    return jnp.concatenate([rot, x[..., ROPE_DIM:]], axis=-1)

def memory_attention(q, mem_n, w_memkv):
    B, T, _ = q.shape
    kv = mem_n @ w_memkv
    k, v = jnp.split(kv, 2, axis=-1)
    q = q.reshape(B, T, MEM_HEADS, MEM_HEAD_DIM)
    k = k.reshape(B, N_MEM, MEM_HEADS, MEM_HEAD_DIM)
    v = v.reshape(B, N_MEM, MEM_HEADS, MEM_HEAD_DIM)
    s = jnp.einsum('bthd,bnhd->bhtn', q, k).astype(jnp.float32) * (MEM_HEAD_DIM ** -0.5)
    p = jax.nn.softmax(s, axis=-1).astype(v.dtype)
    o = jnp.einsum('bhtn,bnhd->bthd', p, v)
    return o.reshape(B, T, MEM_WIDTH)

def gla_chunked(q, k, v, log_a):
    B, T, H, Dk = q.shape
    Dv = v.shape[-1]
    C = GLA_CHUNK
    N = T // C
    f32 = jnp.float32
    q = (q.astype(f32) * (Dk ** -0.5)).reshape(B, N, C, H, Dk)
    k = k.astype(f32).reshape(B, N, C, H, Dk)
    v = v.astype(f32).reshape(B, N, C, H, Dv)
    b = jnp.cumsum(log_a.astype(f32).reshape(B, N, C, H, Dk), axis=2)
    b_last = b[:, :, -1:]
    q_in = q * jnp.exp(b)
    k_in = k * jnp.exp(-b)
    k_out = k * jnp.exp(b_last - b)
    A = jnp.einsum('bnihd,bnjhd->bnhij', q_in, k_in)
    causal = jnp.tril(jnp.ones((C, C), dtype=bool))
    A = jnp.where(causal, A, 0.0)
    o_intra = jnp.einsum('bnhij,bnjhe->bnihe', A, v)
    dS = jnp.einsum('bnjhd,bnjhe->nbhde', k_out, v)
    decay = jnp.exp(b_last[:, :, 0]).transpose(1, 0, 2, 3)

    def step(S, inp):
        dS_c, dec_c = inp
        return dec_c[..., None] * S + dS_c, S

    S0 = jnp.zeros((B, H, Dk, Dv), f32)
    _, S_prev = lax.scan(step, S0, (dS, decay))
    o_inter = jnp.einsum('bnihd,nbhde->bnihe', q_in, S_prev)
    return (o_intra + o_inter).reshape(B, T, H, Dv)

def gla_mixer(h, w_in, w_gate_up, b_gate, gla_norm_w):
    B, T, _ = h.shape
    proj = h @ w_in
    cuts = np.cumsum([GLA_HK, GLA_HK, MIXER_WIDTH, GLA_GATE_RANK, MEM_WIDTH]).tolist()
    q, k, v, g_low, q_mem, gate = jnp.split(proj, cuts, axis=-1)
    log_a = jax.nn.log_sigmoid((g_low @ w_gate_up + b_gate).astype(jnp.float32)) / GLA_GATE_TAU
    o = gla_chunked(q.reshape(B, T, GLA_HEADS, GLA_DK),
                    k.reshape(B, T, GLA_HEADS, GLA_DK),
                    v.reshape(B, T, GLA_HEADS, GLA_DV),
                    log_a.reshape(B, T, GLA_HEADS, GLA_DK))
    o = rmsnorm(o, gla_norm_w).astype(h.dtype).reshape(B, T, MIXER_WIDTH)
    return o, q_mem, gate

def dilated_group(q, k, v, window, dilation):
    B, T, H, Dh = q.shape
    r = dilation
    n = window // dilation
    L = T // r
    nb = -(-L // n)
    Lp = nb * n

    def phase_blocks(x):
        x = x.reshape(B, L, r, H, Dh).transpose(0, 2, 3, 1, 4)
        x = jnp.pad(x, ((0, 0), (0, 0), (0, 0), (0, Lp - L), (0, 0)))
        return x.reshape(B, r, H, nb, n, Dh)

    def with_prev(x):
        prev = jnp.pad(x, ((0, 0), (0, 0), (0, 0), (1, 0), (0, 0), (0, 0)))[:, :, :, :-1]
        return jnp.concatenate([prev, x], axis=4)

    qb = phase_blocks(q)
    kw = with_prev(phase_blocks(k))
    vw = with_prev(phase_blocks(v))
    s = jnp.einsum('bphjqd,bphjkd->bphjqk', qb, kw).astype(jnp.float32) * (Dh ** -0.5)
    qi = jnp.arange(n)[:, None] + n
    ki = jnp.arange(2 * n)[None, :]
    dist = qi - ki
    key_abs = jnp.arange(nb)[:, None, None] * n + ki[None] - n
    mask = (dist >= 0)[None] & (dist <= n)[None] & (key_abs >= 0)
    s = jnp.where(mask, s, -jnp.inf)
    m = jnp.max(s, axis=-1, keepdims=True)
    p = jnp.exp(s - m)
    den = jnp.sum(p, axis=-1, keepdims=True)
    o = jnp.einsum('bphjqk,bphjkd->bphjqd', (p / den).astype(v.dtype), vw)
    lse = (m + jnp.log(den))[..., 0]
    o = o.reshape(B, r, H, Lp, Dh)[:, :, :, :L].transpose(0, 3, 1, 2, 4).reshape(B, T, H, Dh)
    lse = lse.reshape(B, r, H, Lp)[..., :L].transpose(0, 3, 1, 2).reshape(B, T, H)
    return o, lse

def dilated_mixer(h, w_in):
    B, T, _ = h.shape
    pos = jnp.arange(T)
    outs, lses = [], []
    for g, (window, dil) in enumerate(DIL_GROUPS):
        base = g * 3 * MIXER_WIDTH
        qkv = (h @ w_in[:, base:base + 3 * MIXER_WIDTH]).reshape(B, T, 3, DIL_HEADS, DIL_HEAD_DIM)
        q = partial_rope(qkv[:, :, 0], pos)
        k = partial_rope(qkv[:, :, 1], pos)
        o, lse = dilated_group(q, k, qkv[:, :, 2], window, dil)
        outs.append(o)
        lses.append(lse)
    wts = jax.nn.softmax(jnp.stack(lses, axis=0), axis=0)
    o = jnp.einsum('gbth,gbthd->bthd', wts, jnp.stack(outs, axis=0).astype(jnp.float32))
    o = o.astype(h.dtype).reshape(B, T, MIXER_WIDTH)
    rest = h @ w_in[:, len(DIL_GROUPS) * 3 * MIXER_WIDTH:]
    q_mem, gate = jnp.split(rest, [MEM_WIDTH], axis=-1)
    return o, q_mem, gate

def first_inputs(seed: int = 0) -> dict:
    key = jax.random.key(seed)
    ks = jax.random.split(key, 16)
    f32 = jnp.float32
    nrm = lambda k, shape, scale: jax.random.normal(k, shape, f32) * scale
    return {
        "x": nrm(ks[0], (BATCH, SEQ, D_MODEL), 1.0),
        "mem": nrm(ks[1], (BATCH, N_MEM, D_MODEL), 1.0),
        "mem_norm_w": 1.0 + nrm(ks[2], (D_MODEL,), 0.02),
        "norm_w": 1.0 + nrm(ks[3], (DEPTH, D_MODEL), 0.02),
        "w_memkv": nrm(ks[4], (DEPTH, D_MODEL, 2 * MEM_WIDTH), D_MODEL ** -0.5),
        "w_out": nrm(ks[5], (DEPTH, MIX_WIDTH, D_MODEL), MIX_WIDTH ** -0.5),
        "w_in_a": nrm(ks[6], (N_A, D_MODEL, GLA_IN), D_MODEL ** -0.5),
        "w_gate_up": nrm(ks[7], (N_A, GLA_GATE_RANK, GLA_HK), GLA_GATE_RANK ** -0.5),
        "b_gate": nrm(ks[8], (N_A, GLA_HK), 0.1),
        "gla_norm_w": 1.0 + nrm(ks[9], (N_A, GLA_DV), 0.02),
        "w_in_b": nrm(ks[10], (N_B, D_MODEL, DIL_IN), D_MODEL ** -0.5),
        "final_norm_w": 1.0 + nrm(ks[11], (D_MODEL,), 0.02),
    }

def first_block(x, mem, mem_norm_w, norm_w, w_memkv, w_out, w_in_a, w_gate_up, b_gate,
              gla_norm_w, w_in_b, final_norm_w):
    mem_n = rmsnorm(mem, mem_norm_w)
    for i in range(DEPTH):
        h = rmsnorm(x, norm_w[i])
        j = i // N_MIXERS
        if i % N_MIXERS == 0:
            mix, q_mem, gate = gla_mixer(h, w_in_a[j], w_gate_up[j], b_gate[j], gla_norm_w[j])
        else:
            mix, q_mem, gate = dilated_mixer(h, w_in_b[j])
        mem_o = memory_attention(q_mem, mem_n, w_memkv[i])
        branch = jnp.concatenate([mix, mem_o], axis=-1) * jax.nn.silu(gate)
        x = x + branch @ w_out[i]
    return rmsnorm(x, final_norm_w)


CTX_LEN = 256
GRID_W = 64
HG_WIDTH = D_MODEL // 2
HG_DIM = 128
HG_HEADS = HG_WIDTH // HG_DIM
CHUNK = 64
DA_WIDTH = D_MODEL // 4
DA_HEADS = 4
DA_V = DA_WIDTH // DA_HEADS
DA_QK = DA_V // 2
DA_QK_WIDTH = DA_HEADS * 2 * DA_QK
Q_BLOCK = 128
ROPE_THETA_2 = 10000.0
ROPE_AXIS_DIM = DA_QK // 2
FT_WIDTH = D_MODEL // 4
FT_GROUPS = 4
MIX_WIDTH_2 = HG_WIDTH + DA_WIDTH + FT_WIDTH
IN_SPLITS = (HG_WIDTH, HG_WIDTH, HG_WIDTH, HG_WIDTH, HG_WIDTH, DA_QK_WIDTH, DA_QK_WIDTH, DA_WIDTH, FT_WIDTH)
IN_WIDTH = sum(IN_SPLITS)
FF_HIDDEN = ((8 * D_MODEL // 3 + 255) // 256) * 256
N_MOD = 6
EPS = 1e-6


def rms_norm(x, g):
    xf = x.astype(jnp.float32)
    y = xf * lax.rsqrt(jnp.mean(xf * xf, axis=-1, keepdims=True) + EPS)
    return (y * g.astype(jnp.float32)).astype(x.dtype)

def adaln(x, g, shift, scale):
    return rms_norm(x, g) * (1 + scale) + shift

def modulation(cond, w, b):
    return jnp.split(jax.nn.silu(cond) @ w + b, N_MOD, axis=-1)

def split_heads(a, h):
    return a.reshape(a.shape[:-1] + (h, a.shape[-1] // h))

def split_projection(p):
    offsets = [int(o) for o in np.cumsum(IN_SPLITS)[:-1]]
    return jnp.split(p, offsets, axis=-1)

def axial_rope(t_len):
    n_rows = t_len // GRID_W
    rows = jnp.broadcast_to(jnp.arange(n_rows)[:, None], (n_rows, GRID_W)).reshape(-1)
    cols = jnp.broadcast_to(jnp.arange(GRID_W)[None, :], (n_rows, GRID_W)).reshape(-1)
    inv_freq = 1.0 / (ROPE_THETA_2 ** (jnp.arange(0, ROPE_AXIS_DIM, 2, dtype=jnp.float32) / ROPE_AXIS_DIM))
    ang = jnp.stack([rows, cols], axis=-1).astype(jnp.float32)[:, :, None] * inv_freq
    return jnp.cos(ang), jnp.sin(ang)

def apply_rope(x, cos, sin):
    xs = x.reshape(x.shape[:-1] + (2, 2, ROPE_AXIS_DIM // 2)).astype(jnp.float32)
    cs, sn = cos[None, :, None, None], sin[None, :, None, None]
    x1, x2 = xs[..., 0, :], xs[..., 1, :]
    out = jnp.stack([x1 * cs - x2 * sn, x2 * cs + x1 * sn], axis=-2)
    return out.reshape(x.shape).astype(x.dtype)

def gla_chunkwise(q, k, v, log_f, s0):
    b_, t_, h_, _ = q.shape
    dv = v.shape[-1]
    n = t_ // CHUNK

    def chunks(a):
        return a.astype(jnp.float32).reshape(b_, n, CHUNK, h_, a.shape[-1]).transpose(1, 0, 3, 2, 4)

    incl = jnp.tril(jnp.ones((CHUNK, CHUNK), dtype=bool))[:, :, None]

    def step(state, inp):
        qi, ki, vi, gi = inp
        bcum = jnp.cumsum(gi, axis=2)
        o_inter = jnp.einsum('bhtk,bhkv->bhtv', qi * jnp.exp(bcum), state)
        rel = bcum[:, :, :, None, :] - bcum[:, :, None, :, :]
        decay = jnp.exp(jnp.where(incl, rel, -jnp.inf))
        scores = jnp.einsum('bhtk,bhsk,bhtsk->bhts', qi, ki, decay)
        o_intra = jnp.einsum('bhts,bhsv->bhtv', scores, vi)
        blast = bcum[:, :, -1:, :]
        state = state * jnp.exp(blast[:, :, 0, :, None]) + jnp.einsum(
            'bhsk,bhsv->bhkv', ki * jnp.exp(blast - bcum), vi)
        return state, o_inter + o_intra

    s_fin, o = lax.scan(step, s0, (chunks(q), chunks(k), chunks(v), chunks(log_f)))
    return o.transpose(1, 0, 3, 2, 4).reshape(b_, t_, h_, dv), s_fin

def hgrn2_scan(q, v, z, lb, s0, reverse):
    f = lb + (1.0 - lb) * jax.nn.sigmoid(z.astype(jnp.float32))
    k = split_heads(1.0 - f, HG_HEADS)
    log_f = split_heads(jnp.log(f), HG_HEADS)
    if reverse:
        q, k, v, log_f = jnp.flip(q, 1), jnp.flip(k, 1), jnp.flip(v, 1), jnp.flip(log_f, 1)
    o, s = gla_chunkwise(q, k, v, log_f, s0)
    if reverse:
        o = jnp.flip(o, 1)
    return o, s

def diff_softmax_attend(q, keys, vals, lam):
    s = jnp.einsum('bqhmd,bkhmd->bhmqk', q, keys).astype(jnp.float32) * (DA_QK ** -0.5)
    p = jax.nn.softmax(s, axis=-1)
    w = p[:, :, 0] - lam * p[:, :, 1]
    return jnp.einsum('bhqk,bkhv->bqhv', w.astype(vals.dtype), vals)

def fourier_mix(u):
    uh = split_heads(u, FT_GROUPS).astype(jnp.float32)
    y = jnp.fft.fft2(uh, axes=(1, 3), norm="ortho").real
    return y.reshape(u.shape).astype(u.dtype)

def mixer(hl, hc, w_in, w_out, lb_f, lb_b, hg_onorm, da_lam, da_subln, lam_init, cos, sin, with_ctx):
    pl = split_projection(hl @ w_in)
    pc = split_projection(hc @ w_in)
    bsz, t_lat = hl.shape[0], hl.shape[1]

    s0 = jnp.zeros((bsz, HG_HEADS, HG_DIM, HG_DIM), jnp.float32)
    q_c, v_c = split_heads(jax.nn.silu(pc[0]), HG_HEADS), split_heads(pc[1], HG_HEADS)
    q_l, v_l = split_heads(jax.nn.silu(pl[0]), HG_HEADS), split_heads(pl[1], HG_HEADS)
    oc_f, st_f = hgrn2_scan(q_c, v_c, pc[3], lb_f, s0, False)
    oc_b, st_b = hgrn2_scan(q_c, v_c, pc[4], lb_b, s0, True)
    ol_f, _ = hgrn2_scan(q_l, v_l, pl[3], lb_f, st_f, False)
    ol_b, _ = hgrn2_scan(q_l, v_l, pl[4], lb_b, st_b, True)

    def hgrn_out(o, g):
        return (rms_norm(o, hg_onorm).reshape(g.shape) * jax.nn.silu(g)).astype(g.dtype)

    def qk_heads(a):
        return a.reshape(a.shape[:-1] + (DA_HEADS, 2, DA_QK))

    lam_f = da_lam.astype(jnp.float32)
    lam = jnp.exp(jnp.sum(lam_f[0] * lam_f[1])) - jnp.exp(jnp.sum(lam_f[2] * lam_f[3])) + lam_init
    dq_l, dk_l = apply_rope(qk_heads(pl[5]), cos, sin), apply_rope(qk_heads(pl[6]), cos, sin)
    dv_l = split_heads(pl[7], DA_HEADS)
    dq_c, dk_c, dv_c = qk_heads(pc[5]), qk_heads(pc[6]), split_heads(pc[7], DA_HEADS)
    keys = jnp.concatenate([dk_l, dk_c], axis=1)
    vals = jnp.concatenate([dv_l, dv_c], axis=1)
    nb = t_lat // Q_BLOCK
    qb = dq_l.reshape((bsz, nb, Q_BLOCK) + dq_l.shape[2:]).transpose(1, 0, 2, 3, 4, 5)
    od_l = lax.map(lambda qq: diff_softmax_attend(qq, keys, vals, lam), qb)
    od_l = od_l.transpose(1, 0, 2, 3, 4).reshape(bsz, t_lat, DA_HEADS, DA_V)

    def diff_out(o):
        return (rms_norm(o, da_subln) * (1.0 - lam_init)).reshape(o.shape[:2] + (DA_WIDTH,))

    yl = jnp.concatenate([hgrn_out(ol_f + ol_b, pl[2]), diff_out(od_l).astype(hl.dtype),
                          fourier_mix(pl[8])], axis=-1) @ w_out
    if not with_ctx:
        return yl, None
    od_c = diff_softmax_attend(dq_c, dk_c, dv_c, lam)
    yc = jnp.concatenate([hgrn_out(oc_f + oc_b, pc[2]), diff_out(od_c).astype(hc.dtype),
                          fourier_mix(pc[8])], axis=-1) @ w_out
    return yl, yc

def swiglu(h, w_i, w_o):
    g, u = jnp.split(h @ w_i, 2, axis=-1)
    return (jax.nn.silu(g) * u) @ w_o

def second_inputs(seed: int = 0) -> dict:
    key = jax.random.key(seed)
    ks = jax.random.split(key, 15)
    f32 = jnp.float32
    nrm = lambda k, s: jax.random.normal(k, s, f32)
    return {
        "x": nrm(ks[0], (BATCH, SEQ, D_MODEL)),
        "c": nrm(ks[1], (BATCH, D_MODEL)),
        "ctx": nrm(ks[2], (BATCH, CTX_LEN, D_MODEL)),
        "c_ctx": nrm(ks[3], (D_MODEL,)),
        "w_mod": nrm(ks[4], (DEPTH, D_MODEL, N_MOD * D_MODEL)) * (0.5 * D_MODEL ** -0.5),
        "b_mod": nrm(ks[5], (DEPTH, N_MOD * D_MODEL)) * 0.01,
        "norm_g": 1.0 + 0.02 * nrm(ks[6], (DEPTH, 4, D_MODEL)),
        "w_in": nrm(ks[7], (DEPTH, D_MODEL, IN_WIDTH)) * D_MODEL ** -0.5,
        "w_out": nrm(ks[8], (DEPTH, MIX_WIDTH_2, D_MODEL)) * MIX_WIDTH_2 ** -0.5,
        "hg_lb_logits": 0.1 * nrm(ks[9], (2, DEPTH, HG_WIDTH)),
        "hg_onorm": 1.0 + 0.02 * nrm(ks[10], (DEPTH, HG_DIM)),
        "da_lambda": 0.1 * nrm(ks[11], (DEPTH, 4, DA_QK)),
        "da_subln": 1.0 + 0.02 * nrm(ks[12], (DEPTH, DA_V)),
        "w_ffn_in": nrm(ks[13], (DEPTH, D_MODEL, 2 * FF_HIDDEN)) * D_MODEL ** -0.5,
        "w_ffn_out": nrm(ks[14], (DEPTH, FF_HIDDEN, D_MODEL)) * FF_HIDDEN ** -0.5,
    }

def second_block(x, c, ctx, c_ctx, w_mod, b_mod, norm_g, w_in, w_out, hg_lb_logits, hg_onorm,
              da_lambda, da_subln, w_ffn_in, w_ffn_out):
    cos, sin = axial_rope(x.shape[1])
    lb_p = jax.nn.softmax(hg_lb_logits.astype(jnp.float32), axis=1)
    lower_bounds = jnp.cumsum(lb_p, axis=1) - lb_p[:, :1]
    xl, xc = x, ctx
    for l in range(DEPTH):
        with_ctx = l < DEPTH - 1
        lam_init = 0.8 - 0.6 * math.exp(-0.3 * l)
        ml = modulation(c[:, None, :], w_mod[l], b_mod[l])
        mc = modulation(c_ctx[None, None, :], w_mod[l], b_mod[l])
        g = norm_g[l]
        hl = adaln(xl, g[0], ml[0], ml[1])
        hc = adaln(xc, g[0], mc[0], mc[1])
        yl, yc = mixer(hl, hc, w_in[l], w_out[l], lower_bounds[0, l], lower_bounds[1, l], hg_onorm[l],
                       da_lambda[l], da_subln[l], lam_init, cos, sin, with_ctx)
        xl = xl + ml[2] * rms_norm(yl, g[1])
        xl = xl + ml[5] * rms_norm(swiglu(adaln(xl, g[2], ml[3], ml[4]), w_ffn_in[l], w_ffn_out[l]), g[3])
        if with_ctx:
            xc = xc + mc[2] * rms_norm(yc, g[1])
            xc = xc + mc[5] * rms_norm(swiglu(adaln(xc, g[2], mc[3], mc[4]), w_ffn_in[l], w_ffn_out[l]), g[3])
    return xl


def setup_inputs(seed=0):
    out = dict(first_inputs(seed))
    for name, value in second_inputs(seed + 1).items():
        if name != "x":
            out[name + "_2"] = value
    return out


def reference(
    x, mem, mem_norm_w, norm_w, w_memkv, w_out, w_in_a, w_gate_up, b_gate, gla_norm_w, w_in_b,
    final_norm_w, c_2, ctx_2, c_ctx_2, w_mod_2, b_mod_2, norm_g_2, w_in_2, w_out_2,
    hg_lb_logits_2, hg_onorm_2, da_lambda_2, da_subln_2, w_ffn_in_2, w_ffn_out_2,
):
    x = first_block(
        x, mem, mem_norm_w, norm_w, w_memkv, w_out, w_in_a, w_gate_up, b_gate, gla_norm_w,
        w_in_b, final_norm_w,
    )
    return second_block(
        x, c_2, ctx_2, c_ctx_2, w_mod_2, b_mod_2, norm_g_2, w_in_2, w_out_2, hg_lb_logits_2,
        hg_onorm_2, da_lambda_2, da_subln_2, w_ffn_in_2, w_ffn_out_2,
    )


_drawn_inputs = setup_inputs


def setup_inputs(seed=0):
    import zlib

    import numpy as np

    out = dict(_drawn_inputs(seed))
    spreads = {}
    factors = {'mem_norm_w': 8.0,
     'norm_w': 2.813,
     'b_gate': 2.694,
     'gla_norm_w': 5.505,
     'norm_g_2': 3.02,
     'hg_lb_logits_2': 8.0,
     'hg_onorm_2': 8.0,
     'da_subln_2': 8.0}
    for name, (base, spread) in spreads.items():
        noise = np.random.default_rng([zlib.crc32(name.encode()), seed]).standard_normal(out[name].shape)
        drawn = base * np.exp(spread * noise) if base else spread * noise
        out[name] = __import__('jax').numpy.asarray(drawn.astype(out[name].dtype))
    for name, factor in factors.items():
        out[name] = (out[name] * factor).astype(out[name].dtype)
    return out
```

```python
import math
from contextlib import ExitStack

import numpy as np
import concourse.bass as bass
from concourse import mybir

F32 = mybir.dt.float32
BF16 = mybir.dt.bfloat16
ALU = mybir.AluOpType
ACT = mybir.ActivationFunctionType
AX = mybir.AxisListType.X
EPS = 1e-6
D = 1024
T = 512
TC = 256
FF = 2816

CONST_WIDTHS = [("ident", 128), ("ones", 128), ("reset", 768), ("eps", 8), ("drope", 128), ("arope", 128),
                ("cs64", 256), ("dil", 1280)]
CW = {}
_o = 0
for _n, _w in CONST_WIDTHS:
    CW[_n] = (_o, _o + _w)
    _o += _w
CTOT = _o
CBASE = CW["dil"][0]
VROWS = [("mem_norm", 8), ("norm", 16), ("norm_g", 64), ("hg_onorm", 2), ("hg_lb", 16), ("c", 8), ("c_ctx", 8)]
VO = {}
_o = 0
for _n, _w in VROWS:
    VO[_n] = _o
    _o += _w
VTOT = _o


def shape_tables():
    c = np.zeros((128, CTOT), np.float32)
    p = np.arange(128)

    def put(name, a):
        lo, hi = CW[name]
        c[:, lo:hi] = np.asarray(a, np.float32).reshape(128, hi - lo)

    put("ident", np.eye(128))
    put("ones", np.ones((128, 128)))
    r = np.ones((128, 768))
    r[:, ::128] = 0
    put("reset", r)
    r = np.ones((128, 768))
    e = np.zeros((128, 8))
    e[:, 0] = EPS
    e[:, 1] = 1.0
    put("eps", e)
    t = p[:, None] + 128 * np.arange(4)[None, :]
    inv = 500000.0 ** (-np.arange(16) / 16.0)
    ang = (t[:, :, None].astype(np.float32) * inv.astype(np.float32)[None, None, :]).astype(np.float32)
    put("drope", np.stack([np.cos(ang), np.sin(ang)], 1))
    invf = (1.0 / (10000.0 ** (np.arange(0, 16, 2) / 16.0))).astype(np.float32)
    rc = np.stack([t // 64, t % 64], -1).astype(np.float32)
    ang = rc[:, :, :, None] * invf[None, None, None, :]
    put("arope", np.stack([np.cos(ang), np.sin(ang)], 1))
    k = np.arange(64)
    a64 = 2 * np.pi * ((k[:, None] * k[None, :]) % 64) / 64
    z = np.zeros((128, 256))
    for b in range(2):
        z[64 * b:64 * b + 64, 64 * b:64 * b + 64] = np.cos(a64)
        z[64 * b:64 * b + 64, 128 + 64 * b:128 + 64 * b + 64] = -np.sin(a64)
    put("cs64", z)
    s, q = p[:, None], p[None, :]
    lv = np.zeros((128, 2, 8, 128))
    for l in range(7):
        h = 64 >> l
        same = (s // (2 * h)) == (q // (2 * h))
        lv[:, 0, l] = same & (s % (2 * h) < h) & (q % (2 * h) >= h)
        lv[:, 1, l] = same & (s % (2 * h) >= h) & (q % (2 * h) < h)
    lv[:, :, 7] = np.eye(128)[:, None, :]
    neg = -1e30
    qq, ss = p[:, None], p[None, :]
    g0 = np.concatenate([np.where(ss >= qq, 0, neg), np.where(ss <= qq, 0, neg)], 1)
    out = [g0]
    for r in (4, 16):
        off = np.where((qq - ss) % r == 0, 0, neg)
        dg = np.where(((qq - ss) % r == 0) & (ss <= qq), 0, neg)
        out.append(np.concatenate([off, off, off, dg], 1))
    put("dil", np.concatenate(out, 1))

    def dft(n):
        j = np.arange(n)
        a = 2 * np.pi * ((j[:, None] * j[None, :]) % n) / n
        w = np.stack([np.cos(a), np.sin(a)]) / np.sqrt(n * 64.0)
        return w.reshape(2, n // 128, 128, n).transpose(2, 0, 1, 3).reshape(128, -1).astype(np.float32)

    bits = lv.reshape(128, 2048).astype(np.uint16) * np.uint16(0x3F80)
    return c, dft(T), dft(TC), bits


def flat(x):
    if x is None:
        return []
    if isinstance(x, tuple) and len(x) == 2 and isinstance(x[1], int):
        return [x]
    out = []
    for y in x:
        out += flat(y)
    return out


class Lane:

    def __init__(self, e, sem):
        self.e, self.sem, self.n, self.seen = e, sem, 0, {}

    def wait(self, *points):
        for sem, value in flat(points):
            if self.seen.get(id(sem), 0) < value:
                self.seen[id(sem)] = value
                self.e.wait_ge(sem, value)

    def do(self, fn, *after):
        self.wait(*after)
        self.n += 1
        fn(self.e).then_inc(self.sem, 1)
        return (self.sem, self.n)

    def dma(self, slot, out, in_, *after):
        self.wait(slot.freed, *after)
        slot.n += 16
        self.e.dma_start(out, in_).then_inc(slot.sem, 16)
        return (slot.sem, slot.n)


class Slot:

    def __init__(self, ap, sem=None):
        self.ap, self.sem, self.n, self.freed = ap, sem, 0, []

    @property
    def freed(self):
        return self._freed

    @freed.setter
    def freed(self, points):
        self._freed, self.busy = points, False


class Ring:
    def __init__(self, slots):
        self.slots, self.i = slots, 0

    def full(self):
        return self.slots[self.i % len(self.slots)].busy

    def next(self):
        s = self.slots[self.i % len(self.slots)]
        assert not s.busy
        s.busy = True
        self.i += 1
        return s


def interleave(jobs, width):
    live, jobs = [], list(jobs)
    while live or jobs:
        while jobs and len(live) < width:
            live.append(jobs.pop(0))
        for j in list(live):
            try:
                next(j)
            except StopIteration:
                live.remove(j)


def build(nc, A, out, dump=None):
    with ExitStack() as ctx:
        total = [0]

        def sb(name, cols):
            total[0] += cols * 4
            return ctx.enter_context(nc.sbuf_tensor(name, [128, cols], F32))[:, :]

        def sem(name):
            return ctx.enter_context(nc.semaphore(name))

        PS = ctx.enter_context(nc.psum_tensor("PS", [128, 8, 512], F32))[:, :, :]
        pe, act, dve, pool, sp = (Lane(e, sem(f"s_{n}")) for e, n in (
            (nc.tensor, "pe"), (nc.scalar, "act"), (nc.vector, "dve"), (nc.gpsimd, "pool"), (nc.sync, "sp")))
        compute = [pe, act, dve, pool]

        CON = sb("CON", CBASE)
        VEC = sb("VEC", VTOT)
        BMOD = sb("BMOD", 96)
        MOD = sb("MOD", 2 * 96)
        MISC = sb("MISC", 128)
        STAT = sb("STAT", 64 * 8)
        X = sb("X", 4096)
        XC = sb("XC", 2048)
        HT = sb("HT", 8 * 768)
        WR = sb("WR", 3 * 4096)
        HNB = sb("HNB", 1024)
        ARN = 53150 - total[0] // 4
        AR = sb("AR", ARN)

        def con(name):
            lo, hi = CW[name]
            return CON[:, lo:hi]

        ident = con("ident")
        ones = con("ones")
        eps = con("eps")[:, 0:1]
        wring = Ring([Slot(WR[:, 4096 * i:4096 * (i + 1)], sem(f"s_w{i}")) for i in range(3)])
        stats = Ring([Slot(STAT[:, 8 * i:8 * i + 8]) for i in range(64)])
        hns = Ring([Slot(HNB)])
        banks = [Slot(PS[:, b, :]) for b in range(8)]
        misc = Slot(None, sem("s_misc"))
        mslot = Slot(None, sem("s_mask"))

        def bring(*ids):
            return Ring([banks[i] for i in ids])

        def pair(i):
            return Slot(PS[:, i:i + 2, :])

        def barrier():
            points = [(l.sem, l.n) for l in compute]
            for l in compute:
                l.wait(*points)
            return points

        class Arena:
            def __init__(self):
                self.at = 0

            def get(self, cols):
                a = AR[:, self.at:self.at + cols]
                self.at += cols
                assert self.at <= ARN, (self.at, ARN)
                return a

        def evac(n, out_, in_, *after, scale=None):
            if n % 2:
                return act.do(lambda e: e.activation(out_, in_, ACT.Copy, scale=1.0 if scale is None else scale), *after)
            if scale is None:
                return dve.do(lambda e: e.tensor_copy(out_, in_), *after)
            return dve.do(lambda e: e.tensor_scalar(out_, in_, scale, None, ALU.mult), *after)

        def load_w(src, kt, n):
            s = wring.next()
            v = s.ap[:, 0:kt * n].rearrange("p (k n) -> p k n", k=kt)
            src = src if isinstance(src, list) else [(0, n, src)]
            for lo, w, a in src:
                s.ready = sp.dma(s, v[:, :, lo:lo + w], a.rearrange("(k p) n -> p k n", p=128))
            return s, v

        def mm_group(psum, pairs, *after, start=True, stop=True):
            def go(e):
                for i, (l, r) in enumerate(pairs):
                    m = e.matmul(psum, l, r, start=start and i == 0, stop=stop and i == len(pairs) - 1,
                                 skip_group_check=True)
                return m
            return pe.do(go, *after)

        def transposes(bank, ins, *after):
            def go(e):
                for i, a in enumerate(ins):
                    m = e.transpose(bank[0:a.shape[1], 128 * i:128 * i + a.shape[0]], a,
                                    ident[0:a.shape[0], 0:a.shape[0]])
                return m
            return pe.do(go, *after)

        def rstd_of(st, n, count, after):
            t = act.do(lambda e: e.activation(st[:, n:2 * n], st[:, 0:n], ACT.Ln, scale=1.0 / count, bias=eps), after)
            return act.do(lambda e: e.activation(st[:, n:2 * n], st[:, n:2 * n], ACT.Exp, scale=-0.5), t)

        def norm_T(src, dst, col0, g, b, ring, after):
            s, st = hns.next(), stats.next()
            t = act.do(lambda e: e.activation(s.ap, src, ACT.Square, accum_out=st.ap[:, 0:1]), after, s.freed, st.freed)
            t = rstd_of(st.ap, 1, D, t)
            t = dve.do(lambda e: e.tensor_scalar(s.ap, src, st.ap[:, 1:2], None, ALU.mult), t)
            st.freed = t
            done = []
            for hf in range(2):
                bk = ring.next()
                tt = transposes(bk.ap, [s.ap[:, 128 * (4 * hf + k):128 * (4 * hf + k + 1)] for k in range(4)], t, bk.freed)
                o = dst[:, 4 * hf:4 * hf + 4, col0:col0 + 128]
                i3 = bk.ap.rearrange("p (k n) -> p k n", k=4)
                gb = g[:, 4 * hf:4 * hf + 4].unsqueeze(2).broadcast_to([128, 4, 128])
                te = dve.do(lambda e, o=o, i3=i3, gb=gb: e.tensor_tensor(o, i3, gb, ALU.mult), tt)
                bk.freed = te
                if b is not None:
                    bb = b[:, 4 * hf:4 * hf + 4].unsqueeze(2).broadcast_to([128, 4, 128])
                    te = dve.do(lambda e, o=o, bb=bb: e.tensor_tensor(o, o, bb, ALU.add), te)
                done.append(te)
            s.freed = tt
            return done

        def lin_tok(act_k, tiles, w, wv, c0, n, ring, consume, after):
            K = wv.shape[1]
            for i in tiles:
                bk = ring.next()
                t = mm_group(bk.ap[:, 0:n], [(act_k(k)[:, 128 * i:128 * i + 128], wv[:, k, c0:c0 + n]) for k in range(K)],
                             w.ready, after, bk.freed)
                bk.freed = consume(i, bk.ap[:, 0:n], t)
            w.freed = [t]

        def lin_feat(act_k, spans, w, wv, c0, m, ring, consume, after):
            K = wv.shape[1]
            for lo, hi in spans:
                bk = ring.next()
                p = bk.ap[0:m, 0:hi - lo]
                t = mm_group(p, [(wv[:, k, c0:c0 + m], act_k(k)[:, lo:hi]) for k in range(K)], w.ready, after, bk.freed)
                bk.freed = consume(lo, hi, p, t)
            w.freed = [t]

        X3 = X.rearrange("p (i n) -> p i n", i=4)
        XC3 = XC.rearrange("p (i n) -> p i n", i=2)
        HT3 = HT.rearrange("p (k n) -> p k n", k=8)
        hk = lambda k: HT3[:, k, :]

        dumps = []

        def dump_now(name, ap):
            if dump is None:
                return
            pts = barrier()
            s = Slot(None, sem("d_" + name))
            sp.dma(s, dump(name, ap), ap, pts)
            dumps.append((s.sem, s.n))
            for l in compute:
                l.wait((s.sem, s.n))

        c0t = sp.dma(misc, CON, A["k_const"][:, 0:CBASE])
        ar = Arena()
        VR = ar.get(128)
        BR_ = ar.get(128)
        GR = ar.get(256)
        LAMR = ar.get(256)
        FNW = ar.get(1024)
        SC = ar.get(1024)
        rows = {"mem_norm": A["mem_norm_w"].rearrange("(a n) -> a n", n=128),
                "norm": A["norm_w"].rearrange("l (a n) -> (l a) n", n=128),
                "norm_g": A["norm_g_2"].rearrange("l g (a n) -> (l g a) n", n=128),
                "hg_onorm": A["hg_onorm_2"],
                "hg_lb": A["hg_lb_logits_2"].rearrange("d l (a n) -> (d l a) n", n=128),
                "c": A["c_2"].rearrange("o (a n) -> (o a) n", n=128),
                "c_ctx": A["c_ctx_2"].rearrange("(a n) -> a n", n=128)}
        for n_, w_ in VROWS:
            sp.dma(misc, VR[VO[n_]:VO[n_] + w_, :], rows[n_])
        sp.dma(misc, BR_[0:96, :], A["b_mod_2"].rearrange("l (a n) -> (l a) n", n=128))
        sp.dma(misc, GR[0:4, 0:96], A["b_gate"].rearrange("o (a n) -> (o a) n", n=96))
        gw = A["gla_norm_w"]
        sp.dma(misc, GR[0:1, 128:256], gw[:, 0:128])
        sp.dma(misc, GR[1:2, 128:192], gw[:, 128:192])
        sp.dma(misc, GR[1:2, 192:256], gw[:, 0:64])
        sp.dma(misc, GR[2:3, 128:256], gw[:, 64:192])
        sub = A["da_subln_2"]
        for h_ in range(2):
            sp.dma(misc, GR[3:5, 128 + 64 * h_:192 + 64 * h_], sub)
        for l in range(2):
            lm = A["da_lambda_2"][l:l + 1].rearrange("o a n -> o (a n)")
            sp.dma(misc, LAMR[:, 128 * l:128 * l + 128], lm.broadcast_to([128, 128]))
        cready = (misc.sem, misc.n)
        xs = Slot(None, sem("s_x"))
        xready = sp.dma(xs, X3, A["x"].rearrange("o (i p) n -> p (o i) n", p=128))
        xcs = Slot(None, sem("s_xc"))
        xcready = sp.dma(xcs, XC3, A["ctx_2"].rearrange("o (i p) n -> p (o i) n", p=128))

        b0 = bring(0, 1)
        bk = b0.next()
        t = transposes(bk.ap, [VR[0:VTOT, :], BR_[0:96, :], GR[0:4, 0:96], GR[0:5, 128:256]], cready)
        t1 = dve.do(lambda e: e.tensor_copy(VEC, bk.ap[:, 0:VTOT]), t)
        t2 = dve.do(lambda e: e.tensor_copy(BMOD, bk.ap[:, 128:224]), t)
        t3 = dve.do(lambda e: e.tensor_copy(MISC[0:96, 0:4], bk.ap[0:96, 256:260]), t)
        t4 = dve.do(lambda e: e.tensor_copy(MISC[:, 4:9], bk.ap[:, 384:389]), t)
        bk.freed = [t1, t2, t3, t4]
        NBG, GNW, SUBC = MISC[0:96, 0:4], MISC[:, 4:7], MISC[:, 7:9]
        LIN = [0.8 - 0.6 * math.exp(-0.3 * l) for l in range(2)]
        t5 = [dve.do(lambda e, l=l: e.tensor_scalar(MISC[:, 7 + l:8 + l], MISC[:, 7 + l:8 + l], 1.0 - LIN[l], None, ALU.mult), t4)
              for l in range(2)]
        LB = MISC[:, 9:11]
        for l in range(2):
            a4 = LAMR[:, 128 * l:128 * l + 128].rearrange("p (a n) -> p a n", a=4)
            ta = dve.do(lambda e, a4=a4: e.tensor_tensor(SC[:, 0:64].rearrange("p (a n) -> p a n", a=2),
                                                         a4[:, 0:4:2, :], a4[:, 1:4:2, :], ALU.mult), cready,
                        [(dve.sem, dve.n)])
            ta = dve.do(lambda e: e.tensor_reduce(SC[:, 64:66], SC[:, 0:64].rearrange("p (a n) -> p a n", a=2), AX, ALU.add), ta)
            ta = act.do(lambda e: e.activation(SC[:, 66:68], SC[:, 64:66], ACT.Exp), ta)
            ta = dve.do(lambda e: e.tensor_tensor(SC[:, 68:69], SC[:, 66:67], SC[:, 67:68], ALU.subtract), ta)
            dve.do(lambda e, l=l: e.tensor_scalar(LB[:, l:l + 1], SC[:, 68:69], LIN[l], None, ALU.add), ta)
        L3 = VEC[:, VO["hg_lb"]:VO["hg_lb"] + 16].rearrange("p (d l a) -> p d l a", d=2, l=2)
        LOW = MISC[:, 16:32].rearrange("p (d l a) -> p d l a", d=2, l=2)
        ONEM = MISC[:, 32:48].rearrange("p (d l a) -> p d l a", d=2, l=2)
        w4 = [SC[:, 128 + 8 * i:136 + 8 * i].rearrange("p (d a) -> p d a", d=2) for i in range(6)]
        ta = dve.do(lambda e: e.tensor_tensor(w4[0], L3[:, :, 0, :], L3[:, :, 1, :], ALU.max), t1)
        tb = dve.do(lambda e: e.tensor_tensor(w4[1], L3[:, :, 0, :], w4[0], ALU.subtract), ta)
        tc_ = dve.do(lambda e: e.tensor_tensor(w4[2], L3[:, :, 1, :], w4[0], ALU.subtract), ta)
        tb = act.do(lambda e: e.activation(w4[1], w4[1], ACT.Exp), tb)
        tc_ = act.do(lambda e: e.activation(w4[2], w4[2], ACT.Exp), tc_)
        ta = dve.do(lambda e: e.tensor_tensor(w4[3], w4[1], w4[2], ALU.add), tb, tc_)
        ta = dve.do(lambda e: e.reciprocal(w4[4], w4[3]), ta)
        tb = dve.do(lambda e: e.tensor_tensor(w4[1], w4[1], w4[4], ALU.mult), ta)
        tc_ = dve.do(lambda e: e.tensor_tensor(w4[2], w4[2], w4[4], ALU.mult), ta)
        dve.do(lambda e: e.tensor_tensor(LOW[:, :, 0, :], w4[1], w4[1], ALU.subtract), tb)
        ta = dve.do(lambda e: e.tensor_tensor(w4[5], w4[1], w4[2], ALU.add), tb, tc_)
        ta = dve.do(lambda e: e.tensor_tensor(LOW[:, :, 1, :], w4[5], w4[1], ALU.subtract), ta)
        dve.do(lambda e: e.tensor_scalar(ONEM, LOW, -1.0, 1.0, ALU.mult, ALU.add), ta)
        CV = MISC[:, 64:80].rearrange("p (k c) -> p k c", c=2)
        for i, n_ in enumerate(("c", "c_ctx")):
            act.do(lambda e, i=i, n_=n_: e.activation(CV[:, :, i], VEC[:, VO[n_]:VO[n_] + 8], ACT.Silu), t1)
        barrier()

        for l in range(2):
            mring, tring = bring(0, 1, 2), bring(4, 5)
            for c in range(12):
                w, wv = load_w(A["w_mod_2"][l][:, 512 * c:512 * c + 512], 8, 512)
                bk = mring.next()
                t = mm_group(bk.ap[0:2, :], [(CV[:, k, :], wv[:, k, :]) for k in range(8)], w.ready, bk.freed)
                w.freed = t
                half = SC[0:2, 512 * (c % 2):512 * (c % 2) + 512]
                tk = tring.next()
                t = dve.do(lambda e, half=half, bk=bk: e.tensor_copy(half, bk.ap[0:2, :]), t, [(pe.sem, tk.pt)] if hasattr(tk, "pt") else [])
                bk.freed = t
                tt = pe.do(lambda e, half=half, tk=tk: [e.transpose(tk.ap[:, 2 * j:2 * j + 2], half[:, 128 * j:128 * j + 128], ident[0:2, 0:2])
                                                        for j in range(4)][-1], t, tk.freed)
                tk.pt = tt[1]
                o = MOD[:, 96 * l + 8 * c:96 * l + 8 * c + 8].rearrange("p (j c) -> p j c", c=2)
                bb = BMOD[:, 48 * l + 4 * c:48 * l + 4 * c + 4].unsqueeze(2).broadcast_to([128, 4, 2])
                tk.freed = dve.do(lambda e, o=o, tk=tk, bb=bb: e.tensor_tensor(o, tk.ap[:, 0:8].rearrange("p (j c) -> p j c", c=2), bb, ALU.add), tt)
        barrier()

        def modcol(l, j, who):
            return MOD[:, 96 * l:96 * l + 96].rearrange("p (j k c) -> p j k c", j=6, k=8)[:, j, :, who]

        ar = Arena()
        KV = ar.get(2 * 1024)
        first_base = ar.at
        MX = ar.get(2048).rearrange("p (i n) -> p i n", i=2)
        ms = Slot(None, sem("s_mem"))
        mready = sp.dma(ms, MX, A["mem"].rearrange("o (i p) n -> p (o i) n", p=128), [(dve.sem, dve.n), (pe.sem, pe.n), (act.sem, act.n)])
        g = VEC[:, VO["mem_norm"]:VO["mem_norm"] + 8]
        th = [norm_T(MX[:, i, :], HT3, 128 * i, g, None, bring(0, 1, 2, 3), mready) for i in range(2)]
        for l in range(2):
            w, wv = load_w(A["w_memkv"][l], 8, 512)
            kT = KV[:, 1024 * l:1024 * l + 512].rearrange("p (f n) -> p f n", f=2)
            vM = KV[:, 1024 * l + 512:1024 * l + 1024].rearrange("p (i n) -> p i n", i=2)
            r = bring(4, 5, 6, 7)
            for f in range(2):
                lin_feat(hk, [(0, 256)], w, wv, 128 * f, 128, r,
                         lambda lo, hi, p, t, f=f: evac(f, kT[:, f, :], p, t), th)
            lin_tok(hk, range(2), w, wv, 256, 256, r, lambda i, p, t: evac(i, vM[:, i, :], p, t), th)
        barrier()

        def softmax_job(qk, nkeys, tiles, PB, PT, sring, tring, oring, vals, nv, scale, finish, after):
            while sring.full() or stats.full():
                yield
            S = sring.next()
            st = stats.next()
            for j, (c, n, l_, r_) in enumerate(qk):
                t = mm_group(S.ap[:, c:c + n], [(l_, r_)], after, S.freed)
            yield
            while PB.full():
                yield
            P = PB.next()
            t1 = dve.do(lambda e: e.tensor_reduce(st.ap[:, 0:1], S.ap[:, 0:nkeys], AX, ALU.max), t, st.freed)
            t1 = dve.do(lambda e: e.tensor_scalar(st.ap[:, 1:2], st.ap[:, 0:1], -scale, None, ALU.mult), t1)
            yield
            t2 = act.do(lambda e: e.activation(P.ap[:, 0:nkeys], S.ap[:, 0:nkeys], ACT.Exp, bias=st.ap[:, 1:2], scale=scale,
                                               accum_out=st.ap[:, 2:3]), t1, P.freed)
            S.freed = t2
            t3 = dve.do(lambda e: e.reciprocal(st.ap[:, 3:4], st.ap[:, 2:3]), t2)
            yield
            while PT.full():
                yield
            pt = PT.next()
            n = nkeys // 128
            te = []
            for a in range(0, n, 4):
                b = min(n, a + 4)
                bk = tring.next()
                tt = transposes(bk.ap, [P.ap[:, 128 * j:128 * j + 128] for j in range(a, b)], t2, bk.freed)
                te.append(evac(a // 4, pt.ap[:, 128 * a:128 * b], bk.ap[:, 0:128 * (b - a)], tt, pt.freed))
                bk.freed = te[-1]
            P.freed = tt
            yield
            while oring.full():
                yield
            ob = oring.next()
            to = mm_group(ob.ap[:, 0:nv], [(pt.ap[:, 128 * j:128 * j + 128], vals(j)) for j in range(n)], te, ob.freed)
            pt.freed = to
            yield
            ob.freed = finish(ob.ap[:, 0:nv], st.ap[:, 3:4], [to, t3])
            st.freed = ob.freed

        def mem_jobs(l, QM, BR, PB, PT, sring, tring, oring, after):
            kT = KV[:, 1024 * l:1024 * l + 512].rearrange("p (f n) -> p f n", f=2)
            vM = KV[:, 1024 * l + 512:1024 * l + 1024].rearrange("p (i n) -> p i n", i=2)
            for i in range(4):
                for h in range(4):
                    o = 64 * (h % 2)
                    yield softmax_job([(0, 256, QM[o:o + 64, h // 2, 128 * i:128 * i + 128], kT[o:o + 64, h // 2, :])],
                                      256, 2, PB, PT, sring, tring, oring,
                                      lambda j, h=h: vM[:, j, 64 * h:64 * h + 64], 64, 0.125,
                                      lambda p, r, a, i=i, h=h: dve.do(
                                          lambda e: e.tensor_scalar(BR[:, i, 768 + 64 * h:832 + 64 * h], p, r, None, ALU.mult), a),
                                      after)

        def decayed(K, V, nt, q, dirs, vtile, outs, bufs, psA, psT, psO, finish, after):
            TT = 128 * nt
            rst = con("reset")[0:K, 0:TT]
            state, qh, xs_, bs = {}, {}, {}, {}
            for d, (k, lg, rev, order) in enumerate(dirs):
                B = bs[d] = Slot(lg)
                E, KH, KT_, SP, QH, DEC = (bufs[n_][d] for n_ in ("E", "KH", "KT", "SP", "QH", "DEC"))
                if rev:
                    tb = dve.do(lambda e, B=B, lg=lg: e.tensor_tensor_scan(B.ap[0:K, 0:TT][:, ::-1], rst,
                                                                         lg[:, ::-1], 0.0, ALU.mult, ALU.add), after, B.freed)
                else:
                    tb = dve.do(lambda e, B=B, lg=lg: e.tensor_tensor_scan(B.ap[0:K, 0:TT], rst, lg, 0.0, ALU.mult, ALU.add),
                                after, B.freed)
                b3 = B.ap[0:K, 0:TT].rearrange("p (i n) -> p i n", n=128)
                end = b3[:, :, 0:1] if rev else b3[:, :, 127:128]
                e3 = E.ap[0:K, 0:TT].rearrange("p (i n) -> p i n", n=128)
                te = dve.do(lambda e, e3=e3, end=end, b3=b3: e.tensor_tensor(e3, end.broadcast_to([K, nt, 128]), b3, ALU.subtract), tb, E.freed)
                te = act.do(lambda e, E=E: e.activation(E.ap[0:K, 0:TT], E.ap[0:K, 0:TT], ACT.Exp), te)
                td = act.do(lambda e, DEC=DEC, end=end: e.activation(DEC.ap[0:K, 0:nt], end.rearrange("p i o -> p (i o)"), ACT.Exp), tb, DEC.freed)
                tq = act.do(lambda e, QH=QH, B=B: e.activation(QH.ap[0:K, 0:TT], B.ap[0:K, 0:TT], ACT.Exp), tb, QH.freed)
                tk = dve.do(lambda e, KH=KH, E=E, k=k: e.tensor_tensor(KH.ap[0:K, 0:TT], k, E.ap[0:K, 0:TT], ALU.mult), te)
                tq = pool.do(lambda e, QH=QH: e.tensor_tensor(QH.ap[0:K, 0:TT], q, QH.ap[0:K, 0:TT], ALU.mult), tq)
                qh[d] = tq
                yield
                tks = []
                per = 512 // 128
                for a in range(0, nt, per):
                    b = min(nt, a + per)
                    bk = psT.next()
                    tt = transposes(bk.ap, [KH.ap[0:K, 128 * i:128 * i + 128] for i in range(a, b)], tk, bk.freed)
                    o = KT_.ap[:, K * a:K * b].rearrange("p (i n) -> p i n", n=K)
                    i3 = bk.ap[:, 0:128 * (b - a)].rearrange("p (i n) -> p i n", n=128)[:, :, 0:K]
                    tks.append(evac(1, o, i3, tt, KT_.freed))
                    bk.freed = tks[-1]
                KH.freed = tt
                yield
                s3 = SP.ap[0:K, 0:nt * V].rearrange("p (i n) -> p i n", n=V)
                state[d] = {}
                prev = None
                for a, i in enumerate(order[:-1]):
                    nx = order[a + 1]
                    bk = psT.next()
                    tm = mm_group(bk.ap[0:K, 0:V], [(KT_.ap[:, K * i:K * i + K], vtile(i))], tks, bk.freed)
                    if prev is None:
                        ts = dve.do(lambda e, s3=s3, nx=nx, bk=bk: e.tensor_copy(s3[:, nx, :], bk.ap[0:K, 0:V]), tm, SP.freed)
                    else:
                        ts = dve.do(lambda e, s3=s3, nx=nx, bk=bk, i=i, DEC=DEC: e.scalar_tensor_tensor(
                            s3[:, nx, :], s3[:, i, :], DEC.ap[0:K, i:i + 1], bk.ap[0:K, 0:V], ALU.mult, ALU.add), tm, td, prev)
                    bk.freed = ts
                    prev = ts
                    state[d][nx] = ts
                KT_.freed = tm
                DEC.freed = prev
                yield
                xs_[d] = tb
            GT = 2
            rel = {d: [] for d in range(len(dirs))}
            for gi in range(0, nt, GT):
                if not any(i in outs for i in range(gi, gi + GT)):
                    continue
                lo, hi = 128 * gi, 128 * (gi + GT)
                xr = {}
                for d, (k, lg, rev, order) in enumerate(dirs):
                    B = bs[d]
                    XB = bufs["X"][d]
                    x3 = XB.ap[0:K, :].rearrange("p (l n) -> p l n", l=7)
                    tsub = []
                    v = lambda a, h: a.rearrange("p (n t h) -> p n t h", t=2, h=h)
                    for l in range(7):
                        h = 64 >> l
                        n = 128 * GT // (2 * h)
                        b4, x4 = v(B.ap[0:K, lo:hi], h), v(x3[:, l, :], h)
                        ref = b4[:, :, 1, 0:1] if rev else b4[:, :, 0, h - 1:h]
                        ref = ref.broadcast_to([K, n, h])
                        kk, qq = (1, 0) if rev else (0, 1)
                        tsub.append(dve.do(lambda e, x4=x4, ref=ref, b4=b4, kk=kk: e.tensor_tensor(x4[:, :, kk, :], ref, b4[:, :, kk, :], ALU.subtract),
                                           xs_[d], XB.freed))
                        tsub.append(dve.do(lambda e, x4=x4, ref=ref, b4=b4, qq=qq: e.tensor_tensor(x4[:, :, qq, :], b4[:, :, qq, :], ref, ALU.subtract)))
                    tx = act.do(lambda e, XB=XB: e.activation(XB.ap[0:K, :], XB.ap[0:K, :], ACT.Exp), tsub)
                    rel[d].append(tsub[-1])
                    tmul = []
                    for l in range(7):
                        h = 64 >> l
                        x4 = v(x3[:, l, :], h)
                        k4, q4 = v(k[:, lo:hi], h), v(q[:, lo:hi], h)
                        kk, qq = (1, 0) if rev else (0, 1)
                        tmul.append(pool.do(lambda e, x4=x4, k4=k4, kk=kk: e.tensor_tensor(x4[:, :, kk, :], x4[:, :, kk, :], k4[:, :, kk, :], ALU.mult), tx))
                        tmul.append(dve.do(lambda e, x4=x4, q4=q4, qq=qq: e.tensor_tensor(x4[:, :, qq, :], x4[:, :, qq, :], q4[:, :, qq, :], ALU.mult), tx))
                    xr[d] = tmul
                yield
                for i in range(gi, gi + GT):
                    if i not in outs:
                        continue
                    at_ = []
                    for d, (k, lg, rev, order) in enumerate(dirs):
                        XB = bufs["X"][d]
                        x3 = XB.ap[0:K, :].rearrange("p (l n) -> p l n", l=7)
                        S = psA.next()
                        sv = S.ap.rearrange("p b n -> p (b n)").rearrange("p (l n) -> p l n", l=8)
                        c = 128 * (i - gi)

                        def levels(e, sv=sv, x3=x3, c=c, k=k, i=i):
                            for l in range(7):
                                e.matmul(sv[:, l, :], x3[:, l, c:c + 128], x3[:, l, c:c + 128], start=True, stop=True, skip_group_check=True)
                            return e.matmul(sv[:, 7, :], k[:, 128 * i:128 * i + 128], q[:, 128 * i:128 * i + 128],
                                            start=True, stop=True, skip_group_check=True)
                        tl = pe.do(levels, xr[d], S.freed)
                        M, Am = bufs["M"].next(), bufs["A"].next()
                        mk = bufs["mask"][:, 1024 * rev:1024 * rev + 1024].rearrange("p (l n) -> p l n", l=8)
                        m3 = M.ap.rearrange("p (l n) -> p l n", l=8)
                        tm = dve.do(lambda e, m3=m3, sv=sv, mk=mk: e.tensor_tensor(m3, sv, mk, ALU.mult), tl, M.freed)
                        S.freed = tm
                        ta = dve.do(lambda e, Am=Am, M=M: e.tensor_reduce(Am.ap, M.ap.rearrange("p (l n) -> p n l", l=8), AX, ALU.add), tm, Am.freed)
                        M.freed = ta
                        at_.append((Am, ta))
                    yield
                    bk = psO.next()
                    pairs, need = [], []
                    for Am, ta in at_:
                        pairs.append((Am.ap, vtile(i)))
                        need.append(ta)
                    for d in range(len(dirs)):
                        if i in state[d]:
                            s3 = bufs["SP"][d].ap[0:K, 0:nt * V].rearrange("p (i n) -> p i n", n=V)
                            pairs.append((bufs["QH"][d].ap[0:K, 128 * i:128 * i + 128], s3[:, i, :]))
                            need += [state[d][i], qh[d]]
                    to = mm_group(bk.ap[:, 0:V], pairs, need, bk.freed)
                    for Am, ta in at_:
                        Am.freed = to
                    yield
                    bk.freed = finish(i, bk.ap[:, 0:V], to)
                for d in range(len(dirs)):
                    bufs["X"][d].freed = tl
            for d in range(len(dirs)):
                bufs["SP"][d].freed = to
                bufs["QH"][d].freed = to
            bufs["last"] = [tl, to]

        def gla_bufs(ar, K, V, nt, nd):
            TT = 128 * nt
            b = {n_: [Slot(ar.get(c)) for _ in range(nd)] for n_, c in
                 (("KT", K * nt), ("SP", nt * V), ("QH", TT), ("DEC", 8), ("X", 7 * 256))}
            b["E"] = b["KH"] = [Slot(ar.get(TT))] * nd
            b["M"] = Ring([Slot(ar.get(1024)) for _ in range(2)])
            b["A"] = Ring([Slot(ar.get(128)) for _ in range(2 * nd)])
            b["mask"] = ar.get(512 * nd).bitcast(BF16)
            b["mslot"] = mslot
            return b

        def project_out(BR, nb, tiles, gain, extra, wout, consume):
            r = bring(0, 1, 2, 3)
            W_ = [load_w(wout[:, 512 * c:512 * c + 512], 8, 512) for c in range(2)]
            for i in tiles:
                pts = []
                for a in range(0, nb, 4):
                    b = min(nb, a + 4)
                    bk = r.next()
                    tt = transposes(bk.ap, [BR[:, i, 128 * k:128 * k + 128] for k in range(a, b)], bk.freed)
                    ev = []
                    for k in range(a, b):
                        o, s_, g_ = HT3[:, k, 128 * i:128 * i + 128], bk.ap[:, 128 * (k - a):128 * (k - a) + 128], gain(k)
                        if g_ is None:
                            ev.append(evac(a // 4 + i, o, s_, tt))
                        else:
                            ev.append(evac(a // 4 + i, o, s_, tt, scale=g_))
                    bk.freed = ev
                    pts += ev
                src = lambda k: HT3[:, k, :] if k < nb else extra[:, k - nb, :]
                orr = bring(4, 5, 6, 7)
                for c, (w, wv) in enumerate(W_):
                    bk = banks[4 + (2 * i + c) % 4]
                    t = mm_group(bk.ap, [(src(k)[:, 128 * i:128 * i + 128], wv[:, k, :]) for k in range(8)], w.ready, pts, bk.freed)
                    bk.freed = consume(i, c, bk.ap, t)
                    w.freed = [t]

        def add_x(i, c, p, t):
            o = X3[:, i, 512 * c:512 * c + 512]
            return dve.do(lambda e: e.tensor_tensor(o, p, o, ALU.add), t, xready)

        ar = Arena()
        ar.at = first_base
        BR = ar.get(4096).rearrange("p (i n) -> p i n", i=4)
        QM = ar.get(1024).rearrange("p (f n) -> p f n", f=2)
        qkf = ar.get(8 * 512).rearrange("p (f n) -> p f n", f=8)
        VG = ar.get(4 * 768).rearrange("p (i n) -> p i n", i=4)
        LGA = ar.get(4 * 512).rearrange("p (f n) -> p f n", f=4)
        at0 = ar.at
        GL = ar.get(512)
        WGU = ar.get(384)
        TMP = ar.get(2 * 512).rearrange("p (f n) -> p f n", f=2)
        PBs = Ring([Slot(ar.get(256)) for _ in range(4)])
        PTs = Ring([Slot(ar.get(256)) for _ in range(4)])
        ar.at = at0
        gb = gla_bufs(ar, 96, 192, 4, 1)
        pts = barrier()
        mk0 = sp.dma(gb["mslot"], gb["mask"].bitcast(mybir.dt.uint16), A["k_mask"][:, 0:1024], pts)
        wgs = Slot(None, sem("s_wgu"))
        wgready = sp.dma(wgs, WGU[0:16, :], A["w_gate_up"].rearrange("o a n -> (o a) n"), pts)
        g = VEC[:, VO["norm"]:VO["norm"] + 8]
        th = [norm_T(X3[:, i, :], HT3, 128 * i, g, None, bring(0, 1, 2, 3), xready) for i in range(4)]
        r = bring(0, 1, 2, 3, 4, 5, 6, 7)
        wa = A["w_in_a"][0]
        for j in range(2):
            w, wv = load_w(wa[:, 384 * j:384 * j + 384], 8, 384)
            for h in range(4):
                lin_feat(hk, [(0, 512)], w, wv, 96 * h, 96, r,
                         lambda lo, hi, p, t, j=j, h=h: evac(h, qkf[0:96, 4 * j + h, :], p, t, scale=96.0 ** -0.5 if j == 0 else None), th)
        w, wv = load_w(wa[:, 1536:1808], 8, 272)
        lin_feat(hk, [(0, 512)], w, wv, 0, 16, r, lambda lo, hi, p, t: evac(0, GL[0:16, :], p, t), th)
        tgl = (dve.sem, dve.n)
        for f in range(2):
            lin_feat(hk, [(0, 512)], w, wv, 16 + 128 * f, 128, r, lambda lo, hi, p, t, f=f: evac(f, QM[:, f, :], p, t), th)
        tlg = []
        for h in range(4):
            bk = r.next()
            p = bk.ap[0:96, :]
            t = mm_group(p, [(WGU[0:16, 96 * h:96 * h + 96], GL[0:16, :])], wgready, tgl, bk.freed)
            z, m_, n_ = LGA[0:96, h, :], TMP[0:96, 0, :], TMP[0:96, 1, :]
            t = dve.do(lambda e, z=z, p=p, h=h: e.tensor_scalar(z, p, NBG[:, h:h + 1], None, ALU.add), t)
            bk.freed = t
            ta = act.do(lambda e, m_=m_, z=z: e.activation(m_, z, ACT.Abs), t, [(dve.sem, dve.n)])
            ta = act.do(lambda e, m_=m_: e.activation(m_, m_, ACT.Exp, scale=-1.0), ta)
            ta = act.do(lambda e, m_=m_: e.activation(m_, m_, ACT.Ln, bias=con("eps")[0:96, 1:2]), ta)
            tb = dve.do(lambda e, z=z: e.tensor_scalar(z, z, 0.0, 1.0 / 16.0, ALU.min, ALU.mult), ta)
            tlg.append(dve.do(lambda e, z=z, m_=m_: e.scalar_tensor_tensor(z, m_, -1.0 / 16.0, z, ALU.mult, ALU.add), tb))
        for c0, n in ((768, 512), (1280, 256)):
            w, wv = load_w(wa[:, c0:c0 + n], 8, n)
            lin_tok(hk, range(4), w, wv, 0, n, r, lambda i, p, t, c0=c0, n=n: evac(i, VG[:, i, c0 - 768:c0 - 768 + n], p, t), th)
        barrier()

        def gla_jobs():
            for h in range(4):
                def fin(i, p, t, h=h):
                    st = stats.next()
                    s = hns.next()
                    t2 = act.do(lambda e: e.activation(s.ap[:, 0:192], p, ACT.Square, accum_out=st.ap[:, 0:1]), t, st.freed, s.freed)
                    s.freed = t2
                    t2 = rstd_of(st.ap, 1, 192, t2)
                    t2 = dve.do(lambda e: e.tensor_scalar(BR[:, i, 192 * h:192 * h + 192], p, st.ap[:, 1:2], None, ALU.mult), t2)
                    st.freed = t2
                    return t2
                yield decayed(96, 192, 4, qkf[0:96, h, :], [(qkf[0:96, 4 + h, :], LGA[0:96, h, :], 0, [0, 1, 2, 3])],
                              lambda i, h=h: VG[:, i, 192 * h:192 * h + 192], [0, 1, 2, 3], gb,
                              gpsA, gpsT, gpsO, fin, [tlg, mk0])
        gpsA, gpsT, gpsO = Ring([pair(0)]), bring(2, 3), bring(4, 5)
        gpsA.slots.append(Slot(PS[:, 6:8, :]))
        interleave(gla_jobs(), 1)
        barrier()
        mj = list(mem_jobs(0, QM, BR, PBs, PTs, bring(0, 1, 2, 3), bring(4, 5), bring(6, 7), []))
        interleave(mj, 4)
        barrier()

        def gate_mul(hkf, wcols, BR_, tiles, th_):
            rr = bring(0, 1, 2, 3, 4, 5, 6, 7)
            gr = Ring([Slot(HNB[:, 0:512]), Slot(HNB[:, 512:1024])])
            for c in range(2):
                w, wv = load_w(wcols(c), 8, 512)

                def cons(i, p, t, c=c):
                    s = gr.next()
                    ta = act.do(lambda e: e.activation(s.ap, p, ACT.Silu), t, s.freed)
                    o = BR_[:, i, 512 * c:512 * c + 512]
                    s.freed = dve.do(lambda e: e.tensor_tensor(o, o, s.ap, ALU.mult), ta)
                    return ta
                lin_tok(hkf, tiles, w, wv, 0, 512, rr, cons, th_)
            barrier()

        gate_mul(hk, lambda c: wa[:, 1808 + 512 * c:1808 + 512 * c + 512], BR, range(4), [])
        project_out(BR, 8, range(4), lambda k: GNW[:, k % 3:k % 3 + 1] if k < 6 else None, None, A["w_out"][0], add_x)
        barrier()
        dump_now("x1", X)

        ar = Arena()
        ar.at = first_base
        BR = ar.get(4096).rearrange("p (i n) -> p i n", i=4)
        QM = ar.get(1024).rearrange("p (f n) -> p f n", f=2)
        DM = ar.get(1280)
        qkT = [Slot(ar.get(6 * 512).rearrange("p (f n) -> p f n", f=6)) for _ in range(2)]
        VV = [Slot(ar.get(4 * 384).rearrange("p (i n) -> p i n", i=4)) for _ in range(2)]
        SG = Ring([Slot(ar.get(384)) for _ in range(2)])
        RT = Ring([Slot(ar.get(192)) for _ in range(2)])
        SB = Ring([Slot(ar.get(1280)) for _ in range(2)])
        PTb = Ring([Slot(ar.get(1280)) for _ in range(2)])
        pts = barrier()
        dms = Slot(None, sem("s_dm"))
        dmr = sp.dma(dms, DM, A["k_const"][:, CW["dil"][0]:CW["dil"][1]], pts)
        g = VEC[:, VO["norm"] + 8:VO["norm"] + 16]
        th = [norm_T(X3[:, i, :], HT3, 128 * i, g, None, bring(0, 1, 2, 3), []) for i in range(4)]
        wb = A["w_in_b"][0]
        w, wv = load_w(wb[:, 6912:7168], 8, 256)
        for f in range(2):
            lin_feat(hk, [(0, 512)], w, wv, 128 * f, 128, bring(6, 7), lambda lo, hi, p, t, f=f: evac(f, QM[:, f, :], p, t), th)
        cs = con("drope").rearrange("p (c i n) -> p c i n", c=2, i=4)
        lring, tring, oring = bring(3, 4), bring(5, 6), bring(7)
        sall = Slot(PS[:, 0:3, :])

        def head_project(h):
            QK, V_ = qkT[h % 2], VV[h % 2]
            pts = []
            for s_ in range(3):
                w, wv = load_w([(128 * gg, 128, wb[:, 2304 * gg + 768 * s_ + 128 * h:2304 * gg + 768 * s_ + 128 * h + 128])
                                for gg in range(3)], 8, 384)
                for i in range(4):
                    bk = lring.next()
                    t = mm_group(bk.ap[:, 0:384], [(hk(k)[:, 128 * i:128 * i + 128], wv[:, k, :]) for k in range(8)], w.ready, th, bk.freed)
                    w.freed = [t]
                    if s_ == 2:
                        t = evac(1, V_.ap[:, i, :], bk.ap[:, 0:384], t, V_.freed)
                        bk.freed = t
                        pts.append(t)
                        continue
                    S_, R_ = SG.next(), RT.next()
                    t = evac(1, S_.ap, bk.ap[:, 0:384], t, S_.freed)
                    bk.freed = t
                    v = S_.ap.rearrange("p (g n) -> p g n", g=3)
                    x1, x2 = v[:, :, 0:16], v[:, :, 16:32]
                    cc = cs[:, 0, i, :].unsqueeze(1).broadcast_to([128, 3, 16])
                    ss = cs[:, 1, i, :].unsqueeze(1).broadcast_to([128, 3, 16])
                    r4 = R_.ap.rearrange("p (a g n) -> p a g n", a=4, g=3)
                    ts = [dve.do(lambda e, o=r4[:, a], x=x, y=y: e.tensor_tensor(o, x, y, ALU.mult), t, R_.freed)
                          for a, (x, y) in enumerate(((x1, cc), (x2, ss), (x1, ss), (x2, cc)))]
                    tr = [dve.do(lambda e, x1=x1, r4=r4: e.tensor_tensor(x1, r4[:, 0], r4[:, 1], ALU.subtract), ts),
                          dve.do(lambda e, x2=x2, r4=r4: e.tensor_tensor(x2, r4[:, 2], r4[:, 3], ALU.add), ts)]
                    R_.freed = tr
                    bk = tring.next()
                    tt = transposes(bk.ap, [S_.ap[:, 128 * gg:128 * gg + 128] for gg in range(3)], tr, bk.freed)
                    S_.freed = tt
                    o = QK.ap[:, 3 * s_:3 * s_ + 3, 128 * i:128 * i + 128]
                    t = evac(i, o, bk.ap[:, 0:384].rearrange("p (g n) -> p g n", g=3), tt, QK.freed)
                    bk.freed = t
                    pts.append(t)
                    yield
            QK.ready = pts
            QK.users, V_.users = [], []

        def head_attend(h):
            QK, V_ = qkT[h % 2], VV[h % 2]
            for i in range(4):
                n0 = 1 if i == 0 else 2
                n1 = i + 1
                while SB.full() or PTb.full():
                    yield
                st, P, pt = stats.next(), SB.next(), PTb.next()
                def scores(e, i=i, n0=n0, n1=n1):
                    e.matmul(sall.ap[:, 0, 0:128 * n0], QK.ap[:, 0, 128 * i:128 * i + 128], QK.ap[:, 3, 128 * (i + 1 - n0):128 * (i + 1)], start=True, stop=True)
                    e.matmul(sall.ap[:, 1, 0:128 * n1], QK.ap[:, 1, 128 * i:128 * i + 128], QK.ap[:, 4, 0:128 * n1], start=True, stop=True)
                    return e.matmul(sall.ap[:, 2, 0:128 * n1], QK.ap[:, 2, 128 * i:128 * i + 128], QK.ap[:, 5, 0:128 * n1], start=True, stop=True)
                t = pe.do(scores, QK.ready, sall.freed)
                yield
                ns = [n0, n1, n1]
                offs = [0, n0, n0 + n1]
                mends = [256, 768, 1280]
                ta = []
                for gg in range(3):
                    c0, wd = 128 * offs[gg], 128 * ns[gg]
                    ta.append(dve.do(lambda e, gg=gg, c0=c0, wd=wd, P=P: e.scalar_tensor_tensor(
                        P.ap[:, c0:c0 + wd], sall.ap[:, gg, 0:wd], 128.0 ** -0.5, DM[:, mends[gg] - wd:mends[gg]], ALU.mult, ALU.add), t, dmr, P.freed))
                sall.freed = ta
                nk = n0 + 2 * n1
                t1 = dve.do(lambda e, P=P, st=st, nk=nk: e.tensor_reduce(st.ap[:, 0:1], P.ap[:, 0:128 * nk], AX, ALU.max), ta, st.freed)
                t1 = dve.do(lambda e, st=st: e.tensor_scalar(st.ap[:, 1:2], st.ap[:, 0:1], -1.0, None, ALU.mult), t1)
                t2 = act.do(lambda e, P=P, st=st, nk=nk: e.activation(P.ap[:, 0:128 * nk], P.ap[:, 0:128 * nk], ACT.Exp, bias=st.ap[:, 1:2],
                                                              accum_out=st.ap[:, 2:3]), t1)
                t3 = dve.do(lambda e, st=st: e.reciprocal(st.ap[:, 3:4], st.ap[:, 2:3]), t2)
                yield
                te = []
                for a in range(0, nk, 4):
                    b = min(nk, a + 4)
                    bk = tring.next()
                    tt = transposes(bk.ap, [P.ap[:, 128 * j:128 * j + 128] for j in range(a, b)], t2, bk.freed)
                    te.append(evac(a // 4, pt.ap[:, 128 * a:128 * b], bk.ap[:, 0:128 * (b - a)], tt, pt.freed))
                    bk.freed = te[-1]
                P.freed = tt
                yield
                vt = []
                for gg in range(3):
                    first = i + 1 - ns[gg]
                    vt += [V_.ap[:, first + j, 128 * gg:128 * gg + 128] for j in range(ns[gg])]
                ob = oring.next()
                to = mm_group(ob.ap[:, 0:128], [(pt.ap[:, 128 * j:128 * j + 128], vt[j]) for j in range(nk)], te, QK.ready, ob.freed)
                pt.freed = to
                ob.freed = dve.do(lambda e, ob=ob, st=st, i=i: e.tensor_scalar(BR[:, i, 128 * h:128 * h + 128], ob.ap[:, 0:128], st.ap[:, 3:4], None, ALU.mult), to, t3)
                st.freed = ob.freed
                yield
            QK.freed = to
            V_.freed = to

        interleave([head_project(0)], 1)
        for h in range(6):
            jobs = [head_attend(h)] + ([head_project(h + 1)] if h < 5 else [])
            interleave(jobs, 2)
        barrier()
        PBs = Ring([Slot(SB.slots[i].ap[:, 256 * j:256 * j + 256]) for i in range(2) for j in range(2)])
        PTs = Ring([Slot(PTb.slots[i].ap[:, 256 * j:256 * j + 256]) for i in range(2) for j in range(2)])
        interleave(mem_jobs(1, QM, BR, PBs, PTs, bring(0, 1, 2, 3), bring(4, 5), bring(6, 7), []), 4)
        barrier()
        gate_mul(hk, lambda c: wb[:, 7168 + 512 * c:7168 + 512 * c + 512], BR, range(4), [])
        project_out(BR, 8, range(4), lambda k: None, None, A["w_out"][1], add_x)
        barrier()
        dump_now("x2", X)
        ar = Arena()
        FW = ar.get(1024)
        pts = barrier()
        fws = Slot(None, sem("s_fw"))
        fwr = sp.dma(fws, FW, A["final_norm_w"].rearrange("(o n) -> o n", o=1).broadcast_to([128, 1024]), pts)
        for i in range(4):
            s, st = hns.next(), stats.next()
            t = act.do(lambda e, i=i, s=s, st=st: e.activation(s.ap, X3[:, i, :], ACT.Square, accum_out=st.ap[:, 0:1]), s.freed, st.freed)
            s.freed = t
            t = rstd_of(st.ap, 1, D, t)
            t = dve.do(lambda e, i=i, st=st: e.scalar_tensor_tensor(X3[:, i, :], X3[:, i, :], st.ap[:, 1:2], FW, ALU.mult, ALU.mult), t, fwr)
            st.freed = t
        barrier()
        dump_now("x3", X)

        def residual_rows(ar, l, j, gcol):
            GV = ar.get(2048).rearrange("p (c n) -> p c n", c=2)
            cl = ar.get(16)
            dg = Ring([Slot(ar.get(128)) for _ in range(2)])
            rr = bring(0, 1)
            tdone = []
            for who in range(2):
                tcol = dve.do(lambda e, who=who: e.tensor_tensor(cl[:, 8 * who:8 * who + 8], modcol(l, j, who), gcol, ALU.mult))
                for half in range(2):
                    bk = rr.next()
                    for k in range(4):
                        s = dg.next()
                        kk = 4 * half + k
                        t = dve.do(lambda e, s=s, kk=kk, who=who: e.tensor_scalar(s.ap, ident, cl[:, 8 * who + kk:8 * who + kk + 1], None, ALU.mult), tcol, s.freed)
                        t = mm_group(bk.ap[:, 128 * k:128 * k + 128], [(ones, s.ap)], t, bk.freed if k == 0 else [])
                        s.freed = t
                    bk.freed = evac(half, GV[:, who, 512 * half:512 * half + 512], bk.ap, t)
                    tdone.append(bk.freed)
            return GV, tdone

        def scale_cols(ar, l, j, gcol, who):
            a = ar.get(8)
            t = dve.do(lambda e: e.scalar_tensor_tensor(a, modcol(l, j, who), 1.0, gcol, ALU.add, ALU.mult))
            return a, t

        def xt(i):
            return X3[:, i, :] if i < 4 else XC3[:, i - 4, :]

        def add_normed(Y, i, GV, pts):
            s, st = hns.next(), stats.next()
            y = Y[:, i, :]
            t = act.do(lambda e: e.activation(s.ap, y, ACT.Square, accum_out=st.ap[:, 0:1]), pts, s.freed, st.freed)
            s.freed = t
            t = rstd_of(st.ap, 1, D, t)
            gv = GV[:, 0 if i < 4 else 1, :]
            t = dve.do(lambda e: e.scalar_tensor_tensor(y, y, st.ap[:, 1:2], gv, ALU.mult, ALU.mult), t)
            st.freed = t
            return dve.do(lambda e: e.tensor_tensor(xt(i), xt(i), y, ALU.add), t)

        for l in range(2):
            both = l == 0
            nt = 6 if both else 4
            w2 = A["w_in_2"][l]
            gcol = lambda j: VEC[:, VO["norm_g"] + 32 * l + 8 * j:VO["norm_g"] + 32 * l + 8 * j + 8]
            ar = Arena()
            BR = ar.get(6 * 768).rearrange("p (i n) -> p i n", i=6)
            FTT = ar.get(2 * 768).rearrange("p (f n) -> p f n", f=2)
            base = ar.at
            pts = barrier()
            cols = [scale_cols(ar, l, 1, gcol(0), who) for who in range(2)]
            th = [norm_T(xt(i), HT3, 128 * i, cols[i // 4][0], modcol(l, 0, i // 4), bring(0, 1, 2, 3), [cols[i // 4][1], xcready])
                  for i in range(6)]
            QKT = ar.get(4 * 768).rearrange("p (f n) -> p f n", f=4)
            DV = ar.get(6 * 256).rearrange("p (i n) -> p i n", i=6)
            U = ar.get(6 * 256).rearrange("p (i n) -> p i n", i=6)
            SG = Ring([Slot(ar.get(512)) for _ in range(2)])
            RT = Ring([Slot(ar.get(1024)) for _ in range(2)])
            PA = Ring([Slot(ar.get(1536)) for _ in range(2)])
            PTb = Ring([Slot(ar.get(768)) for _ in range(2)])
            PQ = ar.get(2 * 2 * 512).rearrange("p (c f n) -> p c f n", c=2, f=2)
            lring = bring(0, 1, 2, 3)
            tring = bring(4, 5)
            w, wv = load_w(w2[:, 2560:3072], 8, 512)
            arp = con("arope").rearrange("p (c i a n) -> p c i a n", c=2, i=4, a=2)
            qpts = []

            def qk_cons(i, p, t):
                S_ = SG.next()
                t = evac(1, S_.ap, p, t, S_.freed)
                ret = t
                if i < 4:
                    R_ = RT.next()
                    v = S_.ap.rearrange("p (g a c n) -> p g a c n", g=16, a=2, c=2)
                    x1, x2 = v[:, :, :, 0, :], v[:, :, :, 1, :]
                    cc = arp[:, 0, i].unsqueeze(1).broadcast_to([128, 16, 2, 8])
                    ss = arp[:, 1, i].unsqueeze(1).broadcast_to([128, 16, 2, 8])
                    r4 = R_.ap.rearrange("p (q g a n) -> p q g a n", q=4, g=16, a=2)
                    ts = [dve.do(lambda e, o=r4[:, a], x=x, y=y: e.tensor_tensor(o, x, y, ALU.mult), t, R_.freed)
                          for a, (x, y) in enumerate(((x1, cc), (x2, ss), (x1, ss), (x2, cc)))]
                    t = [dve.do(lambda e: e.tensor_tensor(x1, r4[:, 0], r4[:, 1], ALU.subtract), ts),
                         dve.do(lambda e: e.tensor_tensor(x2, r4[:, 2], r4[:, 3], ALU.add), ts)]
                    R_.freed = t
                bk = tring.next()
                tt = transposes(bk.ap, [S_.ap[:, 128 * f:128 * f + 128] for f in range(4)], t, bk.freed)
                S_.freed = tt
                bk.freed = evac(i, QKT[:, :, 128 * i:128 * i + 128], bk.ap.rearrange("p (f n) -> p f n", f=4), tt)
                qpts.append(bk.freed)
                return ret
            lin_tok(hk, range(6), w, wv, 0, 512, lring, qk_cons, th)
            w, wv = load_w(w2[:, 3072:3584], 8, 512)
            lin_tok(hk, range(6), w, wv, 0, 256, lring, lambda i, p, t: evac(i, DV[:, i, :], p, t), th)
            lin_tok(hk, range(nt), w, wv, 256, 256, lring, lambda i, p, t: evac(i, U[:, i, :], p, t), th)
            dpt = barrier()
            cs64 = con("cs64")
            for who, (n, name, tiles0, off) in enumerate(((T, "k_dft", 0, 0), (TC, "k_dftc", 4, 512))):
                if who and not both:
                    continue
                kt = n // 128
                tabs = []
                for c in range(2):
                    s = wring.next()
                    v = s.ap[:, 0:kt * n].rearrange("p (k n) -> p k n", k=kt)
                    s.ready = sp.dma(s, s.ap[:, 0:kt * n], A[name][:, c * kt * n:(c + 1) * kt * n])
                    tabs.append((s, v))
                ev = []
                for c in range(2):
                    s, v = tabs[c]
                    for f in range(2):
                        bk = lring.next()
                        t = mm_group(bk.ap[:, 0:n], [(U[:, tiles0 + k, 128 * f:128 * f + 128], v[:, k, :]) for k in range(kt)], s.ready, bk.freed)
                        s.freed = [t]
                        bk.freed = evac(f, PQ[:, c, f, 0:n], bk.ap[:, 0:n], t, [(pe.sem, pe.n)] if who else [])
                        ev.append(bk.freed)
                for f in range(2):
                    bk = tring.next()
                    t = mm_group(bk.ap[:, 0:n], [(cs64[:, 128 * c:128 * c + 128], PQ[:, c, f, 0:n]) for c in range(2)], ev, bk.freed)
                    bk.freed = evac(f, FTT[:, f, off:off + n], bk.ap[:, 0:n], t)
            barrier()
            sring = Ring([Slot(PS[:, 0:2, :]), Slot(PS[:, 2:4, :])])
            oring = bring(6, 7)

            def da_job(i, h):
                lat = i < 4
                keys = [(0, 512), (512, 768)] if lat else [(512, 768)]
                nk = 6 if lat else 2
                while PA.full() or PTb.full():
                    yield
                P, pt, st = PA.next(), PTb.next(), stats.next()
                te = []
                for m_ in range(2):
                    while sring.full():
                        yield
                    S = sring.next()
                    f, o = h // 2, (h % 2) * 64 + 32 * m_
                    sv = S.ap.rearrange("p b n -> p (b n)")

                    def sc(e, sv=sv, f=f, o=o):
                        c = 0
                        for lo, hi in keys:
                            r_ = e.matmul(sv[:, c:c + hi - lo], QKT[o:o + 32, f, 128 * i:128 * i + 128], QKT[o:o + 32, 2 + f, lo:hi], start=True, stop=True)
                            c += hi - lo
                        return r_
                    t = pe.do(sc, S.freed)
                    yield
                    t1 = dve.do(lambda e, sv=sv, m_=m_: e.tensor_reduce(st.ap[:, m_:m_ + 1], sv[:, 0:128 * nk], AX, ALU.max), t, st.freed)
                    t1 = dve.do(lambda e, m_=m_: e.tensor_scalar(st.ap[:, m_:m_ + 1], st.ap[:, m_:m_ + 1], -(32.0 ** -0.5), None, ALU.mult), t1)
                    t2 = act.do(lambda e, sv=sv, m_=m_: e.activation(P.ap[:, 768 * m_:768 * m_ + 128 * nk], sv[:, 0:128 * nk], ACT.Exp, bias=st.ap[:, m_:m_ + 1],
                                                                     scale=32.0 ** -0.5, accum_out=st.ap[:, 2 + m_:3 + m_]), t1, P.freed)
                    S.freed = t2
                    te.append(t2)
                yield
                t = dve.do(lambda e: e.reciprocal(st.ap[:, 4:6], st.ap[:, 2:4]), te)
                t = dve.do(lambda e: e.tensor_scalar(st.ap[:, 5:6], st.ap[:, 5:6], LB[:, l:l + 1], None, ALU.mult), t)
                p0, p1 = P.ap[:, 0:128 * nk], P.ap[:, 768:768 + 128 * nk]
                t = dve.do(lambda e: e.tensor_scalar(p1, p1, st.ap[:, 5:6], None, ALU.mult), t)
                t = dve.do(lambda e: e.scalar_tensor_tensor(p0, p0, st.ap[:, 4:5], p1, ALU.mult, ALU.subtract), t)
                st.freed = t
                yield
                tv = []
                for a in range(0, nk, 4):
                    b = min(nk, a + 4)
                    bk = tring.next()
                    tt = transposes(bk.ap, [P.ap[:, 128 * j:128 * j + 128] for j in range(a, b)], t, bk.freed)
                    tv.append(evac(1, pt.ap[:, 128 * a:128 * b], bk.ap[:, 0:128 * (b - a)], tt, pt.freed))
                    bk.freed = tv[-1]
                P.freed = tt
                yield
                while oring.full():
                    yield
                ob = oring.next()
                k0 = 0 if lat else 4
                to = mm_group(ob.ap[:, 0:64], [(pt.ap[:, 128 * j:128 * j + 128], DV[:, k0 + j, 64 * h:64 * h + 64]) for j in range(nk)], tv, ob.freed)
                pt.freed = to
                yield
                s2 = stats.next()
                s = hns.next()
                t = act.do(lambda e: e.activation(s.ap[:, 0:64], ob.ap[:, 0:64], ACT.Square, accum_out=s2.ap[:, 0:1]), to, s2.freed, s.freed)
                s.freed = t
                t = rstd_of(s2.ap, 1, 64, t)
                t = dve.do(lambda e: e.tensor_scalar(BR[:, i, 512 + 64 * h:576 + 64 * h], ob.ap[:, 0:64], s2.ap[:, 1:2], None, ALU.mult), t)
                ob.freed = t
                s2.freed = t
            interleave([da_job(i, h) for i in range(nt) for h in range(4)], 2)

            ar.at = base
            pts = barrier()
            QF = ar.get(768)
            KF = [ar.get(768) for _ in range(2)]
            LG = [ar.get(768) for _ in range(2)]
            VH = ar.get(768).rearrange("p (i n) -> p i n", i=6)
            GH = ar.get(768).rearrange("p (i n) -> p i n", i=6)
            hb = gla_bufs(ar, 128, 128, 6, 2)
            mk = sp.dma(hb["mslot"], hb["mask"].bitcast(mybir.dt.uint16), A["k_mask"], pts)
            spans = [(0, 512), (512, 768)]
            for h in range(4):
                rr = bring(0, 1, 2, 3, 4, 5, 6, 7)
                w, wv = load_w([(0, 128, w2[:, 128 * h:128 * h + 128]), (128, 128, w2[:, 1536 + 128 * h:1536 + 128 * h + 128]),
                                (256, 128, w2[:, 2048 + 128 * h:2048 + 128 * h + 128])], 8, 384)
                hp = []

                def qcons(lo, hi, p, t):
                    t = act.do(lambda e: e.activation(QF[:, lo:hi], p, ACT.Silu), t)
                    hp.append(t)
                    return t
                lin_feat(hk, spans if both else spans[:1], w, wv, 0, 128, rr, qcons, [])
                for d in range(2):
                    def zcons(lo, hi, p, t, d=d):
                        lb, om = LOW[:, d, l, h:h + 1], ONEM[:, d, l, h:h + 1]
                        o = LG[d][:, lo:hi]
                        k_ = KF[d][:, lo:hi]
                        ta = act.do(lambda e: e.activation(o, p, ACT.Sigmoid), t)
                        tk = act.do(lambda e: e.activation(k_, p, ACT.Sigmoid, scale=-1.0), t)
                        hp.append(dve.do(lambda e: e.tensor_scalar(k_, k_, om, None, ALU.mult), tk))
                        tb = dve.do(lambda e: e.tensor_scalar(o, o, om, lb, ALU.mult, ALU.add), ta)
                        tb = dve.do(lambda e: e.tensor_scalar(o, o, 1e-19, None, ALU.max), tb)
                        hp.append(act.do(lambda e: e.activation(o, o, ACT.Ln), tb))
                        return [ta, tk]
                    lin_feat(hk, spans, w, wv, 128 + 128 * d, 128, rr, zcons, [])
                w, wv = load_w([(0, 128, w2[:, 512 + 128 * h:512 + 128 * h + 128]), (128, 128, w2[:, 1024 + 128 * h:1024 + 128 * h + 128])], 8, 256)

                def vcons(i, p, t):
                    t1 = dve.do(lambda e: e.tensor_copy(VH[:, i, :], p[:, 0:128]), t)
                    t2 = act.do(lambda e: e.activation(GH[:, i, :], p[:, 128:256], ACT.Silu), t, t1)
                    hp.extend([t1, t2])
                    return [t1, t2]
                lin_tok(hk, range(6), w, wv, 0, 256, rr, vcons, [])
                barrier()

                def fin(i, p, t, h=h):
                    st = stats.next()
                    s = hns.next()
                    t2 = act.do(lambda e: e.activation(s.ap[:, 0:128], p, ACT.Square, accum_out=st.ap[:, 0:1]), t, st.freed, s.freed)
                    s.freed = t2
                    t2 = rstd_of(st.ap, 1, 128, t2)
                    t2 = dve.do(lambda e: e.scalar_tensor_tensor(BR[:, i, 128 * h:128 * h + 128], p, st.ap[:, 1:2], GH[:, i, :], ALU.mult, ALU.mult), t2)
                    st.freed = t2
                    return t2
                if not both:
                    tz = dve.do(lambda e: e.memset(QF[:, 512:768], 0.0)) if h == 0 else None
                job = decayed(128, 128, 6, QF, [(KF[0], LG[0], 0, [4, 5, 0, 1, 2, 3]), (KF[1], LG[1], 1, [5, 4, 3, 2, 1, 0])],
                              lambda i: VH[:, i, :], list(range(nt)), hb, Ring([Slot(PS[:, 0:2, :]), Slot(PS[:, 2:4, :])]),
                              bring(4, 5), bring(6, 7), fin, [mk] + ([tz] if not both and h == 0 else []))
                interleave([job], 1)
                barrier()
            ar.at = base
            Y = ar.get(6 * 1024).rearrange("p (i n) -> p i n", i=6)
            GV, gpt = residual_rows(ar, l, 2, gcol(1))
            ON = VEC[:, VO["hg_onorm"] + l:VO["hg_onorm"] + l + 1]
            project_out(BR, 6, range(nt), lambda k: ON if k < 4 else SUBC[:, l:l + 1], FTT, A["w_out_2"][l],
                        lambda i, c, p, t: evac(i + c, Y[:, i, 512 * c:512 * c + 512], p, t))
            barrier()
            for i in range(nt):
                add_normed(Y, i, GV, gpt)
            barrier()
            dump_now(f"y{l}", X)
            ar = Arena()
            ACTT = ar.get(22 * 128 * nt).rearrange("p (j n) -> p j n", j=22)
            cols = [scale_cols(ar, l, 4, gcol(2), who) for who in range(2)]
            th = [norm_T(xt(i), HT3, 128 * i, cols[i // 4][0], modcol(l, 3, i // 4), bring(0, 1, 2, 3), [cols[i // 4][1]])
                  for i in range(nt)]
            wi, wo = A["w_ffn_in_2"][l], A["w_ffn_out_2"][l]
            rr = bring(0, 1, 2, 3, 4, 5, 6, 7)
            sp_ = [(0, 512), (512, 768)] if both else [(0, 512)]
            pts = barrier()
            for jj in range(11):
                w, wv = load_w([(0, 256, wi[:, 256 * jj:256 * jj + 256]), (256, 256, wi[:, FF + 256 * jj:FF + 256 * jj + 256])], 8, 512)
                for j2 in range(2):
                    for lo, hi in sp_:
                        o = ACTT[:, 2 * jj + j2, lo:hi]
                        tg = []

                        def gc(lo, hi, p, t, o=o):
                            tg.append(act.do(lambda e: e.activation(o, p, ACT.Silu), t))
                            return tg[0]

                        def uc(lo, hi, p, t, o=o):
                            return dve.do(lambda e: e.tensor_tensor(o, o, p, ALU.mult), t, tg)
                        lin_feat(hk, [(lo, hi)], w, wv, 128 * j2, 128, rr, gc, th)
                        lin_feat(hk, [(lo, hi)], w, wv, 256 + 128 * j2, 128, rr, uc, th)
            barrier()
            Y = HT[:, 0:nt * 1024].rearrange("p (i n) -> p i n", i=nt)
            for c in range(2):
                pb = [banks[(i + c * nt) % 8] for i in range(nt)]
                for k0, kn in ((0, 8), (8, 8), (16, 6)):
                    w, wv = load_w(wo[128 * k0:128 * (k0 + kn), 512 * c:512 * c + 512], kn, 512)
                    for i in range(nt):
                        t = mm_group(pb[i].ap, [(ACTT[:, k0 + k, 128 * i:128 * i + 128], wv[:, k, :]) for k in range(kn)],
                                     w.ready, pb[i].freed if k0 == 0 else [], start=k0 == 0, stop=k0 == 16)
                        if k0 == 16:
                            pb[i].freed = evac(i, Y[:, i, 512 * c:512 * c + 512], pb[i].ap, t)
                    w.freed = [t]
            barrier()
            ar = Arena()
            GV, gpt = residual_rows(ar, l, 5, gcol(3))
            for i in range(nt):
                add_normed(Y, i, GV, gpt)
            barrier()
            dump_now(f"z{l}", X)

        outs = Slot(None, sem("s_out"))
        ot = sp.dma(outs, out.rearrange("o (i p) n -> p (o i) n", p=128), X3, barrier())
        sp.wait(ot, dumps)


_INS = ["x", "mem", "mem_norm_w", "norm_w", "w_memkv", "w_out", "w_in_a", "w_gate_up", "b_gate", "gla_norm_w",
        "w_in_b", "final_norm_w", "c_2", "ctx_2", "c_ctx_2", "w_mod_2", "b_mod_2", "norm_g_2", "w_in_2", "w_out_2",
        "hg_lb_logits_2", "hg_onorm_2", "da_lambda_2", "da_subln_2", "w_ffn_in_2", "w_ffn_out_2"]


def kernel(**inputs):
    import numpy as _np
    import concourse.bacc as _bacc
    from concourse import mybir as _mybir
    from concourse.bass_utils import run_bass_kernel_spmd as _run

    nc = _bacc.Bacc("TRN2", target_bir_lowering=False, num_devices=1)
    arrays, A = {}, {}
    for name in _INS:
        a = _np.ascontiguousarray(inputs[name])
        arrays[f"in_{name}"] = a
        A[name] = nc.dram_tensor(f"in_{name}", a.shape, _mybir.dt.from_np(a.dtype), kind="ExternalInput").ap()
    for name, a in zip(("k_const", "k_dft", "k_dftc", "k_mask"), shape_tables()):
        arrays[name] = a
        A[name] = nc.dram_tensor(name, a.shape, _mybir.dt.from_np(a.dtype), kind="ExternalInput").ap()
    out = nc.dram_tensor("out_0", (1, 512, 1024), _mybir.dt.float32, kind="ExternalOutput").ap()
    build(nc, A, out)
    r = _run(nc, [arrays], core_ids=[0])
    return r.results[0]["out_0"]
```

```python
import math
from contextlib import ExitStack

import numpy as np
import concourse.bass as bass
from concourse import mybir

F32 = mybir.dt.float32
F32R = mybir.dt.float32r
BF16 = mybir.dt.bfloat16
ALU = mybir.AluOpType
ACT = mybir.ActivationFunctionType
AX = mybir.AxisListType.X
EPS = 1e-6
D = 1024
T = 512
TC = 256
FF = 2816

CONST_WIDTHS = [("ident", 128), ("ones", 128), ("reset", 768), ("eps", 8), ("drope", 128), ("arope", 128),
                ("cs64", 256), ("dil", 1280)]
CW = {}
_o = 0
for _n, _w in CONST_WIDTHS:
    CW[_n] = (_o, _o + _w)
    _o += _w
CTOT = _o
CBASE = CW["dil"][0]
VROWS = [("mem_norm", 8), ("norm", 16), ("norm_g", 64), ("hg_onorm", 2), ("hg_lb", 16), ("c", 8), ("c_ctx", 8)]
VO = {}
_o = 0
for _n, _w in VROWS:
    VO[_n] = _o
    _o += _w
VTOT = _o


def shape_tables():
    c = np.zeros((128, CTOT), np.float32)
    p = np.arange(128)

    def put(name, a):
        lo, hi = CW[name]
        c[:, lo:hi] = np.asarray(a, np.float32).reshape(128, hi - lo)

    put("ident", np.eye(128))
    put("ones", np.ones((128, 128)))
    r = np.ones((128, 768))
    r[:, ::128] = 0
    put("reset", r)
    r = np.ones((128, 768))
    e = np.zeros((128, 8))
    e[:, 0] = EPS
    e[:, 1] = 1.0
    put("eps", e)
    t = p[:, None] + 128 * np.arange(4)[None, :]
    inv = 500000.0 ** (-np.arange(16) / 16.0)
    ang = (t[:, :, None].astype(np.float32) * inv.astype(np.float32)[None, None, :]).astype(np.float32)
    put("drope", np.stack([np.cos(ang), np.sin(ang)], 1))
    invf = (1.0 / (10000.0 ** (np.arange(0, 16, 2) / 16.0))).astype(np.float32)
    rc = np.stack([t // 64, t % 64], -1).astype(np.float32)
    ang = rc[:, :, :, None] * invf[None, None, None, :]
    put("arope", np.stack([np.cos(ang), np.sin(ang)], 1))
    k = np.arange(64)
    a64 = 2 * np.pi * ((k[:, None] * k[None, :]) % 64) / 64
    z = np.zeros((128, 256))
    for b in range(2):
        z[64 * b:64 * b + 64, 64 * b:64 * b + 64] = np.cos(a64)
        z[64 * b:64 * b + 64, 128 + 64 * b:128 + 64 * b + 64] = -np.sin(a64)
    put("cs64", z)
    s, q = p[:, None], p[None, :]
    lv = np.zeros((128, 2, 8, 128))
    for l in range(7):
        h = 64 >> l
        same = (s // (2 * h)) == (q // (2 * h))
        lv[:, 0, l] = same & (s % (2 * h) < h) & (q % (2 * h) >= h)
        lv[:, 1, l] = same & (s % (2 * h) >= h) & (q % (2 * h) < h)
    lv[:, :, 7] = np.eye(128)[:, None, :]
    neg = -1e30
    qq, ss = p[:, None], p[None, :]
    g0 = np.concatenate([np.where(ss >= qq, 0, neg), np.where(ss <= qq, 0, neg)], 1)
    out = [g0]
    for r in (4, 16):
        off = np.where((qq - ss) % r == 0, 0, neg)
        dg = np.where(((qq - ss) % r == 0) & (ss <= qq), 0, neg)
        out.append(np.concatenate([off, off, off, dg], 1))
    put("dil", np.concatenate(out, 1))

    def dft(n):
        j = np.arange(n)
        a = 2 * np.pi * ((j[:, None] * j[None, :]) % n) / n
        w = np.stack([np.cos(a), np.sin(a)]) / np.sqrt(n * 64.0)
        return w.reshape(2, n // 128, 128, n).transpose(2, 0, 1, 3).reshape(128, -1).astype(np.float32)

    bits = lv.reshape(128, 2048).astype(np.uint16) * np.uint16(0x3F80)
    return c, dft(T), dft(TC), bits


def flat(x):
    if x is None:
        return []
    if isinstance(x, tuple) and len(x) == 2 and isinstance(x[1], int):
        return [x]
    out = []
    for y in x:
        out += flat(y)
    return out


class Lane:

    def __init__(self, e, sem):
        self.e, self.sem, self.n, self.seen = e, sem, 0, {}

    def wait(self, *points):
        for sem, value in flat(points):
            if self.seen.get(id(sem), 0) < value:
                self.seen[id(sem)] = value
                self.e.wait_ge(sem, value)

    def do(self, fn, *after):
        self.wait(*after)
        self.n += 1
        fn(self.e).then_inc(self.sem, 1)
        return (self.sem, self.n)

    def dma(self, slot, out, in_, *after):
        self.wait(slot.freed, *after)
        slot.n += 16
        self.e.dma_start(out, in_).then_inc(slot.sem, 16)
        return (slot.sem, slot.n)


class Scalar:

    SETS = {ACT.Exp: "natural_log_exp_and_others", ACT.Ln: "natural_log_exp_and_others",
            ACT.Silu: "silu_and_others", ACT.Sigmoid: "sigmoid_and_others"}

    def __init__(self, e):
        self.e, self.loaded = e, None
        self.wait_ge, self.dma_start = e.wait_ge, e.dma_start

    def activation(self, out, in_, func, **kw):
        need = self.SETS.get(func)
        if need is not None and need != self.loaded:
            self.e.preload_act_table_set(need)
            self.loaded = need
        return self.e.activation(out, in_, func, **kw)


class Slot:

    def __init__(self, ap, sem=None):
        self.ap, self.sem, self.n, self.freed = ap, sem, 0, []

    @property
    def freed(self):
        return self._freed

    @freed.setter
    def freed(self, points):
        self._freed, self.busy = points, False


class Ring:
    def __init__(self, slots):
        self.slots, self.i = slots, 0

    def full(self):
        return self.slots[self.i % len(self.slots)].busy

    def next(self):
        s = self.slots[self.i % len(self.slots)]
        assert not s.busy
        s.busy = True
        self.i += 1
        return s


def interleave(jobs, width):
    live, jobs = [], list(jobs)
    while live or jobs:
        while jobs and len(live) < width:
            live.append(jobs.pop(0))
        for j in list(live):
            try:
                next(j)
            except StopIteration:
                live.remove(j)


def build(nc, A, out, dump=None):
    with ExitStack() as ctx:
        total = [0]

        def sb(name, cols):
            total[0] += cols * 4
            return ctx.enter_context(nc.sbuf_tensor(name, [128, cols], F32))[:, :]

        def sem(name):
            return ctx.enter_context(nc.semaphore(name))

        PS = ctx.enter_context(nc.psum_tensor("PS", [128, 8, 512], F32))[:, :, :]
        pe, act, dve, pool, sp = (Lane(e, sem(f"s_{n}")) for e, n in (
            (nc.tensor, "pe"), (Scalar(nc.scalar), "act"), (nc.vector, "dve"), (nc.gpsimd, "pool"), (nc.sync, "sp")))
        compute = [pe, act, dve, pool]

        CON = sb("CON", CBASE)
        VEC = sb("VEC", VTOT)
        BMOD = sb("BMOD", 96)
        MOD = sb("MOD", 2 * 96)
        MISC = sb("MISC", 128)
        STAT = sb("STAT", 64 * 8)
        X = sb("X", 4096)
        XC = sb("XC", 2048)
        HT = sb("HT", 8 * 768)
        WR = sb("WR", 2 * 4096)
        HNB = sb("HNB", 1024)
        EX = sb("EX", 4096)
        ARN = 53150 - total[0] // 4
        arena = [ExitStack()]
        uid = [0]

        def claim(*shapes):
            arena[0].close()
            arena[0] = ctx.enter_context(ExitStack())
            uid[0] += 1
            return [arena[0].enter_context(nc.sbuf_tensor(f"{n_}{uid[0]}", [128, c_], t_))[:, :] for n_, c_, t_ in shapes]

        AR, = claim(("AR", ARN, F32))

        def con(name):
            lo, hi = CW[name]
            return CON[:, lo:hi]

        ident = con("ident")
        ones = con("ones")
        eps = con("eps")[:, 0:1]
        wring = Ring([Slot(WR[:, 4096 * i:4096 * (i + 1)], sem(f"s_w{i}")) for i in range(2)])
        stats = Ring([Slot(STAT[:, 8 * i:8 * i + 8]) for i in range(64)])
        hns = Ring([Slot(HNB)])
        banks = [Slot(PS[:, b, :]) for b in range(8)]
        misc = Slot(None, sem("s_misc"))
        mslot = Slot(None, sem("s_mask"))
        XSP = nc.dram_tensor("x_spill", (128, 6144), F32, kind="Internal").ap()

        class Spill:

            def __init__(self):
                self.slot = Slot(None, sem("s_spill"))

            def dma_out(self, q, src, dst, *after):
                return q.dma(self.slot, dst, src, *after)

            def dma_in(self, q, dst, src, *after):
                return q.dma(self.slot, dst, src, *after)

        spill = Spill()

        def bring(*ids):
            return Ring([banks[i] for i in ids])

        def pair(i):
            return Slot(PS[:, i:i + 2, :])

        def barrier():
            points = [(l.sem, l.n) for l in compute]
            for l in compute:
                l.wait(*points)
            return points

        class Arena:
            def __init__(self, base=None, size=None):
                self.at, self.base, self.size = 0, AR if base is None else base, size or ARN

            def get(self, cols):
                assert self.at + cols <= self.size, (self.at, cols, self.size)
                a = self.base[:, self.at:self.at + cols]
                self.at += cols
                return a

        def evac(n, out_, in_, *after, scale=None):
            if n % 2:
                return act.do(lambda e: e.activation(out_, in_, ACT.Copy, scale=1.0 if scale is None else scale), *after)
            if scale is None:
                return dve.do(lambda e: e.tensor_copy(out_, in_), *after)
            return dve.do(lambda e: e.tensor_scalar(out_, in_, scale, None, ALU.mult), *after)

        def load_w(src, kt, n):
            s = wring.next()
            v = s.ap[:, 0:kt * n].rearrange("p (k n) -> p k n", k=kt)
            src = src if isinstance(src, list) else [(0, n, src)]
            for lo, w, a in src:
                s.ready = sp.dma(s, v[:, :, lo:lo + w], a.rearrange("(k p) n -> p k n", p=128))
            return s, v

        def mm_group(psum, pairs, *after, start=True, stop=True):
            def go(e):
                for i, (l, r) in enumerate(pairs):
                    m = e.matmul(psum, l, r, start=start and i == 0, stop=stop and i == len(pairs) - 1,
                                 skip_group_check=True)
                return m
            return pe.do(go, *after)

        def transposes(bank, ins, *after):
            def go(e):
                for i, a in enumerate(ins):
                    m = e.transpose(bank[0:a.shape[1], 128 * i:128 * i + a.shape[0]], a,
                                    ident[0:a.shape[0], 0:a.shape[0]])
                return m
            return pe.do(go, *after)

        def rstd_of(st, n, count, after):
            t = act.do(lambda e: e.activation(st[:, n:2 * n], st[:, 0:n], ACT.Ln, scale=1.0 / count, bias=eps), after)
            return act.do(lambda e: e.activation(st[:, n:2 * n], st[:, n:2 * n], ACT.Exp, scale=-0.5), t)

        def norm_T(src, dst, col0, g, b, ring, after):
            s, st = hns.next(), stats.next()
            t = act.do(lambda e: e.activation(s.ap, src, ACT.Square, accum_out=st.ap[:, 0:1]), after, s.freed, st.freed)
            t = rstd_of(st.ap, 1, D, t)
            t = dve.do(lambda e: e.tensor_scalar(s.ap, src, st.ap[:, 1:2], None, ALU.mult), t)
            st.freed = t
            done = []
            for hf in range(2):
                bk = ring.next()
                tt = transposes(bk.ap, [s.ap[:, 128 * (4 * hf + k):128 * (4 * hf + k + 1)] for k in range(4)], t, bk.freed)
                o = dst[:, 4 * hf:4 * hf + 4, col0:col0 + 128]
                i3 = bk.ap.rearrange("p (k n) -> p k n", k=4)
                gb = g[:, 4 * hf:4 * hf + 4].unsqueeze(2).broadcast_to([128, 4, 128])
                te = dve.do(lambda e, o=o, i3=i3, gb=gb: e.tensor_tensor(o, i3, gb, ALU.mult), tt)
                bk.freed = te
                if b is not None:
                    bb = b[:, 4 * hf:4 * hf + 4].unsqueeze(2).broadcast_to([128, 4, 128])
                    te = dve.do(lambda e, o=o, bb=bb: e.tensor_tensor(o, o, bb, ALU.add), te)
                done.append(te)
            s.freed = tt
            return done

        def split(hi, lo, src, *after):
            t1 = act.do(lambda e: e.activation(hi, src, ACT.Copy), *after)
            t2 = dve.do(lambda e: e.tensor_tensor(lo, src, hi.bitcast(F32), ALU.subtract), t1, *after)
            return t1, t2

        def norm_split(src, dst, col0, g, b, ring, tmps, after):
            s, st = hns.next(), stats.next()
            t = act.do(lambda e: e.activation(s.ap, src, ACT.Square, accum_out=st.ap[:, 0:1]), after, s.freed, st.freed)
            t = rstd_of(st.ap, 1, D, t)
            t = dve.do(lambda e: e.tensor_scalar(s.ap, src, st.ap[:, 1:2], None, ALU.mult), t)
            st.freed = t
            done = []
            for hf in range(2):
                bk, m = ring.next(), tmps.next()
                tt = transposes(bk.ap, [s.ap[:, 128 * (4 * hf + k):128 * (4 * hf + k + 1)] for k in range(4)], t, bk.freed)
                m3 = m.ap.rearrange("p (k n) -> p k n", k=4)
                i3 = bk.ap.rearrange("p (k n) -> p k n", k=4)
                gb = g[:, 4 * hf:4 * hf + 4].unsqueeze(2).broadcast_to([128, 4, 128])
                te = dve.do(lambda e: e.tensor_tensor(m3, i3, gb, ALU.mult), tt, m.freed)
                bk.freed = te
                if b is not None:
                    bb = b[:, 4 * hf:4 * hf + 4].unsqueeze(2).broadcast_to([128, 4, 128])
                    te = dve.do(lambda e: e.tensor_tensor(m3, m3, bb, ALU.add), te)
                o = [d[:, 4 * hf:4 * hf + 4, col0:col0 + 128] for d in dst]
                t1, t2 = split(o[0], o[1], m3, te)
                m.freed = t2
                done += [t1, t2]
            s.freed = tt
            return done

        def lin_tok(act_k, tiles, w, wv, c0, n, ring, consume, after):
            K = wv.shape[1]
            for i in tiles:
                bk = ring.next()
                t = mm_group(bk.ap[:, 0:n], [(act_k(k)[:, 128 * i:128 * i + 128], wv[:, k, c0:c0 + n]) for k in range(K)],
                             w.ready, after, bk.freed)
                bk.freed = consume(i, bk.ap[:, 0:n], t)
            w.freed = [t]

        def lin_feat(act_k, spans, w, wv, c0, m, ring, consume, after):
            K = wv.shape[1]
            for lo, hi in spans:
                bk = ring.next()
                p = bk.ap[0:m, 0:hi - lo]
                t = mm_group(p, [(wv[:, k, c0:c0 + m], act_k(k)[:, lo:hi]) for k in range(K)], w.ready, after, bk.freed)
                bk.freed = consume(lo, hi, p, t)
            w.freed = [t]

        X3 = X.rearrange("p (i n) -> p i n", i=4)
        XC3 = XC.rearrange("p (i n) -> p i n", i=2)
        HT3 = HT.rearrange("p (k n) -> p k n", k=8)
        hk = lambda k: HT3[:, k, :]

        dumps = []

        def dump_now(name, ap):
            if dump is None:
                return
            pts = barrier()
            s = Slot(None, sem("d_" + name))
            sp.dma(s, dump(name, ap), ap, pts)
            dumps.append((s.sem, s.n))
            for l in compute:
                l.wait((s.sem, s.n))

        c0t = sp.dma(misc, CON, A["k_const"][:, 0:CBASE])
        ar = Arena()
        VR = ar.get(128)
        BR_ = ar.get(128)
        GR = ar.get(256)
        LAMR = ar.get(256)
        FNW = ar.get(1024)
        SC = ar.get(1024)
        rows = {"mem_norm": A["mem_norm_w"].rearrange("(a n) -> a n", n=128),
                "norm": A["norm_w"].rearrange("l (a n) -> (l a) n", n=128),
                "norm_g": A["norm_g_2"].rearrange("l g (a n) -> (l g a) n", n=128),
                "hg_onorm": A["hg_onorm_2"],
                "hg_lb": A["hg_lb_logits_2"].rearrange("d l (a n) -> (d l a) n", n=128),
                "c": A["c_2"].rearrange("o (a n) -> (o a) n", n=128),
                "c_ctx": A["c_ctx_2"].rearrange("(a n) -> a n", n=128)}
        for n_, w_ in VROWS:
            sp.dma(misc, VR[VO[n_]:VO[n_] + w_, :], rows[n_])
        sp.dma(misc, BR_[0:96, :], A["b_mod_2"].rearrange("l (a n) -> (l a) n", n=128))
        sp.dma(misc, GR[0:4, 0:96], A["b_gate"].rearrange("o (a n) -> (o a) n", n=96))
        gw = A["gla_norm_w"]
        sp.dma(misc, GR[0:1, 128:256], gw[:, 0:128])
        sp.dma(misc, GR[1:2, 128:192], gw[:, 128:192])
        sp.dma(misc, GR[1:2, 192:256], gw[:, 0:64])
        sp.dma(misc, GR[2:3, 128:256], gw[:, 64:192])
        sub = A["da_subln_2"]
        for h_ in range(2):
            sp.dma(misc, GR[3:5, 128 + 64 * h_:192 + 64 * h_], sub)
        for l in range(2):
            lm = A["da_lambda_2"][l:l + 1].rearrange("o a n -> o (a n)")
            sp.dma(misc, LAMR[:, 128 * l:128 * l + 128], lm.broadcast_to([128, 128]))
        cready = (misc.sem, misc.n)
        xs = Slot(None, sem("s_x"))
        xready = sp.dma(xs, X3, A["x"].rearrange("o (i p) n -> p (o i) n", p=128))
        xcs = Slot(None, sem("s_xc"))
        xcready = sp.dma(xcs, XC3, A["ctx_2"].rearrange("o (i p) n -> p (o i) n", p=128))

        b0 = bring(0, 1)
        bk = b0.next()
        t = transposes(bk.ap, [VR[0:VTOT, :], BR_[0:96, :], GR[0:4, 0:96], GR[0:5, 128:256]], cready)
        t1 = dve.do(lambda e: e.tensor_copy(VEC, bk.ap[:, 0:VTOT]), t)
        t2 = dve.do(lambda e: e.tensor_copy(BMOD, bk.ap[:, 128:224]), t)
        t3 = dve.do(lambda e: e.tensor_copy(MISC[0:96, 0:4], bk.ap[0:96, 256:260]), t)
        t4 = dve.do(lambda e: e.tensor_copy(MISC[:, 4:9], bk.ap[:, 384:389]), t)
        bk.freed = [t1, t2, t3, t4]
        NBG, GNW, SUBC = MISC[0:96, 0:4], MISC[:, 4:7], MISC[:, 7:9]
        LIN = [0.8 - 0.6 * math.exp(-0.3 * l) for l in range(2)]
        t5 = [dve.do(lambda e, l=l: e.tensor_scalar(MISC[:, 7 + l:8 + l], MISC[:, 7 + l:8 + l], 1.0 - LIN[l], None, ALU.mult), t4)
              for l in range(2)]
        LB = MISC[:, 9:11]
        for l in range(2):
            a4 = LAMR[:, 128 * l:128 * l + 128].rearrange("p (a n) -> p a n", a=4)
            ta = dve.do(lambda e, a4=a4: e.tensor_tensor(SC[:, 0:64].rearrange("p (a n) -> p a n", a=2),
                                                         a4[:, 0:4:2, :], a4[:, 1:4:2, :], ALU.mult), cready,
                        [(dve.sem, dve.n)])
            ta = dve.do(lambda e: e.tensor_reduce(SC[:, 64:66], SC[:, 0:64].rearrange("p (a n) -> p a n", a=2), AX, ALU.add), ta)
            ta = act.do(lambda e: e.activation(SC[:, 66:68], SC[:, 64:66], ACT.Exp), ta)
            ta = dve.do(lambda e: e.tensor_tensor(SC[:, 68:69], SC[:, 66:67], SC[:, 67:68], ALU.subtract), ta)
            dve.do(lambda e, l=l: e.tensor_scalar(LB[:, l:l + 1], SC[:, 68:69], LIN[l], None, ALU.add), ta)
        L3 = VEC[:, VO["hg_lb"]:VO["hg_lb"] + 16].rearrange("p (d l a) -> p d l a", d=2, l=2)
        LOW = MISC[:, 16:32].rearrange("p (d l a) -> p d l a", d=2, l=2)
        ONEM = MISC[:, 32:48].rearrange("p (d l a) -> p d l a", d=2, l=2)
        w4 = [SC[:, 128 + 8 * i:136 + 8 * i].rearrange("p (d a) -> p d a", d=2) for i in range(6)]
        ta = dve.do(lambda e: e.tensor_tensor(w4[0], L3[:, :, 0, :], L3[:, :, 1, :], ALU.max), t1)
        tb = dve.do(lambda e: e.tensor_tensor(w4[1], L3[:, :, 0, :], w4[0], ALU.subtract), ta)
        tc_ = dve.do(lambda e: e.tensor_tensor(w4[2], L3[:, :, 1, :], w4[0], ALU.subtract), ta)
        tb = act.do(lambda e: e.activation(w4[1], w4[1], ACT.Exp), tb)
        tc_ = act.do(lambda e: e.activation(w4[2], w4[2], ACT.Exp), tc_)
        ta = dve.do(lambda e: e.tensor_tensor(w4[3], w4[1], w4[2], ALU.add), tb, tc_)
        ta = dve.do(lambda e: e.reciprocal(w4[4], w4[3]), ta)
        tb = dve.do(lambda e: e.tensor_tensor(w4[1], w4[1], w4[4], ALU.mult), ta)
        tc_ = dve.do(lambda e: e.tensor_tensor(w4[2], w4[2], w4[4], ALU.mult), ta)
        dve.do(lambda e: e.tensor_tensor(LOW[:, :, 0, :], w4[1], w4[1], ALU.subtract), tb)
        ta = dve.do(lambda e: e.tensor_tensor(w4[5], w4[1], w4[2], ALU.add), tb, tc_)
        ta = dve.do(lambda e: e.tensor_tensor(LOW[:, :, 1, :], w4[5], w4[1], ALU.subtract), ta)
        dve.do(lambda e: e.tensor_scalar(ONEM, LOW, -1.0, 1.0, ALU.mult, ALU.add), ta)
        CV = MISC[:, 64:80].rearrange("p (k c) -> p k c", c=2)
        for i, n_ in enumerate(("c", "c_ctx")):
            act.do(lambda e, i=i, n_=n_: e.activation(CV[:, :, i], VEC[:, VO[n_]:VO[n_] + 8], ACT.Silu), t1)
        barrier()

        def modulation(halves, mbank, tbank):
            for l in range(2):
                for c in range(12):
                    w, wv = load_w(A["w_mod_2"][l][:, 512 * c:512 * c + 512], 8, 512)
                    mm_group(mbank.ap[0:2, :], [(CV[:, k, :], wv[:, k, :]) for k in range(4)], w.ready, mbank.freed, stop=False)
                    yield
                    t = mm_group(mbank.ap[0:2, :], [(CV[:, k, :], wv[:, k, :]) for k in range(4, 8)], start=False)
                    w.freed = t
                    half = halves.next()
                    t = dve.do(lambda e: e.tensor_copy(half.ap, mbank.ap[0:2, :]), t, half.freed)
                    mbank.freed = t
                    yield
                    tt = pe.do(lambda e: [e.transpose(tbank.ap[:, 2 * j:2 * j + 2], half.ap[:, 128 * j:128 * j + 128], ident[0:2, 0:2])
                                          for j in range(4)][-1], t, tbank.freed)
                    half.freed = tt
                    o = MOD[:, 96 * l + 8 * c:96 * l + 8 * c + 8].rearrange("p (j c) -> p j c", c=2)
                    bb = BMOD[:, 48 * l + 4 * c:48 * l + 4 * c + 4].unsqueeze(2).broadcast_to([128, 4, 2])
                    tbank.freed = dve.do(lambda e: e.tensor_tensor(o, tbank.ap[:, 0:8].rearrange("p (j c) -> p j c", c=2), bb, ALU.add), tt)

        def modcol(l, j, who):
            return MOD[:, 96 * l:96 * l + 96].rearrange("p (j k c) -> p j k c", j=6, k=8)[:, j, :, who]

        ar = Arena()
        KV = ar.get(2 * 1024)
        first_base = ar.at
        MX = ar.get(2048).rearrange("p (i n) -> p i n", i=2)
        ms = Slot(None, sem("s_mem"))
        mready = sp.dma(ms, MX, A["mem"].rearrange("o (i p) n -> p (o i) n", p=128), [(dve.sem, dve.n), (pe.sem, pe.n), (act.sem, act.n)])
        g = VEC[:, VO["mem_norm"]:VO["mem_norm"] + 8]
        th = [norm_T(MX[:, i, :], HT3, 128 * i, g, None, bring(0, 1, 2, 3), mready) for i in range(2)]
        for l in range(2):
            w, wv = load_w(A["w_memkv"][l], 8, 512)
            kT = KV[:, 1024 * l:1024 * l + 512].rearrange("p (f n) -> p f n", f=2)
            vM = KV[:, 1024 * l + 512:1024 * l + 1024].rearrange("p (i n) -> p i n", i=2)
            r = bring(4, 5, 6, 7)
            for f in range(2):
                lin_feat(hk, [(0, 256)], w, wv, 128 * f, 128, r,
                         lambda lo, hi, p, t, f=f: evac(f, kT[:, f, :], p, t), th)
            lin_tok(hk, range(2), w, wv, 256, 256, r, lambda i, p, t: evac(i, vM[:, i, :], p, t), th)
        barrier()

        def softmax_job(qk, nkeys, tiles, PB, PT, sring, tring, oring, vals, nv, scale, finish, after):
            while sring.full() or stats.full():
                yield
            S = sring.next()
            st = stats.next()
            for j, (c, n, l_, r_) in enumerate(qk):
                t = mm_group(S.ap[:, c:c + n], [(l_, r_)], after, S.freed)
            yield
            while PB.full():
                yield
            P = PB.next()
            t1 = dve.do(lambda e: e.tensor_reduce(st.ap[:, 0:1], S.ap[:, 0:nkeys], AX, ALU.max), t, st.freed)
            t1 = dve.do(lambda e: e.tensor_scalar(st.ap[:, 1:2], st.ap[:, 0:1], -scale, None, ALU.mult), t1)
            yield
            t2 = act.do(lambda e: e.activation(P.ap[:, 0:nkeys], S.ap[:, 0:nkeys], ACT.Exp, bias=st.ap[:, 1:2], scale=scale,
                                               accum_out=st.ap[:, 2:3]), t1, P.freed)
            S.freed = t2
            t3 = dve.do(lambda e: e.reciprocal(st.ap[:, 3:4], st.ap[:, 2:3]), t2)
            yield
            while PT.full():
                yield
            pt = PT.next()
            n = nkeys // 128
            te = []
            for a in range(0, n, 4):
                b = min(n, a + 4)
                bk = tring.next()
                tt = transposes(bk.ap, [P.ap[:, 128 * j:128 * j + 128] for j in range(a, b)], t2, bk.freed)
                te.append(evac(a // 4, pt.ap[:, 128 * a:128 * b], bk.ap[:, 0:128 * (b - a)], tt, pt.freed))
                bk.freed = te[-1]
            P.freed = tt
            yield
            while oring.full():
                yield
            ob = oring.next()
            to = mm_group(ob.ap[:, 0:nv], [(pt.ap[:, 128 * j:128 * j + 128], vals(j)) for j in range(n)], te, ob.freed)
            pt.freed = to
            yield
            ob.freed = finish(ob.ap[:, 0:nv], st.ap[:, 3:4], [to, t3])
            st.freed = ob.freed

        def mem_jobs(l, QM, BR, PB, PT, sring, tring, oring, after):
            kT = KV[:, 1024 * l:1024 * l + 512].rearrange("p (f n) -> p f n", f=2)
            vM = KV[:, 1024 * l + 512:1024 * l + 1024].rearrange("p (i n) -> p i n", i=2)
            for i in range(4):
                for h in range(4):
                    o = 64 * (h % 2)
                    yield softmax_job([(0, 256, QM[o:o + 64, h // 2, 128 * i:128 * i + 128], kT[o:o + 64, h // 2, :])],
                                      256, 2, PB, PT, sring, tring, oring,
                                      lambda j, h=h: vM[:, j, 64 * h:64 * h + 64], 64, 0.125,
                                      lambda p, r, a, i=i, h=h: dve.do(
                                          lambda e: e.tensor_scalar(BR[:, i, 768 + 64 * h:832 + 64 * h], p, r, None, ALU.mult), a),
                                      after)

        def decayed(K, V, nt, q, dirs, vtile, outs, bufs, psA, psT, psO, finish, after):
            TT = 128 * nt
            rst = con("reset")[0:K, 0:TT]
            nd = len(dirs)
            cum, td, tq, tks, state, prev = {}, {}, {}, {}, {}, {}
            for d, (k, lg, rev, order) in enumerate(dirs):
                o_, i_ = (lg[:, ::-1], lg[:, ::-1]) if rev else (lg, lg)
                cum[d] = dve.do(lambda e: e.tensor_tensor_scan(o_, rst, i_, 0.0, ALU.mult, ALU.add), after)

            def build(i):
                got = []
                for d, (k, lg, rev, order) in enumerate(dirs):
                    XB = bufs["X"][d].next()
                    x3 = XB.ap[0:K, :].rearrange("p (l n) -> p l n", l=7)
                    lo, hi = 128 * i, 128 * i + 128
                    v = lambda a, h: a.rearrange("p (n t h) -> p n t h", t=2, h=h)
                    t = []
                    for l in range(7):
                        h = 64 >> l
                        b4 = v(lg[:, lo:hi], h)
                        ref = b4[:, :, 1, 0:1] if rev else b4[:, :, 0, h - 1:h]
                        w2h = lambda a: a.rearrange("p (n h) -> p n h", h=2 * h)
                        t.append(dve.do(lambda e: e.tensor_tensor(w2h(x3[:, l, :]), w2h(lg[:, lo:hi]), ref.broadcast_to([K, 64 // h, 2 * h]),
                                                                  ALU.subtract), cum[d], XB.freed))
                    t = act.do(lambda e: e.activation(XB.ap[0:K, :], XB.ap[0:K, :], ACT.Abs), t)
                    t = act.do(lambda e: e.activation(XB.ap[0:K, :], XB.ap[0:K, :], ACT.Exp, scale=-1.0), t)
                    got.append((XB, x3, t))
                return got

            def weigh(i, built):
                got = []
                lo, hi = 128 * i, 128 * i + 128
                v = lambda a, h: a.rearrange("p (n t h) -> p n t h", t=2, h=h)
                for (XB, x3, t), (k, lg, rev, order) in zip(built, dirs):
                    mul = []
                    for l in range(7):
                        h = 64 >> l
                        x4, k4, q4 = v(x3[:, l, :], h), v(k[:, lo:hi], h), v(q[:, lo:hi], h)
                        kk, qq = (1, 0) if rev else (0, 1)
                        mul.append(pool.do(lambda e: e.tensor_tensor(x4[:, :, kk, :], x4[:, :, kk, :], k4[:, :, kk, :], ALU.mult), t))
                        mul.append(dve.do(lambda e: e.tensor_tensor(x4[:, :, qq, :], x4[:, :, qq, :], q4[:, :, qq, :], ALU.mult), t))
                    got.append((XB, x3, [mul[-2], mul[-1]]))
                return got

            def levels(i, built):
                out_ = []
                for (XB, x3, ready_), (k, lg, rev, order) in zip(built, dirs):
                    S = psA.next()
                    sv = S.ap.rearrange("p b n -> p (b n)").rearrange("p (l n) -> p l n", l=8)

                    def go(e):
                        for l in range(7):
                            e.matmul(sv[:, l, :], x3[:, l, :], x3[:, l, :], start=True, stop=True, skip_group_check=True)
                        return e.matmul(sv[:, 7, :], k[:, 128 * i:128 * i + 128], q[:, 128 * i:128 * i + 128],
                                        start=True, stop=True, skip_group_check=True)
                    tl = pe.do(go, ready_, S.freed)
                    XB.freed = tl
                    out_.append((S, sv, rev, tl))
                return out_

            def reduce_(lv):
                at_ = []
                for S, sv, rev, tl in lv:
                    M, Am = bufs["M"].next(), bufs["A"].next()
                    mk = bufs["mask"][:, 1024 * rev:1024 * rev + 1024].rearrange("p (l n) -> p l n", l=8)
                    m3 = M.ap.rearrange("p (l n) -> p l n", l=8)
                    tm = dve.do(lambda e: e.tensor_tensor(m3, sv, mk, ALU.mult), tl, M.freed)
                    S.freed = tm
                    ta = dve.do(lambda e: e.tensor_reduce(Am.ap, M.ap.rearrange("p (l n) -> p n l", l=8), AX, ALU.add), tm, Am.freed)
                    M.freed = ta
                    at_.append((Am, ta))
                return at_

            def output(i, at_):
                bk = psO.next()
                pairs, need = [(Am.ap, vtile(i)) for Am, _ in at_], [ta for _, ta in at_]
                for d in range(nd):
                    if i in state[d]:
                        s3 = bufs["SP"][d].ap[0:K, 0:nt * V].rearrange("p (i n) -> p i n", n=V)
                        pairs.append((bufs["QH"][d].ap[0:K, 128 * i:128 * i + 128], s3[:, i, :]))
                        need += [state[d][i], tq[d]]
                to = mm_group(bk.ap[:, 0:V], pairs, need, bk.freed)
                for Am, _ in at_:
                    Am.freed = to
                last = finish(i, bk.ap[:, 0:V], to)

                def end():
                    bk.freed = last()
                return to, end

            built = build(outs[0])
            yield
            built = weigh(outs[0], built)
            for d, (k, lg, rev, order) in enumerate(dirs):
                KH, KT_, SP, QH, DEC = (bufs[n_][d] for n_ in ("KH", "KT", "SP", "QH", "DEC"))
                b3 = lg.rearrange("p (i n) -> p i n", n=128)
                end = b3[:, :, 0:1] if rev else b3[:, :, 127:128]
                e3 = KH.ap[0:K, 0:TT].rearrange("p (i n) -> p i n", n=128)
                te = dve.do(lambda e: e.tensor_tensor(e3, end.broadcast_to([K, nt, 128]), b3, ALU.subtract), cum[d], KH.freed)
                te = act.do(lambda e: e.activation(KH.ap[0:K, 0:TT], KH.ap[0:K, 0:TT], ACT.Exp), te)
                td[d] = act.do(lambda e: e.activation(DEC.ap[0:K, 0:nt], end.rearrange("p i o -> p (i o)"), ACT.Exp), cum[d], DEC.freed)
                tq[d] = act.do(lambda e: e.activation(QH.ap[0:K, 0:TT], lg, ACT.Exp), cum[d], QH.freed)
                tk = dve.do(lambda e: e.tensor_tensor(KH.ap[0:K, 0:TT], k, KH.ap[0:K, 0:TT], ALU.mult), te)
                tq[d] = pool.do(lambda e: e.tensor_tensor(QH.ap[0:K, 0:TT], q, QH.ap[0:K, 0:TT], ALU.mult), tq[d])
                yield
                tks[d] = []
                for a in range(0, nt, 4):
                    b = min(nt, a + 4)
                    bk = psT.next()
                    tt = transposes(bk.ap, [KH.ap[0:K, 128 * i:128 * i + 128] for i in range(a, b)], tk, bk.freed)
                    o = KT_.ap[:, K * a:K * b].rearrange("p (i n) -> p i n", n=K)
                    i3 = bk.ap[:, 0:128 * (b - a)].rearrange("p (i n) -> p i n", n=128)[:, :, 0:K]
                    bk.freed = evac(1, o, i3, tt, KT_.freed)
                    tks[d].append(bk.freed)
                KH.freed = tt
                state[d] = {}
            yield
            for a in range(nt - 1):
                for d, (k, lg, rev, order) in enumerate(dirs):
                    KT_, SP, DEC = (bufs[n_][d] for n_ in ("KT", "SP", "DEC"))
                    s3 = SP.ap[0:K, 0:nt * V].rearrange("p (i n) -> p i n", n=V)
                    i, nx = order[a], order[a + 1]
                    bk = psT.next()
                    tm = mm_group(bk.ap[0:K, 0:V], [(KT_.ap[:, K * i:K * i + K], vtile(i))], tks[d], bk.freed)
                    if a == 0:
                        ts = dve.do(lambda e: e.tensor_copy(s3[:, nx, :], bk.ap[0:K, 0:V]), tm, SP.freed)
                    else:
                        ts = dve.do(lambda e: e.scalar_tensor_tensor(s3[:, nx, :], s3[:, i, :], DEC.ap[0:K, i:i + 1], bk.ap[0:K, 0:V],
                                                                     ALU.mult, ALU.add), tm, td[d], prev[d])
                    bk.freed = prev[d] = state[d][nx] = ts
                    KT_.freed, DEC.freed = tm, ts
                if a % 2:
                    yield
            late = None
            for n, i in enumerate(outs):
                lv = levels(i, built)
                end = output(*late)[1] if late else None
                if n + 1 < len(outs):
                    built = build(outs[n + 1])
                yield
                late = (i, reduce_(lv))
                if end:
                    end()
                if n + 1 < len(outs):
                    built = weigh(outs[n + 1], built)
                yield
            to, end = output(*late)
            end()
            for d in range(nd):
                bufs["SP"][d].freed = bufs["QH"][d].freed = to

        def gla_bufs(ar, K, V, nt, nd):
            TT = 128 * nt
            b = {n_: [Slot(ar.get(c)) for _ in range(nd)] for n_, c in
                 (("KT", K * nt), ("SP", nt * V), ("QH", TT), ("DEC", 8))}
            b["X"] = [Ring([Slot(ar.get(7 * 128)) for _ in range(2)]) for _ in range(nd)]
            b["KH"] = [Slot(ar.get(TT))] * nd
            b["M"] = Ring([Slot(ar.get(1024)) for _ in range(2)])
            b["A"] = Ring([Slot(ar.get(128)) for _ in range(2 * nd)])
            b["mask"] = ar.get(512 * nd).bitcast(BF16)
            b["mslot"] = mslot
            return b

        def project_out(BR, nb, tiles, gain, extra, wout, consume):
            r = bring(0, 1, 2, 3)
            W_ = [load_w(wout[:, 512 * c:512 * c + 512], 8, 512) for c in range(2)]
            for i in tiles:
                pts = []
                for a in range(0, nb, 4):
                    b = min(nb, a + 4)
                    bk = r.next()
                    tt = transposes(bk.ap, [BR[:, i, 128 * k:128 * k + 128] for k in range(a, b)], bk.freed)
                    ev = []
                    for k in range(a, b):
                        o, s_, g_ = HT3[:, k, 128 * i:128 * i + 128], bk.ap[:, 128 * (k - a):128 * (k - a) + 128], gain(k)
                        if g_ is None:
                            ev.append(evac(a // 4 + i, o, s_, tt))
                        else:
                            ev.append(evac(a // 4 + i, o, s_, tt, scale=g_))
                    bk.freed = ev
                    pts += ev
                src = lambda k: HT3[:, k, :] if k < nb else extra[:, k - nb, :]
                orr = bring(4, 5, 6, 7)
                for c, (w, wv) in enumerate(W_):
                    bk = banks[4 + (2 * i + c) % 4]
                    t = mm_group(bk.ap, [(src(k)[:, 128 * i:128 * i + 128], wv[:, k, :]) for k in range(8)], w.ready, pts, bk.freed)
                    bk.freed = consume(i, c, bk.ap, t)
                    w.freed = [t]

        def add_x(i, c, p, t):
            o = X3[:, i, 512 * c:512 * c + 512]
            return dve.do(lambda e: e.tensor_tensor(o, p, o, ALU.add), t, xready)

        ar = Arena()
        ar.at = first_base
        BR = ar.get(4096).rearrange("p (i n) -> p i n", i=4)
        QM = ar.get(1024).rearrange("p (f n) -> p f n", f=2)
        qkf = ar.get(8 * 512).rearrange("p (f n) -> p f n", f=8)
        VG = ar.get(4 * 768).rearrange("p (i n) -> p i n", i=4)
        LGA = ar.get(4 * 512).rearrange("p (f n) -> p f n", f=4)
        at0 = ar.at
        GL = ar.get(512)
        WGU = ar.get(384)
        TMP = ar.get(2 * 512).rearrange("p (f n) -> p f n", f=2)
        PBs = Ring([Slot(ar.get(256)) for _ in range(4)])
        PTs = Ring([Slot(ar.get(256)) for _ in range(4)])
        ar.at = at0
        gb = gla_bufs(ar, 96, 192, 4, 1)
        pts = barrier()
        mk0 = sp.dma(gb["mslot"], gb["mask"].bitcast(mybir.dt.uint16), A["k_mask"][:, 0:1024], pts)
        wgs = Slot(None, sem("s_wgu"))
        wgready = sp.dma(wgs, WGU[0:16, :], A["w_gate_up"].rearrange("o a n -> (o a) n"), pts)
        g = VEC[:, VO["norm"]:VO["norm"] + 8]
        th = [norm_T(X3[:, i, :], HT3, 128 * i, g, None, bring(0, 1, 2, 3), xready) for i in range(4)]
        r = bring(0, 1, 2, 3, 4, 5, 6, 7)
        wa = A["w_in_a"][0]
        for j in range(2):
            w, wv = load_w(wa[:, 384 * j:384 * j + 384], 8, 384)
            for h in range(4):
                lin_feat(hk, [(0, 512)], w, wv, 96 * h, 96, r,
                         lambda lo, hi, p, t, j=j, h=h: evac(h, qkf[0:96, 4 * j + h, :], p, t, scale=96.0 ** -0.5 if j == 0 else None), th)
        w, wv = load_w(wa[:, 1536:1808], 8, 272)
        lin_feat(hk, [(0, 512)], w, wv, 0, 16, r, lambda lo, hi, p, t: evac(0, GL[0:16, :], p, t), th)
        tgl = (dve.sem, dve.n)
        for f in range(2):
            lin_feat(hk, [(0, 512)], w, wv, 16 + 128 * f, 128, r, lambda lo, hi, p, t, f=f: evac(f, QM[:, f, :], p, t), th)
        tlg = []
        for h in range(4):
            bk = r.next()
            p = bk.ap[0:96, :]
            t = mm_group(p, [(WGU[0:16, 96 * h:96 * h + 96], GL[0:16, :])], wgready, tgl, bk.freed)
            z, m_, n_ = LGA[0:96, h, :], TMP[0:96, 0, :], TMP[0:96, 1, :]
            t = dve.do(lambda e, z=z, p=p, h=h: e.tensor_scalar(z, p, NBG[:, h:h + 1], None, ALU.add), t)
            bk.freed = t
            ta = act.do(lambda e, m_=m_, z=z: e.activation(m_, z, ACT.Abs), t, [(dve.sem, dve.n)])
            ta = act.do(lambda e, m_=m_: e.activation(m_, m_, ACT.Exp, scale=-1.0), ta)
            ta = act.do(lambda e, m_=m_: e.activation(m_, m_, ACT.Ln, bias=con("eps")[0:96, 1:2]), ta)
            tb = dve.do(lambda e, z=z: e.tensor_scalar(z, z, 0.0, 1.0 / 16.0, ALU.min, ALU.mult), ta)
            tlg.append(dve.do(lambda e, z=z, m_=m_: e.scalar_tensor_tensor(z, m_, -1.0 / 16.0, z, ALU.mult, ALU.add), tb))
        for c0, n in ((768, 512), (1280, 256)):
            w, wv = load_w(wa[:, c0:c0 + n], 8, n)
            lin_tok(hk, range(4), w, wv, 0, n, r, lambda i, p, t, c0=c0, n=n: evac(i, VG[:, i, c0 - 768:c0 - 768 + n], p, t), th)
        barrier()

        def gla_jobs():
            for h in range(4):
                def fin(i, p, t, h=h):
                    st = stats.next()
                    s = hns.next()
                    t2 = act.do(lambda e: e.activation(s.ap[:, 0:192], p, ACT.Square, accum_out=st.ap[:, 0:1]), t, st.freed, s.freed)
                    s.freed = t2
                    t2 = rstd_of(st.ap, 1, 192, t2)

                    def end():
                        st.freed = dve.do(lambda e: e.tensor_scalar(BR[:, i, 192 * h:192 * h + 192], p, st.ap[:, 1:2], None, ALU.mult), t2)
                        return st.freed
                    return end
                yield decayed(96, 192, 4, qkf[0:96, h, :], [(qkf[0:96, 4 + h, :], LGA[0:96, h, :], 0, [0, 1, 2, 3])],
                              lambda i, h=h: VG[:, i, 192 * h:192 * h + 192], [0, 1, 2, 3], gb,
                              gpsA, gpsT, gpsO, fin, [tlg, mk0])
        gpsA, gpsT, gpsO = Ring([pair(0)]), bring(2, 3), bring(4, 5)
        mod_halves = ar.get(1024)
        mod_job = modulation(Ring([Slot(mod_halves[0:2, 512 * i:512 * i + 512]) for i in range(2)]), banks[6], banks[7])
        gla_all = (x for j_ in gla_jobs() for x in j_)
        interleave([gla_all, mod_job], 2)
        barrier()
        mj = list(mem_jobs(0, QM, BR, PBs, PTs, bring(0, 1, 2, 3), bring(4, 5), bring(6, 7), []))
        interleave(mj, 4)
        barrier()

        def gate_mul(hkf, wcols, BR_, tiles, th_):
            rr = bring(0, 1, 2, 3, 4, 5, 6, 7)
            gr = Ring([Slot(HNB[:, 0:512]), Slot(HNB[:, 512:1024])])
            for c in range(2):
                w, wv = load_w(wcols(c), 8, 512)

                def cons(i, p, t, c=c):
                    s = gr.next()
                    ta = act.do(lambda e: e.activation(s.ap, p, ACT.Silu), t, s.freed)
                    o = BR_[:, i, 512 * c:512 * c + 512]
                    s.freed = dve.do(lambda e: e.tensor_tensor(o, o, s.ap, ALU.mult), ta)
                    return ta
                lin_tok(hkf, tiles, w, wv, 0, 512, rr, cons, th_)
            barrier()

        gate_mul(hk, lambda c: wa[:, 1808 + 512 * c:1808 + 512 * c + 512], BR, range(4), [])
        project_out(BR, 8, range(4), lambda k: GNW[:, k % 3:k % 3 + 1] if k < 6 else None, None, A["w_out"][0], add_x)
        barrier()
        dump_now("x1", X)

        ar = Arena()
        ar.at = first_base
        BR = ar.get(4096).rearrange("p (i n) -> p i n", i=4)
        QM = ar.get(1024).rearrange("p (f n) -> p f n", f=2)
        DM = ar.get(1280)
        qkT = [Slot(ar.get(6 * 512).rearrange("p (f n) -> p f n", f=6)) for _ in range(2)]
        VV = [Slot(ar.get(4 * 384).rearrange("p (i n) -> p i n", i=4)) for _ in range(2)]
        SG = Ring([Slot(ar.get(384)) for _ in range(2)])
        RT = Ring([Slot(ar.get(192)) for _ in range(2)])
        SB = Ring([Slot(ar.get(1280)) for _ in range(2)])
        PTb = Ring([Slot(ar.get(1280)) for _ in range(2)])
        pts = barrier()
        dms = Slot(None, sem("s_dm"))
        dmr = sp.dma(dms, DM, A["k_const"][:, CW["dil"][0]:CW["dil"][1]], pts)
        g = VEC[:, VO["norm"] + 8:VO["norm"] + 16]
        th = [norm_T(X3[:, i, :], HT3, 128 * i, g, None, bring(0, 1, 2, 3), []) for i in range(4)]
        wb = A["w_in_b"][0]
        w, wv = load_w(wb[:, 6912:7168], 8, 256)
        for f in range(2):
            lin_feat(hk, [(0, 512)], w, wv, 128 * f, 128, bring(6, 7), lambda lo, hi, p, t, f=f: evac(f, QM[:, f, :], p, t), th)
        cs = con("drope").rearrange("p (c i n) -> p c i n", c=2, i=4)
        lring, tring, oring = bring(3, 4), bring(5, 6), bring(7)
        sall = Slot(PS[:, 0:3, :])

        def head_project(h):
            QK, V_ = qkT[h % 2], VV[h % 2]
            pts = []
            for s_ in range(3):
                w, wv = load_w([(128 * gg, 128, wb[:, 2304 * gg + 768 * s_ + 128 * h:2304 * gg + 768 * s_ + 128 * h + 128])
                                for gg in range(3)], 8, 384)
                for i in range(4):
                    bk = lring.next()
                    t = mm_group(bk.ap[:, 0:384], [(hk(k)[:, 128 * i:128 * i + 128], wv[:, k, :]) for k in range(8)], w.ready, th, bk.freed)
                    w.freed = [t]
                    if s_ == 2:
                        t = evac(1, V_.ap[:, i, :], bk.ap[:, 0:384], t, V_.freed)
                        bk.freed = t
                        pts.append(t)
                        continue
                    S_, R_ = SG.next(), RT.next()
                    t = evac(1, S_.ap, bk.ap[:, 0:384], t, S_.freed)
                    bk.freed = t
                    v = S_.ap.rearrange("p (g n) -> p g n", g=3)
                    x1, x2 = v[:, :, 0:16], v[:, :, 16:32]
                    cc = cs[:, 0, i, :].unsqueeze(1).broadcast_to([128, 3, 16])
                    ss = cs[:, 1, i, :].unsqueeze(1).broadcast_to([128, 3, 16])
                    r4 = R_.ap.rearrange("p (a g n) -> p a g n", a=4, g=3)
                    ts = [dve.do(lambda e, o=r4[:, a], x=x, y=y: e.tensor_tensor(o, x, y, ALU.mult), t, R_.freed)
                          for a, (x, y) in enumerate(((x1, cc), (x2, ss), (x1, ss), (x2, cc)))]
                    tr = [dve.do(lambda e, x1=x1, r4=r4: e.tensor_tensor(x1, r4[:, 0], r4[:, 1], ALU.subtract), ts),
                          dve.do(lambda e, x2=x2, r4=r4: e.tensor_tensor(x2, r4[:, 2], r4[:, 3], ALU.add), ts)]
                    R_.freed = tr
                    bk = tring.next()
                    tt = transposes(bk.ap, [S_.ap[:, 128 * gg:128 * gg + 128] for gg in range(3)], tr, bk.freed)
                    S_.freed = tt
                    o = QK.ap[:, 3 * s_:3 * s_ + 3, 128 * i:128 * i + 128]
                    t = evac(i, o, bk.ap[:, 0:384].rearrange("p (g n) -> p g n", g=3), tt, QK.freed)
                    bk.freed = t
                    pts.append(t)
                    yield
            QK.ready = pts
            QK.users, V_.users = [], []

        def head_attend(h):
            QK, V_ = qkT[h % 2], VV[h % 2]
            for i in range(4):
                n0 = 1 if i == 0 else 2
                n1 = i + 1
                while SB.full() or PTb.full():
                    yield
                st, P, pt = stats.next(), SB.next(), PTb.next()
                def scores(e, i=i, n0=n0, n1=n1):
                    e.matmul(sall.ap[:, 0, 0:128 * n0], QK.ap[:, 0, 128 * i:128 * i + 128], QK.ap[:, 3, 128 * (i + 1 - n0):128 * (i + 1)], start=True, stop=True)
                    e.matmul(sall.ap[:, 1, 0:128 * n1], QK.ap[:, 1, 128 * i:128 * i + 128], QK.ap[:, 4, 0:128 * n1], start=True, stop=True)
                    return e.matmul(sall.ap[:, 2, 0:128 * n1], QK.ap[:, 2, 128 * i:128 * i + 128], QK.ap[:, 5, 0:128 * n1], start=True, stop=True)
                t = pe.do(scores, QK.ready, sall.freed)
                yield
                ns = [n0, n1, n1]
                offs = [0, n0, n0 + n1]
                mends = [256, 768, 1280]
                ta = []
                for gg in range(3):
                    c0, wd = 128 * offs[gg], 128 * ns[gg]
                    ta.append(dve.do(lambda e, gg=gg, c0=c0, wd=wd, P=P: e.scalar_tensor_tensor(
                        P.ap[:, c0:c0 + wd], sall.ap[:, gg, 0:wd], 128.0 ** -0.5, DM[:, mends[gg] - wd:mends[gg]], ALU.mult, ALU.add), t, dmr, P.freed))
                sall.freed = ta
                nk = n0 + 2 * n1
                t1 = dve.do(lambda e, P=P, st=st, nk=nk: e.tensor_reduce(st.ap[:, 0:1], P.ap[:, 0:128 * nk], AX, ALU.max), ta, st.freed)
                t1 = dve.do(lambda e, st=st: e.tensor_scalar(st.ap[:, 1:2], st.ap[:, 0:1], -1.0, None, ALU.mult), t1)
                t2 = act.do(lambda e, P=P, st=st, nk=nk: e.activation(P.ap[:, 0:128 * nk], P.ap[:, 0:128 * nk], ACT.Exp, bias=st.ap[:, 1:2],
                                                              accum_out=st.ap[:, 2:3]), t1)
                t3 = dve.do(lambda e, st=st: e.reciprocal(st.ap[:, 3:4], st.ap[:, 2:3]), t2)
                yield
                te = []
                for a in range(0, nk, 4):
                    b = min(nk, a + 4)
                    bk = tring.next()
                    tt = transposes(bk.ap, [P.ap[:, 128 * j:128 * j + 128] for j in range(a, b)], t2, bk.freed)
                    te.append(evac(a // 4, pt.ap[:, 128 * a:128 * b], bk.ap[:, 0:128 * (b - a)], tt, pt.freed))
                    bk.freed = te[-1]
                P.freed = tt
                yield
                vt = []
                for gg in range(3):
                    first = i + 1 - ns[gg]
                    vt += [V_.ap[:, first + j, 128 * gg:128 * gg + 128] for j in range(ns[gg])]
                ob = oring.next()
                to = mm_group(ob.ap[:, 0:128], [(pt.ap[:, 128 * j:128 * j + 128], vt[j]) for j in range(nk)], te, QK.ready, ob.freed)
                pt.freed = to
                ob.freed = dve.do(lambda e, ob=ob, st=st, i=i: e.tensor_scalar(BR[:, i, 128 * h:128 * h + 128], ob.ap[:, 0:128], st.ap[:, 3:4], None, ALU.mult), to, t3)
                st.freed = ob.freed
                yield
            QK.freed = to
            V_.freed = to

        interleave([head_project(0)], 1)
        for h in range(6):
            jobs = [head_attend(h)] + ([head_project(h + 1)] if h < 5 else [])
            interleave(jobs, 2)
        barrier()
        PBs = Ring([Slot(SB.slots[i].ap[:, 256 * j:256 * j + 256]) for i in range(2) for j in range(2)])
        PTs = Ring([Slot(PTb.slots[i].ap[:, 256 * j:256 * j + 256]) for i in range(2) for j in range(2)])
        interleave(mem_jobs(1, QM, BR, PBs, PTs, bring(0, 1, 2, 3), bring(4, 5), bring(6, 7), []), 4)
        barrier()
        gate_mul(hk, lambda c: wb[:, 7168 + 512 * c:7168 + 512 * c + 512], BR, range(4), [])
        project_out(BR, 8, range(4), lambda k: None, None, A["w_out"][1], add_x)
        barrier()
        dump_now("x2", X)
        ar = Arena()
        FW = ar.get(1024)
        pts = barrier()
        fws = Slot(None, sem("s_fw"))
        fwr = sp.dma(fws, FW, A["final_norm_w"].rearrange("(o n) -> o n", o=1).broadcast_to([128, 1024]), pts)
        for i in range(4):
            s, st = hns.next(), stats.next()
            t = act.do(lambda e, i=i, s=s, st=st: e.activation(s.ap, X3[:, i, :], ACT.Square, accum_out=st.ap[:, 0:1]), s.freed, st.freed)
            s.freed = t
            t = rstd_of(st.ap, 1, D, t)
            t = dve.do(lambda e, i=i, st=st: e.scalar_tensor_tensor(X3[:, i, :], X3[:, i, :], st.ap[:, 1:2], FW, ALU.mult, ALU.mult), t, fwr)
            st.freed = t
        barrier()
        dump_now("x3", X)

        def residual_rows(ar, l, j, gcol):
            GV = ar.get(2048).rearrange("p (c n) -> p c n", c=2)
            cl = ar.get(16)
            dg = Ring([Slot(ar.get(128)) for _ in range(2)])
            rr = bring(0, 1)
            tdone = []
            for who in range(2):
                tcol = dve.do(lambda e, who=who: e.tensor_tensor(cl[:, 8 * who:8 * who + 8], modcol(l, j, who), gcol, ALU.mult))
                for half in range(2):
                    bk = rr.next()
                    for k in range(4):
                        s = dg.next()
                        kk = 4 * half + k
                        t = dve.do(lambda e, s=s, kk=kk, who=who: e.tensor_scalar(s.ap, ident, cl[:, 8 * who + kk:8 * who + kk + 1], None, ALU.mult), tcol, s.freed)
                        t = mm_group(bk.ap[:, 128 * k:128 * k + 128], [(ones, s.ap)], t, bk.freed if k == 0 else [])
                        s.freed = t
                    bk.freed = evac(half, GV[:, who, 512 * half:512 * half + 512], bk.ap, t)
                    tdone.append(bk.freed)
            return GV, tdone

        def scale_cols(ar, l, j, gcol, who):
            a = ar.get(8)
            t = dve.do(lambda e: e.scalar_tensor_tensor(a, modcol(l, j, who), 1.0, gcol, ALU.add, ALU.mult))
            return a, t

        def xt(i):
            return X3[:, i, :] if i < 4 else XC3[:, i - 4, :]

        def add_normed(Y, i, GV, pts):
            s, st = hns.next(), stats.next()
            y = Y[:, i, :]
            t = act.do(lambda e: e.activation(s.ap, y, ACT.Square, accum_out=st.ap[:, 0:1]), pts, s.freed, st.freed)
            s.freed = t
            t = rstd_of(st.ap, 1, D, t)
            gv = GV[:, 0 if i < 4 else 1, :]
            t = dve.do(lambda e: e.scalar_tensor_tensor(y, y, st.ap[:, 1:2], gv, ALU.mult, ALU.mult), t)
            st.freed = t
            return dve.do(lambda e: e.tensor_tensor(xt(i), xt(i), y, ALU.add), t)

        for l in range(2):
            both = l == 0
            nt = 6 if both else 4
            w2 = A["w_in_2"][l]
            gcol = lambda j: VEC[:, VO["norm_g"] + 32 * l + 8 * j:VO["norm_g"] + 32 * l + 8 * j + 8]
            ar = Arena()
            BR = ar.get(6 * 768).rearrange("p (i n) -> p i n", i=6)
            FTT = ar.get(2 * 768).rearrange("p (f n) -> p f n", f=2)
            base = ar.at
            pts = barrier()
            cols = [scale_cols(ar, l, 1, gcol(0), who) for who in range(2)]
            th = [norm_T(xt(i), HT3, 128 * i, cols[i // 4][0], modcol(l, 0, i // 4), bring(0, 1, 2, 3), [cols[i // 4][1], xcready])
                  for i in range(6)]
            QKT = ar.get(4 * 768).rearrange("p (f n) -> p f n", f=4)
            DV = ar.get(6 * 256).rearrange("p (i n) -> p i n", i=6)
            U = ar.get(6 * 256).rearrange("p (i n) -> p i n", i=6)
            SG = Ring([Slot(ar.get(512)) for _ in range(2)])
            RT = Ring([Slot(ar.get(1024)) for _ in range(2)])
            PA = Ring([Slot(ar.get(1536)) for _ in range(3)])
            PTb = Ring([Slot(ar.get(768)) for _ in range(3)])
            PQ = ar.get(2 * 2 * 512).rearrange("p (c f n) -> p c f n", c=2, f=2)
            lring = bring(0, 1, 2, 3)
            tring = bring(4, 5)
            w, wv = load_w(w2[:, 2560:3072], 8, 512)
            arp = con("arope").rearrange("p (c i a n) -> p c i a n", c=2, i=4, a=2)
            qpts = []

            def qk_cons(i, p, t):
                S_ = SG.next()
                t = evac(1, S_.ap, p, t, S_.freed)
                ret = t
                if i < 4:
                    R_ = RT.next()
                    v = S_.ap.rearrange("p (g a c n) -> p g a c n", g=16, a=2, c=2)
                    x1, x2 = v[:, :, :, 0, :], v[:, :, :, 1, :]
                    cc = arp[:, 0, i].unsqueeze(1).broadcast_to([128, 16, 2, 8])
                    ss = arp[:, 1, i].unsqueeze(1).broadcast_to([128, 16, 2, 8])
                    r4 = R_.ap.rearrange("p (q g a n) -> p q g a n", q=4, g=16, a=2)
                    ts = [dve.do(lambda e, o=r4[:, a], x=x, y=y: e.tensor_tensor(o, x, y, ALU.mult), t, R_.freed)
                          for a, (x, y) in enumerate(((x1, cc), (x2, ss), (x1, ss), (x2, cc)))]
                    t = [dve.do(lambda e: e.tensor_tensor(x1, r4[:, 0], r4[:, 1], ALU.subtract), ts),
                         dve.do(lambda e: e.tensor_tensor(x2, r4[:, 2], r4[:, 3], ALU.add), ts)]
                    R_.freed = t
                bk = tring.next()
                tt = transposes(bk.ap, [S_.ap[:, 128 * f:128 * f + 128] for f in range(4)], t, bk.freed)
                S_.freed = tt
                bk.freed = evac(i, QKT[:, :, 128 * i:128 * i + 128], bk.ap.rearrange("p (f n) -> p f n", f=4), tt)
                qpts.append(bk.freed)
                return ret
            lin_tok(hk, range(6), w, wv, 0, 512, lring, qk_cons, th)
            w, wv = load_w(w2[:, 3072:3584], 8, 512)
            lin_tok(hk, range(6), w, wv, 0, 256, lring, lambda i, p, t: evac(i, DV[:, i, :], p, t), th)
            lin_tok(hk, range(nt), w, wv, 256, 256, lring, lambda i, p, t: evac(i, U[:, i, :], p, t), th)
            dpt = barrier()
            cs64 = con("cs64")
            for who, (n, name, tiles0, off) in enumerate(((T, "k_dft", 0, 0), (TC, "k_dftc", 4, 512))):
                if who and not both:
                    continue
                kt = n // 128
                tabs = []
                for c in range(2):
                    s = wring.next()
                    v = s.ap[:, 0:kt * n].rearrange("p (k n) -> p k n", k=kt)
                    s.ready = sp.dma(s, s.ap[:, 0:kt * n], A[name][:, c * kt * n:(c + 1) * kt * n])
                    tabs.append((s, v))
                ev = []
                for c in range(2):
                    s, v = tabs[c]
                    for f in range(2):
                        bk = lring.next()
                        t = mm_group(bk.ap[:, 0:n], [(U[:, tiles0 + k, 128 * f:128 * f + 128], v[:, k, :]) for k in range(kt)], s.ready, bk.freed)
                        s.freed = [t]
                        bk.freed = evac(f, PQ[:, c, f, 0:n], bk.ap[:, 0:n], t, [(pe.sem, pe.n)] if who else [])
                        ev.append(bk.freed)
                for f in range(2):
                    bk = tring.next()
                    t = mm_group(bk.ap[:, 0:n], [(cs64[:, 128 * c:128 * c + 128], PQ[:, c, f, 0:n]) for c in range(2)], ev, bk.freed)
                    bk.freed = evac(f, FTT[:, f, off:off + n], bk.ap[:, 0:n], t)
            barrier()
            sring = Ring([Slot(PS[:, 0:2, :]), Slot(PS[:, 2:4, :]), Slot(PS[:, 4:6, :])])
            tring = bring(6)
            oring = bring(7)

            def da_job(i, h):
                lat = i < 4
                keys = [(0, 512), (512, 768)] if lat else [(512, 768)]
                nk = 6 if lat else 2
                while PA.full() or PTb.full():
                    yield
                P, pt, st = PA.next(), PTb.next(), stats.next()
                te = []
                for m_ in range(2):
                    while sring.full():
                        yield
                    S = sring.next()
                    f, o = h // 2, (h % 2) * 64 + 32 * m_
                    sv = S.ap.rearrange("p b n -> p (b n)")

                    def sc(e, sv=sv, f=f, o=o):
                        c = 0
                        for lo, hi in keys:
                            r_ = e.matmul(sv[:, c:c + hi - lo], QKT[o:o + 32, f, 128 * i:128 * i + 128], QKT[o:o + 32, 2 + f, lo:hi], start=True, stop=True)
                            c += hi - lo
                        return r_
                    t = pe.do(sc, S.freed)
                    yield
                    t1 = dve.do(lambda e, sv=sv, m_=m_: e.tensor_reduce(st.ap[:, m_:m_ + 1], sv[:, 0:128 * nk], AX, ALU.max), t, st.freed)
                    t1 = dve.do(lambda e, m_=m_: e.tensor_scalar(st.ap[:, m_:m_ + 1], st.ap[:, m_:m_ + 1], -(32.0 ** -0.5), None, ALU.mult), t1)
                    t2 = act.do(lambda e, sv=sv, m_=m_: e.activation(P.ap[:, 768 * m_:768 * m_ + 128 * nk], sv[:, 0:128 * nk], ACT.Exp, bias=st.ap[:, m_:m_ + 1],
                                                                     scale=32.0 ** -0.5, accum_out=st.ap[:, 2 + m_:3 + m_]), t1, P.freed)
                    S.freed = t2
                    te.append(t2)
                yield
                t = dve.do(lambda e: e.reciprocal(st.ap[:, 4:6], st.ap[:, 2:4]), te)
                t = dve.do(lambda e: e.tensor_scalar(st.ap[:, 5:6], st.ap[:, 5:6], LB[:, l:l + 1], None, ALU.mult), t)
                p0, p1 = P.ap[:, 0:128 * nk], P.ap[:, 768:768 + 128 * nk]
                t = dve.do(lambda e: e.tensor_scalar(p1, p1, st.ap[:, 5:6], None, ALU.mult), t)
                t = dve.do(lambda e: e.scalar_tensor_tensor(p0, p0, st.ap[:, 4:5], p1, ALU.mult, ALU.subtract), t)
                st.freed = t
                yield
                tv = []
                for a in range(0, nk, 4):
                    b = min(nk, a + 4)
                    bk = tring.next()
                    tt = transposes(bk.ap, [P.ap[:, 128 * j:128 * j + 128] for j in range(a, b)], t, bk.freed)
                    tv.append(evac(1, pt.ap[:, 128 * a:128 * b], bk.ap[:, 0:128 * (b - a)], tt, pt.freed))
                    bk.freed = tv[-1]
                P.freed = tt
                yield
                while oring.full():
                    yield
                ob = oring.next()
                k0 = 0 if lat else 4
                to = mm_group(ob.ap[:, 0:64], [(pt.ap[:, 128 * j:128 * j + 128], DV[:, k0 + j, 64 * h:64 * h + 64]) for j in range(nk)], tv, ob.freed)
                pt.freed = to
                yield
                s2 = stats.next()
                s = hns.next()
                t = act.do(lambda e: e.activation(s.ap[:, 0:64], ob.ap[:, 0:64], ACT.Square, accum_out=s2.ap[:, 0:1]), to, s2.freed, s.freed)
                s.freed = t
                t = rstd_of(s2.ap, 1, 64, t)
                t = dve.do(lambda e: e.tensor_scalar(BR[:, i, 512 + 64 * h:576 + 64 * h], ob.ap[:, 0:64], s2.ap[:, 1:2], None, ALU.mult), t)
                ob.freed = t
                s2.freed = t
            interleave([da_job(i, h) for i in range(nt) for h in range(4)], 3)

            ar.at = base
            pts = barrier()
            spill.dma_out(sp, X, XSP[:, 0:4096], pts)
            xsp = spill.dma_out(sp, XC, XSP[:, 4096:6144], pts)
            sets = []
            for b_ in range(2):
                get = (lambda n, b_=b_: X[:, 768 * n:768 * n + 768] if n < 5 else XC[:, 768 * (n - 5):768 * (n - 4)]) if b_ \
                    else (lambda n: ar.get(768))
                t6 = [get(n) for n in range(7)]
                sets.append((t6[0], t6[1:3], t6[3:5], t6[5].rearrange("p (i n) -> p i n", i=6), t6[6].rearrange("p (i n) -> p i n", i=6)))
            set_free = [[], [xsp]]
            hb = gla_bufs(ar, 128, 128, 6, 2)
            mk = sp.dma(hb["mslot"], hb["mask"].bitcast(mybir.dt.uint16), A["k_mask"], pts)
            spans = [(0, 512), (512, 768)]
            tz = [dve.do(lambda e, q_=q_: e.memset(q_[0][:, 512:768], 0.0), xsp) for q_ in sets] if not both else []
            ready = {}

            def project(h):
                QF, KF, LG, VH, GH = sets[h % 2]
                fr = set_free[h % 2]
                rr = bring(6, 7)
                w, wv = load_w([(0, 128, w2[:, 128 * h:128 * h + 128]), (128, 128, w2[:, 1536 + 128 * h:1536 + 128 * h + 128]),
                                (256, 128, w2[:, 2048 + 128 * h:2048 + 128 * h + 128])], 8, 384)
                hp = []

                def qcons(lo, hi, p, t):
                    t = act.do(lambda e: e.activation(QF[:, lo:hi], p, ACT.Silu), t, fr)
                    hp.append(t)
                    return t
                for sp1 in spans if both else spans[:1]:
                    lin_feat(hk, [sp1], w, wv, 0, 128, rr, qcons, [])
                    yield
                lns = []
                for d in range(2):
                    def zcons(lo, hi, p, t):
                        lb, om = LOW[:, d, l, h:h + 1], ONEM[:, d, l, h:h + 1]
                        o = LG[d][:, lo:hi]
                        k_ = KF[d][:, lo:hi]
                        ta = act.do(lambda e: e.activation(o, p, ACT.Sigmoid), t, fr)
                        tk = act.do(lambda e: e.activation(k_, p, ACT.Sigmoid, scale=-1.0), t)
                        hp.append(dve.do(lambda e: e.tensor_scalar(k_, k_, om, None, ALU.mult), tk))
                        tb = dve.do(lambda e: e.tensor_scalar(o, o, om, lb, ALU.mult, ALU.add), ta)
                        lns.append((o, dve.do(lambda e: e.tensor_scalar(o, o, 1e-19, None, ALU.max), tb)))
                        return [ta, tk]
                    for sp1 in spans:
                        lin_feat(hk, [sp1], w, wv, 128 + 128 * d, 128, rr, zcons, [])
                        yield
                w, wv = load_w([(0, 128, w2[:, 512 + 128 * h:512 + 128 * h + 128]), (128, 128, w2[:, 1024 + 128 * h:1024 + 128 * h + 128])], 8, 256)

                def vcons(i, p, t):
                    t1 = dve.do(lambda e: e.tensor_copy(VH[:, i, :], p[:, 0:128]), t, fr)
                    t2 = act.do(lambda e: e.activation(GH[:, i, :], p[:, 128:256], ACT.Silu), t, t1)
                    hp.extend([t1, t2])
                    return [t1, t2]
                for i in range(6):
                    lin_tok(hk, [i], w, wv, 0, 256, rr, vcons, [])
                    yield
                for o, tb in lns:
                    hp.append(act.do(lambda e: e.activation(o, o, ACT.Ln), tb))
                ready[h] = hp

            def recur(h):
                QF, KF, LG, VH, GH = sets[h % 2]

                def fin(i, p, t):
                    st = stats.next()
                    s = hns.next()
                    t2 = act.do(lambda e: e.activation(s.ap[:, 0:128], p, ACT.Square, accum_out=st.ap[:, 0:1]), t, st.freed, s.freed)
                    s.freed = t2
                    t2 = rstd_of(st.ap, 1, 128, t2)

                    def end():
                        st.freed = dve.do(lambda e: e.scalar_tensor_tensor(BR[:, i, 128 * h:128 * h + 128], p, st.ap[:, 1:2], GH[:, i, :],
                                                                           ALU.mult, ALU.mult), t2)
                        return st.freed
                    return end
                yield from decayed(128, 128, 6, QF, [(KF[0], LG[0], 0, [4, 5, 0, 1, 2, 3]), (KF[1], LG[1], 1, [5, 4, 3, 2, 1, 0])],
                                   lambda i: VH[:, i, :], list(range(nt)), hb, Ring([pair(0), pair(2)]),
                                   bring(4), bring(5), fin, [mk, ready[h], tz])
                set_free[h % 2] = [(q_.sem, q_.n) for q_ in compute]
            interleave([project(0)], 1)
            for h in range(4):
                interleave([recur(h)] + ([project(h + 1)] if h < 3 else []), 2)
            pts = barrier()
            spill.dma_in(sp, X, XSP[:, 0:4096], pts, xsp)
            xready = spill.dma_in(sp, XC, XSP[:, 4096:6144])
            for q_ in (act, dve, pool):
                q_.wait(xready)
            ar.at = base
            Y = ar.get(6 * 1024).rearrange("p (i n) -> p i n", i=6)
            GV, gpt = residual_rows(ar, l, 2, gcol(1))
            ON = VEC[:, VO["hg_onorm"] + l:VO["hg_onorm"] + l + 1]
            project_out(BR, 6, range(nt), lambda k: ON if k < 4 else SUBC[:, l:l + 1], FTT, A["w_out_2"][l],
                        lambda i, c, p, t: evac(i + c, Y[:, i, 512 * c:512 * c + 512], p, t))
            barrier()
            for i in range(nt):
                add_normed(Y, i, GV, gpt)
            barrier()
            dump_now(f"y{l}", X)
            TT = 128 * nt
            HR, WC, AC = claim(("HR", 2 * 8 * TT, F32R), ("WC", 3 * 2048, F32R), ("AC", 2 * 4 * TT, F32R))
            xar = Arena(EX, 4096)
            HH = [HR[:, 8 * TT * p_:8 * TT * (p_ + 1)].rearrange("p (k n) -> p k n", k=8) for p_ in range(2)]
            tmps = Ring([Slot(xar.get(512)) for _ in range(2)])
            pr = Ring([Slot(xar.get(512)) for _ in range(3)])
            cols = [scale_cols(xar, l, 4, gcol(2), who) for who in range(2)]
            th = [norm_split(xt(i), HH, 128 * i, cols[i // 4][0], modcol(l, 3, i // 4), bring(0, 1, 2, 3), tmps, cols[i // 4][1])
                  for i in range(nt)]
            wi, wo = A["w_ffn_in_2"][l], A["w_ffn_out_2"][l]
            wcr = Ring([Slot(WC[:, 2048 * i:2048 * i + 2048]) for i in range(3)])
            acs = [Slot(AC[:, 4 * TT * i:4 * TT * (i + 1)].rearrange("p (s j n) -> p s j n", s=2, j=2)) for i in range(2)]
            spans = [(0, 512), (512, 768)] if both else [(0, 512)]
            Y = HT[:, 0:nt * 1024].rearrange("p (i n) -> p i n", i=nt)
            sched = []
            for b in range(12):
                if b < 11:
                    sched += [("up", b, kp) for kp in range(4)] + [("act", b, 0)]
                if b >= 1:
                    sched += [("down", b - 1, c) for c in range(2)]
            work = [x for x in sched if x[0] != "act"]
            staged, conv = {}, {}

            def convert(kind, b, c):
                if kind == "up" and c == 0:
                    staged["up"] = load_w([(0, 256, wi[:, 256 * b:256 * b + 256]), (256, 256, wi[:, FF + 256 * b:FF + 256 * b + 256])], 8, 512)
                if kind == "down" and c == 0:
                    staged["down"] = load_w(wo[256 * b:256 * b + 256, :], 2, 1024)
                w, wv = staged[kind]
                src = wv[:, 2 * c:2 * c + 2, :] if kind == "up" else wv[:, :, 512 * c:512 * c + 512]
                s = wcr.next()
                o = s.ap.rearrange("p (s k n) -> p s k n", s=2, k=2)
                t1, t2 = split(o[:, 0], o[:, 1], src, w.ready, s.freed)
                if c == (3 if kind == "up" else 1):
                    w.freed = t2
                conv[kind, b, c] = (s, o, [t1, t2])

            ubank = {}
            for q_ in range(4):
                ubank[q_, 0] = (q_, PS[:, q_, 0:512])
                ubank[q_, 1] = (4 + q_ // 2, PS[:, 4 + q_ // 2, 256 * (q_ % 2):256 * (q_ % 2) + 256])
            drn = Ring([banks[6], banks[7]] if both else [banks[i] for i in (4, 5, 6, 7)])
            updone = {}
            yprev = {}
            for n_, x in enumerate(work[:2]):
                convert(*x)
            at = 2
            for kind, b, c in sched:
                if kind != "act" and at < len(work):
                    convert(*work[at])
                    at += 1
                if kind == "up":
                    s, o, rdy = conv.pop((kind, b, c))
                    need = [banks[i].freed for i in range(6)] if c == 0 else []

                    def up(e):
                        for q_ in range(4):
                            for sp_, (lo, hi) in enumerate(spans):
                                bi, p = ubank[q_, sp_]
                                for kk in range(2):
                                    k = 2 * c + kk
                                    st = c == 0 and kk == 0 and not (sp_ == 1 and q_ % 2 == 1)
                                    wh, wl = o[:, 0, kk, 128 * q_:128 * q_ + 128], o[:, 1, kk, 128 * q_:128 * q_ + 128]
                                    e.matmul(p, wh, HH[0][:, k, lo:hi], start=st, stop=False, skip_group_check=True)
                                    e.matmul(p, wh, HH[1][:, k, lo:hi], start=False, stop=False, skip_group_check=True)
                                    m = e.matmul(p, wl, HH[0][:, k, lo:hi], start=False, stop=c == 3 and kk == 1, skip_group_check=True)
                        return m
                    s.freed = updone[b] = pe.do(up, rdy, th, need)
                elif kind == "act":
                    a = acs[b % 2]
                    pts = []
                    fr = {}
                    for j2 in range(2):
                        for sp_, (lo, hi) in enumerate(spans):
                            (bg, pg), (bu, pu) = ubank[j2, sp_], ubank[2 + j2, sp_]
                            h = pr.next()
                            v = h.ap[:, 0:hi - lo]
                            t = act.do(lambda e: e.activation(v, pg, ACT.Silu), updone[b], h.freed)
                            fr.setdefault(bg, []).append(t)
                            t = dve.do(lambda e: e.tensor_tensor(v, v, pu, ALU.mult), t)
                            fr.setdefault(bu, []).append(t)
                            t1, t2 = split(a.ap[:, 0, j2, lo:hi], a.ap[:, 1, j2, lo:hi], v, t, a.freed)
                            h.freed = t2
                            pts += [t1, t2]
                    for bi, t in fr.items():
                        banks[bi].freed = t
                    a.ready = pts
                else:
                    s, o, rdy = conv.pop((kind, b, c))
                    a = acs[b % 2]
                    for i in range(nt):
                        bk = drn.next()
                        tk = slice(128 * i, 128 * i + 128)

                        def down(e):
                            for kk in range(2):
                                ah, al = a.ap[:, 0, kk, tk], a.ap[:, 1, kk, tk]
                                e.matmul(bk.ap, ah, o[:, 0, kk, :], start=kk == 0, stop=False, skip_group_check=True)
                                e.matmul(bk.ap, ah, o[:, 1, kk, :], start=False, stop=False, skip_group_check=True)
                                m = e.matmul(bk.ap, al, o[:, 0, kk, :], start=False, stop=kk == 1, skip_group_check=True)
                            return m
                        t = pe.do(down, rdy, a.ready, bk.freed)
                        y = Y[:, i, 512 * c:512 * c + 512]
                        if b == 0:
                            bk.freed = dve.do(lambda e: e.tensor_copy(y, bk.ap), t)
                        else:
                            bk.freed = dve.do(lambda e: e.tensor_tensor(y, y, bk.ap, ALU.add), t, yprev[i, c])
                        yprev[i, c] = bk.freed
                    s.freed = t
                    if c == 1:
                        a.freed = t
            barrier()
            xar = Arena(EX, 4096)
            GV, gpt = residual_rows(xar, l, 5, gcol(3))
            for i in range(nt):
                add_normed(Y, i, GV, gpt)
            barrier()
            dump_now(f"z{l}", X)
            AR, = claim(("AR", ARN, F32))

        outs = Slot(None, sem("s_out"))
        ot = sp.dma(outs, out.rearrange("o (i p) n -> p (o i) n", p=128), X3, barrier())
        sp.wait(ot, dumps)


_INS = ["x", "mem", "mem_norm_w", "norm_w", "w_memkv", "w_out", "w_in_a", "w_gate_up", "b_gate", "gla_norm_w",
        "w_in_b", "final_norm_w", "c_2", "ctx_2", "c_ctx_2", "w_mod_2", "b_mod_2", "norm_g_2", "w_in_2", "w_out_2",
        "hg_lb_logits_2", "hg_onorm_2", "da_lambda_2", "da_subln_2", "w_ffn_in_2", "w_ffn_out_2"]


def kernel(**inputs):
    import numpy as _np
    import concourse.bacc as _bacc
    from concourse import mybir as _mybir
    from concourse.bass_utils import run_bass_kernel_spmd as _run

    nc = _bacc.Bacc("TRN2", target_bir_lowering=False, num_devices=1)
    arrays, A = {}, {}
    for name in _INS:
        a = _np.ascontiguousarray(inputs[name])
        arrays[f"in_{name}"] = a
        A[name] = nc.dram_tensor(f"in_{name}", a.shape, _mybir.dt.from_np(a.dtype), kind="ExternalInput").ap()
    for name, a in zip(("k_const", "k_dft", "k_dftc", "k_mask"), shape_tables()):
        arrays[name] = a
        A[name] = nc.dram_tensor(name, a.shape, _mybir.dt.from_np(a.dtype), kind="ExternalInput").ap()
    out = nc.dram_tensor("out_0", (1, 512, 1024), _mybir.dt.float32, kind="ExternalOutput").ap()
    build(nc, A, out)
    r = _run(nc, [arrays], core_ids=[0])
    return r.results[0]["out_0"]
```

```python
import math
from contextlib import ExitStack

import numpy as np
import concourse.bass as bass
from concourse import mybir

F32 = mybir.dt.float32
F32R = mybir.dt.float32r
BF16 = mybir.dt.bfloat16
ALU = mybir.AluOpType
ACT = mybir.ActivationFunctionType
AX = mybir.AxisListType.X
EPS = 1e-6
D = 1024
T = 512
TC = 256
FF = 2816

CONST_WIDTHS = [("ident", 128), ("ones", 128), ("reset", 768), ("eps", 8), ("drope", 128), ("arope", 128),
                ("cs64", 256), ("dil", 1280)]
CW = {}
_o = 0
for _n, _w in CONST_WIDTHS:
    CW[_n] = (_o, _o + _w)
    _o += _w
CTOT = _o
CBASE = CW["dil"][0]
VROWS = [("mem_norm", 8), ("norm", 16), ("norm_g", 64), ("hg_onorm", 2), ("hg_lb", 16), ("c", 8), ("c_ctx", 8)]
VO = {}
_o = 0
for _n, _w in VROWS:
    VO[_n] = _o
    _o += _w
VTOT = _o


def shape_tables():
    c = np.zeros((128, CTOT), np.float32)
    p = np.arange(128)

    def put(name, a):
        lo, hi = CW[name]
        c[:, lo:hi] = np.asarray(a, np.float32).reshape(128, hi - lo)

    put("ident", np.eye(128))
    put("ones", np.ones((128, 128)))
    r = np.ones((128, 768))
    r[:, ::128] = 0
    put("reset", r)
    e = np.zeros((128, 8))
    e[:, 0] = EPS
    e[:, 1] = 1.0
    put("eps", e)
    t = p[:, None] + 128 * np.arange(4)[None, :]
    inv = 500000.0 ** (-np.arange(16) / 16.0)
    ang = (t[:, :, None].astype(np.float32) * inv.astype(np.float32)[None, None, :]).astype(np.float32)
    put("drope", np.stack([np.cos(ang), np.sin(ang)], 1))
    invf = (1.0 / (10000.0 ** (np.arange(0, 16, 2) / 16.0))).astype(np.float32)
    rc = np.stack([t // 64, t % 64], -1).astype(np.float32)
    ang = rc[:, :, :, None] * invf[None, None, None, :]
    put("arope", np.stack([np.cos(ang), np.sin(ang)], 1))
    k = np.arange(64)
    a64 = 2 * np.pi * ((k[:, None] * k[None, :]) % 64) / 64
    z = np.zeros((128, 256))
    for b in range(2):
        z[64 * b:64 * b + 64, 64 * b:64 * b + 64] = np.cos(a64)
        z[64 * b:64 * b + 64, 128 + 64 * b:128 + 64 * b + 64] = -np.sin(a64)
    put("cs64", z)
    s, q = p[:, None], p[None, :]
    lv = np.zeros((128, 2, 8, 128))
    for l in range(7):
        h = 64 >> l
        same = (s // (2 * h)) == (q // (2 * h))
        lv[:, 0, l] = same & (s % (2 * h) < h) & (q % (2 * h) >= h)
        lv[:, 1, l] = same & (s % (2 * h) >= h) & (q % (2 * h) < h)
    lv[:, :, 7] = np.eye(128)[:, None, :]
    neg = -1e30
    qq, ss = p[:, None], p[None, :]
    g0 = np.concatenate([np.where(ss >= qq, 0, neg), np.where(ss <= qq, 0, neg)], 1)
    out = [g0]
    for r in (4, 16):
        off = np.where((qq - ss) % r == 0, 0, neg)
        dg = np.where(((qq - ss) % r == 0) & (ss <= qq), 0, neg)
        out.append(np.concatenate([off, off, off, dg], 1))
    put("dil", np.concatenate(out, 1))

    def dft(n):
        j = np.arange(n)
        a = 2 * np.pi * ((j[:, None] * j[None, :]) % n) / n
        w = np.stack([np.cos(a), np.sin(a)]) / np.sqrt(n * 64.0)
        return w.reshape(2, n // 128, 128, n).transpose(2, 0, 1, 3).reshape(128, -1).astype(np.float32)

    bits = lv.reshape(128, 2048).astype(np.uint16) * np.uint16(0x3F80)
    return c, dft(T), dft(TC), bits


def flat(x):
    if x is None:
        return []
    if isinstance(x, tuple) and len(x) == 2 and isinstance(x[1], int):
        return [x]
    out = []
    for y in x:
        out += flat(y)
    return out


class Lane:

    def __init__(self, e, sem):
        self.e, self.sem, self.n, self.seen = e, sem, 0, {}

    def wait(self, *points):
        for sem, value in flat(points):
            if self.seen.get(id(sem), 0) < value:
                self.seen[id(sem)] = value
                self.e.wait_ge(sem, value)

    def do(self, fn, *after):
        self.wait(*after)
        self.n += 1
        fn(self.e).then_inc(self.sem, 1)
        return (self.sem, self.n)

    def dma(self, slot, out, in_, *after):
        self.wait(slot.freed, *after)
        slot.n += 16
        self.e.dma_start(out, in_).then_inc(slot.sem, 16)
        return (slot.sem, slot.n)


class Scalar:

    SETS = {ACT.Exp: "natural_log_exp_and_others", ACT.Ln: "natural_log_exp_and_others",
            ACT.Silu: "silu_and_others", ACT.Sigmoid: "sigmoid_and_others"}

    def __init__(self, e):
        self.e, self.loaded = e, None
        self.wait_ge, self.dma_start = e.wait_ge, e.dma_start

    def activation(self, out, in_, func, **kw):
        need = self.SETS.get(func)
        if need is not None and need != self.loaded:
            self.e.preload_act_table_set(need)
            self.loaded = need
        return self.e.activation(out, in_, func, **kw)


class Slot:

    def __init__(self, ap, sem=None):
        self.ap, self.sem, self.n, self.freed = ap, sem, 0, []

    @property
    def freed(self):
        return self._freed

    @freed.setter
    def freed(self, points):
        self._freed, self.busy = points, False


class Ring:
    def __init__(self, slots):
        self.slots, self.i = slots, 0

    def full(self):
        return all(s.busy for s in self.slots)

    def next(self):
        assert not self.full()
        while self.slots[self.i % len(self.slots)].busy:
            self.i += 1
        s = self.slots[self.i % len(self.slots)]
        s.busy = True
        self.i += 1
        return s


def together(lead, follow, rate, start=0):
    for _ in range(start):
        next(follow, None)
    due = 0
    for _ in lead:
        due += rate
        while due >= 1:
            due -= 1
            next(follow, None)
    for _ in follow:
        pass


def interleave(jobs, width):
    live, jobs = [], list(jobs)
    while live or jobs:
        while jobs and len(live) < width:
            live.append(jobs.pop(0))
        for j in list(live):
            try:
                next(j)
            except StopIteration:
                live.remove(j)


def build(nc, A, out, dump=None):
    with ExitStack() as ctx:
        total = [0]

        def sb(name, cols):
            total[0] += cols * 4
            return ctx.enter_context(nc.sbuf_tensor(name, [128, cols], F32))[:, :]

        def sem(name):
            return ctx.enter_context(nc.semaphore(name))

        PS = ctx.enter_context(nc.psum_tensor("PS", [128, 8, 512], F32))[:, :, :]
        pe, act, dve, pool, sp = (Lane(e, sem(f"s_{n}")) for e, n in (
            (nc.tensor, "pe"), (Scalar(nc.scalar), "act"), (nc.vector, "dve"), (nc.gpsimd, "pool"), (nc.sync, "sp")))
        compute = [pe, act, dve, pool]

        CON = sb("CON", CBASE)
        VEC = sb("VEC", VTOT)
        BMOD = sb("BMOD", 96)
        MOD = sb("MOD", 2 * 96)
        MISC = sb("MISC", 128)
        STAT = sb("STAT", 64 * 8)
        X = sb("X", 4096)
        XC = sb("XC", 2048)
        HT = sb("HT", 8 * 768)
        WR = sb("WR", 2 * 4096)
        HNB = sb("HNB", 1024)
        EX = sb("EX", 4096)
        ARN = 53150 - total[0] // 4
        arena = [ExitStack()]
        uid = [0]

        def claim(*shapes):
            arena[0].close()
            arena[0] = ctx.enter_context(ExitStack())
            uid[0] += 1
            return [arena[0].enter_context(nc.sbuf_tensor(f"{n_}{uid[0]}", [128, c_], t_))[:, :] for n_, c_, t_ in shapes]

        AR, = claim(("AR", ARN, F32))

        def con(name):
            lo, hi = CW[name]
            return CON[:, lo:hi]

        ident = con("ident")
        ones = con("ones")
        eps = con("eps")[:, 0:1]
        wring = Ring([Slot(WR[:, 4096 * i:4096 * (i + 1)], sem(f"s_w{i}")) for i in range(2)])
        stats = Ring([Slot(STAT[:, 8 * i:8 * i + 8]) for i in range(64)])
        hns = Ring([Slot(HNB)])
        hn2 = Ring([hns.slots[0], Slot(EX[:, 3072:4096])])
        banks = [Slot(PS[:, b, :]) for b in range(8)]
        misc = Slot(None, sem("s_misc"))
        mslot = Slot(None, sem("s_mask"))
        XSP = nc.dram_tensor("x_spill", (128, 6144), F32, kind="Internal").ap()

        class Spill:

            def __init__(self):
                self.slot = Slot(None, sem("s_spill"))

            def dma_out(self, q, src, dst, *after):
                return q.dma(self.slot, dst, src, *after)

            def dma_in(self, q, dst, src, *after):
                return q.dma(self.slot, dst, src, *after)

        spill = Spill()

        def bring(*ids):
            return Ring([banks[i] for i in ids])

        def pair(i):
            return Slot(PS[:, i:i + 2, :])

        def barrier():
            points = [(l.sem, l.n) for l in compute]
            for l in compute:
                l.wait(*points)
            return points

        class Arena:
            def __init__(self, base=None, size=None):
                self.at, self.base, self.size = 0, AR if base is None else base, size or ARN

            def get(self, cols):
                assert self.at + cols <= self.size, (self.at, cols, self.size)
                a = self.base[:, self.at:self.at + cols]
                self.at += cols
                return a

        def evac(n, out_, in_, *after, scale=None):
            if n % 2:
                return act.do(lambda e: e.activation(out_, in_, ACT.Copy, scale=1.0 if scale is None else scale), *after)
            if scale is None:
                return dve.do(lambda e: e.tensor_copy(out_, in_), *after)
            return dve.do(lambda e: e.tensor_scalar(out_, in_, scale, None, ALU.mult), *after)

        def load_w(src, kt, n, ring=wring):
            s = ring.next()
            v = s.ap[:, 0:kt * n].rearrange("p (k n) -> p k n", k=kt)
            src = src if isinstance(src, list) else [(0, n, src)]
            for lo, w, a in src:
                s.ready = sp.dma(s, v[:, :, lo:lo + w], a.rearrange("(k p) n -> p k n", p=128))
            return s, v

        def mm_group(psum, pairs, *after, start=True, stop=True):
            def go(e):
                for i, (l, r) in enumerate(pairs):
                    m = e.matmul(psum, l, r, start=start and i == 0, stop=stop and i == len(pairs) - 1,
                                 skip_group_check=True)
                return m
            return pe.do(go, *after)

        def transposes(bank, ins, *after):
            def go(e):
                for i, a in enumerate(ins):
                    m = e.transpose(bank[0:a.shape[1], 128 * i:128 * i + a.shape[0]], a,
                                    ident[0:a.shape[0], 0:a.shape[0]])
                return m
            return pe.do(go, *after)

        def rstd_of(st, n, count, after):
            t = act.do(lambda e: e.activation(st[:, n:2 * n], st[:, 0:n], ACT.Ln, scale=1.0 / count, bias=eps), after)
            return act.do(lambda e: e.activation(st[:, n:2 * n], st[:, n:2 * n], ACT.Exp, scale=-0.5), t)

        def norm_T(src, dst, col0, g, b, ring, after):
            s, st = hn2.next(), stats.next()
            t = act.do(lambda e: e.activation(s.ap, src, ACT.Square, accum_out=st.ap[:, 0:1]), after, s.freed, st.freed)
            t = rstd_of(st.ap, 1, D, t)
            t = dve.do(lambda e: e.tensor_scalar(s.ap, src, st.ap[:, 1:2], None, ALU.mult), t)
            st.freed = t
            done = []
            for hf in range(2):
                bk = ring.next()
                tt = transposes(bk.ap, [s.ap[:, 128 * (4 * hf + k):128 * (4 * hf + k + 1)] for k in range(4)], t, bk.freed)
                o = dst[:, 4 * hf:4 * hf + 4, col0:col0 + 128]
                i3 = bk.ap.rearrange("p (k n) -> p k n", k=4)
                gb = g[:, 4 * hf:4 * hf + 4].unsqueeze(2).broadcast_to([128, 4, 128])
                te = dve.do(lambda e, o=o, i3=i3, gb=gb: e.tensor_tensor(o, i3, gb, ALU.mult), tt)
                bk.freed = te
                if b is not None:
                    bb = b[:, 4 * hf:4 * hf + 4].unsqueeze(2).broadcast_to([128, 4, 128])
                    te = dve.do(lambda e, o=o, bb=bb: e.tensor_tensor(o, o, bb, ALU.add), te)
                done.append(te)
            s.freed = tt
            return done

        def split(hi, lo, src, *after):
            t1 = act.do(lambda e: e.activation(hi, src, ACT.Copy), *after)
            t2 = dve.do(lambda e: e.tensor_tensor(lo, src, hi.bitcast(F32), ALU.subtract), t1, *after)
            return t1, t2

        def norm_split(src, dst, col0, g, b, ring, tmps, after, done):
            s, st = hn2.next(), stats.next()
            t = act.do(lambda e: e.activation(s.ap, src, ACT.Square, accum_out=st.ap[:, 0:1]), after, s.freed, st.freed)
            t = rstd_of(st.ap, 1, D, t)
            t = dve.do(lambda e: e.tensor_scalar(s.ap, src, st.ap[:, 1:2], None, ALU.mult), t)
            st.freed = t
            yield
            for hf in range(2):
                bk, m = ring.next(), tmps.next()
                tt = transposes(bk.ap, [s.ap[:, 128 * (4 * hf + k):128 * (4 * hf + k + 1)] for k in range(4)], t, bk.freed)
                m3 = m.ap.rearrange("p (k n) -> p k n", k=4)
                i3 = bk.ap.rearrange("p (k n) -> p k n", k=4)
                gb = g[:, 4 * hf:4 * hf + 4].unsqueeze(2).broadcast_to([128, 4, 128])
                te = dve.do(lambda e: e.tensor_tensor(m3, i3, gb, ALU.mult), tt, m.freed)
                bk.freed = te
                if b is not None:
                    bb = b[:, 4 * hf:4 * hf + 4].unsqueeze(2).broadcast_to([128, 4, 128])
                    te = dve.do(lambda e: e.tensor_tensor(m3, m3, bb, ALU.add), te)
                o = [d[:, 4 * hf:4 * hf + 4, col0:col0 + 128] for d in dst]
                t1, t2 = split(o[0], o[1], m3, te)
                m.freed = t2
                done += [t1, t2]
            s.freed = tt

        def lin_tok(act_k, tiles, w, wv, c0, n, ring, consume, after):
            K = wv.shape[1]
            for i in tiles:
                bk = ring.next()
                t = mm_group(bk.ap[:, 0:n], [(act_k(k)[:, 128 * i:128 * i + 128], wv[:, k, c0:c0 + n]) for k in range(K)],
                             w.ready, after, bk.freed)
                bk.freed = consume(i, bk.ap[:, 0:n], t)
            w.freed = [t]

        def lin_feat(act_k, spans, w, wv, c0, m, ring, consume, after):
            K = wv.shape[1]
            for lo, hi in spans:
                bk = ring.next()
                p = bk.ap[0:m, 0:hi - lo]
                t = mm_group(p, [(wv[:, k, c0:c0 + m], act_k(k)[:, lo:hi]) for k in range(K)], w.ready, after, bk.freed)
                bk.freed = consume(lo, hi, p, t)
            w.freed = [t]

        X3 = X.rearrange("p (i n) -> p i n", i=4)
        XC3 = XC.rearrange("p (i n) -> p i n", i=2)
        HT3 = HT.rearrange("p (k n) -> p k n", k=8)
        hk = lambda k: HT3[:, k, :]

        dumps = []

        def dump_now(name, ap):
            if dump is None:
                return
            pts = barrier()
            s = Slot(None, sem("d_" + name))
            sp.dma(s, dump(name, ap), ap, pts)
            dumps.append((s.sem, s.n))
            for l in compute:
                l.wait((s.sem, s.n))

        sp.dma(misc, CON, A["k_const"][:, 0:CBASE])
        ar = Arena()
        VR = ar.get(128)
        BR_ = ar.get(128)
        GR = ar.get(256)
        LAMR = ar.get(256)
        SC = ar.get(1024)
        rows = {"mem_norm": A["mem_norm_w"].rearrange("(a n) -> a n", n=128),
                "norm": A["norm_w"].rearrange("l (a n) -> (l a) n", n=128),
                "norm_g": A["norm_g_2"].rearrange("l g (a n) -> (l g a) n", n=128),
                "hg_onorm": A["hg_onorm_2"],
                "hg_lb": A["hg_lb_logits_2"].rearrange("d l (a n) -> (d l a) n", n=128),
                "c": A["c_2"].rearrange("o (a n) -> (o a) n", n=128),
                "c_ctx": A["c_ctx_2"].rearrange("(a n) -> a n", n=128)}
        for n_, w_ in VROWS:
            sp.dma(misc, VR[VO[n_]:VO[n_] + w_, :], rows[n_])
        sp.dma(misc, BR_[0:96, :], A["b_mod_2"].rearrange("l (a n) -> (l a) n", n=128))
        sp.dma(misc, GR[0:4, 0:96], A["b_gate"].rearrange("o (a n) -> (o a) n", n=96))
        gw = A["gla_norm_w"]
        sp.dma(misc, GR[0:1, 128:256], gw[:, 0:128])
        sp.dma(misc, GR[1:2, 128:192], gw[:, 128:192])
        sp.dma(misc, GR[1:2, 192:256], gw[:, 0:64])
        sp.dma(misc, GR[2:3, 128:256], gw[:, 64:192])
        sub = A["da_subln_2"]
        for h_ in range(2):
            sp.dma(misc, GR[3:5, 128 + 64 * h_:192 + 64 * h_], sub)
        for l in range(2):
            lm = A["da_lambda_2"][l:l + 1].rearrange("o a n -> o (a n)")
            sp.dma(misc, LAMR[:, 128 * l:128 * l + 128], lm.broadcast_to([128, 128]))
        cready = (misc.sem, misc.n)
        MX = EX[:, 0:2048].rearrange("p (i n) -> p i n", i=2)
        ms = Slot(None, sem("s_mem"))
        mready = sp.dma(ms, MX, A["mem"].rearrange("o (i p) n -> p (o i) n", p=128))
        xs = Slot(None, sem("s_x"))
        xready = sp.dma(xs, X3, A["x"].rearrange("o (i p) n -> p (o i) n", p=128))
        xcs = Slot(None, sem("s_xc"))
        xcready = sp.dma(xcs, XC3, A["ctx_2"].rearrange("o (i p) n -> p (o i) n", p=128))

        b0 = bring(0, 1)
        bk = b0.next()
        t = transposes(bk.ap, [VR[0:VTOT, :], BR_[0:96, :], GR[0:4, 0:96], GR[0:5, 128:256]], cready)
        t1 = dve.do(lambda e: e.tensor_copy(VEC, bk.ap[:, 0:VTOT]), t)
        t2 = dve.do(lambda e: e.tensor_copy(BMOD, bk.ap[:, 128:224]), t)
        t3 = dve.do(lambda e: e.tensor_copy(MISC[0:96, 0:4], bk.ap[0:96, 256:260]), t)
        t4 = dve.do(lambda e: e.tensor_copy(MISC[:, 4:9], bk.ap[:, 384:389]), t)
        bk.freed = [t1, t2, t3, t4]
        NBG, GNW, SUBC = MISC[0:96, 0:4], MISC[:, 4:7], MISC[:, 7:9]
        LIN = [0.8 - 0.6 * math.exp(-0.3 * l) for l in range(2)]
        for l in range(2):
            dve.do(lambda e: e.tensor_scalar(MISC[:, 7 + l:8 + l], MISC[:, 7 + l:8 + l], 1.0 - LIN[l], None, ALU.mult), t4)
        LB = MISC[:, 9:11]
        for l in range(2):
            a4 = LAMR[:, 128 * l:128 * l + 128].rearrange("p (a n) -> p a n", a=4)
            ta = dve.do(lambda e, a4=a4: e.tensor_tensor(SC[:, 0:64].rearrange("p (a n) -> p a n", a=2),
                                                         a4[:, 0:4:2, :], a4[:, 1:4:2, :], ALU.mult), cready,
                        [(dve.sem, dve.n)])
            ta = dve.do(lambda e: e.tensor_reduce(SC[:, 64:66], SC[:, 0:64].rearrange("p (a n) -> p a n", a=2), AX, ALU.add), ta)
            ta = act.do(lambda e: e.activation(SC[:, 66:68], SC[:, 64:66], ACT.Exp), ta)
            ta = dve.do(lambda e: e.tensor_tensor(SC[:, 68:69], SC[:, 66:67], SC[:, 67:68], ALU.subtract), ta)
            dve.do(lambda e, l=l: e.tensor_scalar(LB[:, l:l + 1], SC[:, 68:69], LIN[l], None, ALU.add), ta)
        L3 = VEC[:, VO["hg_lb"]:VO["hg_lb"] + 16].rearrange("p (d l a) -> p d l a", d=2, l=2)
        LOW = MISC[:, 16:32].rearrange("p (d l a) -> p d l a", d=2, l=2)
        ONEM = MISC[:, 32:48].rearrange("p (d l a) -> p d l a", d=2, l=2)
        w4 = [SC[:, 128 + 8 * i:136 + 8 * i].rearrange("p (d a) -> p d a", d=2) for i in range(6)]
        ta = dve.do(lambda e: e.tensor_tensor(w4[0], L3[:, :, 0, :], L3[:, :, 1, :], ALU.max), t1)
        tb = dve.do(lambda e: e.tensor_tensor(w4[1], L3[:, :, 0, :], w4[0], ALU.subtract), ta)
        tc_ = dve.do(lambda e: e.tensor_tensor(w4[2], L3[:, :, 1, :], w4[0], ALU.subtract), ta)
        tb = act.do(lambda e: e.activation(w4[1], w4[1], ACT.Exp), tb)
        tc_ = act.do(lambda e: e.activation(w4[2], w4[2], ACT.Exp), tc_)
        ta = dve.do(lambda e: e.tensor_tensor(w4[3], w4[1], w4[2], ALU.add), tb, tc_)
        ta = dve.do(lambda e: e.reciprocal(w4[4], w4[3]), ta)
        tb = dve.do(lambda e: e.tensor_tensor(w4[1], w4[1], w4[4], ALU.mult), ta)
        tc_ = dve.do(lambda e: e.tensor_tensor(w4[2], w4[2], w4[4], ALU.mult), ta)
        dve.do(lambda e: e.tensor_tensor(LOW[:, :, 0, :], w4[1], w4[1], ALU.subtract), tb)
        ta = dve.do(lambda e: e.tensor_tensor(w4[5], w4[1], w4[2], ALU.add), tb, tc_)
        ta = dve.do(lambda e: e.tensor_tensor(LOW[:, :, 1, :], w4[5], w4[1], ALU.subtract), ta)
        dve.do(lambda e: e.tensor_scalar(ONEM, LOW, -1.0, 1.0, ALU.mult, ALU.add), ta)
        CV = MISC[:, 64:80].rearrange("p (k c) -> p k c", c=2)
        for i, n_ in enumerate(("c", "c_ctx")):
            act.do(lambda e, i=i, n_=n_: e.activation(CV[:, :, i], VEC[:, VO[n_]:VO[n_] + 8], ACT.Silu), t1)
        barrier()

        def modulation(layers, halves, mbank, tbank):
            for l in layers:
                for c in range(12):
                    w, wv = load_w(A["w_mod_2"][l][:, 512 * c:512 * c + 512], 8, 512)
                    mm_group(mbank.ap[0:2, :], [(CV[:, k, :], wv[:, k, :]) for k in range(4)], w.ready, mbank.freed, stop=False)
                    yield
                    t = mm_group(mbank.ap[0:2, :], [(CV[:, k, :], wv[:, k, :]) for k in range(4, 8)], start=False)
                    w.freed = t
                    half = halves.next()
                    t = dve.do(lambda e: e.tensor_copy(half.ap, mbank.ap[0:2, :]), t, half.freed)
                    mbank.freed = t
                    yield
                    tt = pe.do(lambda e: [e.transpose(tbank.ap[:, 2 * j:2 * j + 2], half.ap[:, 128 * j:128 * j + 128], ident[0:2, 0:2])
                                          for j in range(4)][-1], t, tbank.freed)
                    half.freed = tt
                    o = MOD[:, 96 * l + 8 * c:96 * l + 8 * c + 8].rearrange("p (j c) -> p j c", c=2)
                    bb = BMOD[:, 48 * l + 4 * c:48 * l + 4 * c + 4].unsqueeze(2).broadcast_to([128, 4, 2])
                    tbank.freed = dve.do(lambda e: e.tensor_tensor(o, tbank.ap[:, 0:8].rearrange("p (j c) -> p j c", c=2), bb, ALU.add), tt)

        def modcol(l, j, who):
            return MOD[:, 96 * l:96 * l + 96].rearrange("p (j k c) -> p j k c", j=6, k=8)[:, j, :, who]

        ar = Arena()
        KV = ar.get(2 * 1024)
        first_base = ar.at
        g = VEC[:, VO["mem_norm"]:VO["mem_norm"] + 8]
        th = [norm_T(MX[:, i, :], HT3, 128 * i, g, None, bring(0, 1, 2, 3), mready) for i in range(2)]
        for l in range(2):
            w, wv = load_w(A["w_memkv"][l], 8, 512)
            kT = KV[:, 1024 * l:1024 * l + 512].rearrange("p (f n) -> p f n", f=2)
            vM = KV[:, 1024 * l + 512:1024 * l + 1024].rearrange("p (i n) -> p i n", i=2)
            r = bring(4, 5, 6, 7)
            for f in range(2):
                lin_feat(hk, [(0, 256)], w, wv, 128 * f, 128, r,
                         lambda lo, hi, p, t, f=f: evac(f, kT[:, f, :], p, t), th)
            lin_tok(hk, range(2), w, wv, 256, 256, r, lambda i, p, t: evac(i, vM[:, i, :], p, t), th)
        barrier()

        def softmax_job(qk, nkeys, tiles, PB, PT, sring, tring, oring, vals, nv, scale, finish, after):
            while sring.full() or stats.full():
                yield
            S = sring.next()
            st = stats.next()
            for j, (c, n, l_, r_) in enumerate(qk):
                t = mm_group(S.ap[:, c:c + n], [(l_, r_)], after, S.freed)
            yield
            while PB.full():
                yield
            P = PB.next()
            t1 = dve.do(lambda e: e.tensor_reduce(st.ap[:, 0:1], S.ap[:, 0:nkeys], AX, ALU.max), t, st.freed)
            t1 = dve.do(lambda e: e.tensor_scalar(st.ap[:, 1:2], st.ap[:, 0:1], -scale, None, ALU.mult), t1)
            yield
            t2 = act.do(lambda e: e.activation(P.ap[:, 0:nkeys], S.ap[:, 0:nkeys], ACT.Exp, bias=st.ap[:, 1:2], scale=scale,
                                               accum_out=st.ap[:, 2:3]), t1, P.freed)
            S.freed = t2
            t3 = dve.do(lambda e: e.reciprocal(st.ap[:, 3:4], st.ap[:, 2:3]), t2)
            yield
            while PT.full():
                yield
            pt = PT.next()
            n = nkeys // 128
            te = []
            for a in range(0, n, 4):
                b = min(n, a + 4)
                bk = tring.next()
                tt = transposes(bk.ap, [P.ap[:, 128 * j:128 * j + 128] for j in range(a, b)], t2, bk.freed)
                te.append(evac(a // 4, pt.ap[:, 128 * a:128 * b], bk.ap[:, 0:128 * (b - a)], tt, pt.freed))
                bk.freed = te[-1]
            P.freed = tt
            yield
            while oring.full():
                yield
            ob = oring.next()
            to = mm_group(ob.ap[:, 0:nv], [(pt.ap[:, 128 * j:128 * j + 128], vals(j)) for j in range(n)], te, ob.freed)
            pt.freed = to
            yield
            ob.freed = finish(ob.ap[:, 0:nv], st.ap[:, 3:4], [to, t3])
            st.freed = ob.freed

        def mem_jobs(l, QM, BR, PB, PT, sring, tring, oring, after):
            kT = KV[:, 1024 * l:1024 * l + 512].rearrange("p (f n) -> p f n", f=2)
            vM = KV[:, 1024 * l + 512:1024 * l + 1024].rearrange("p (i n) -> p i n", i=2)
            for i in range(4):
                for h in range(4):
                    o = 64 * (h % 2)
                    yield softmax_job([(0, 256, QM[o:o + 64, h // 2, 128 * i:128 * i + 128], kT[o:o + 64, h // 2, :])],
                                      256, 2, PB, PT, sring, tring, oring,
                                      lambda j, h=h: vM[:, j, 64 * h:64 * h + 64], 64, 0.125,
                                      lambda p, r, a, i=i, h=h: dve.do(
                                          lambda e: e.tensor_scalar(BR[:, i, 768 + 64 * h:832 + 64 * h], p, r, None, ALU.mult), a),
                                      after)

        def decayed(K, V, nt, q, dirs, vtile, outs, bufs, psA, psT, psO, finish, after, vready=lambda: []):
            TT = 128 * nt
            rst = con("reset")[0:K, 0:TT]
            nd = len(dirs)
            cum, td, tq, tks, state, prev, first = {}, {}, {}, {}, {}, {}, {}

            def build(i):
                got = []
                for d, (k, lg, rev, order) in enumerate(dirs):
                    XB = bufs["X"][d].next()
                    x3 = XB.ap[0:K, :].rearrange("p (l n) -> p l n", l=7)
                    lo, hi = 128 * i, 128 * i + 128
                    v = lambda a, h: a.rearrange("p (n t h) -> p n t h", t=2, h=h)
                    t = []
                    for l in range(7):
                        h = 64 >> l
                        b4 = v(lg[:, lo:hi], h)
                        ref = b4[:, :, 1, 0:1] if rev else b4[:, :, 0, h - 1:h]
                        w2h = lambda a: a.rearrange("p (n h) -> p n h", h=2 * h)
                        t.append(dve.do(lambda e: e.tensor_tensor(w2h(x3[:, l, :]), w2h(lg[:, lo:hi]), ref.broadcast_to([K, 64 // h, 2 * h]),
                                                                  ALU.subtract), cum[d], XB.freed))
                    t = act.do(lambda e: e.activation(XB.ap[0:K, :], XB.ap[0:K, :], ACT.Abs), t)
                    t = act.do(lambda e: e.activation(XB.ap[0:K, :], XB.ap[0:K, :], ACT.Exp, scale=-1.0), t)
                    got.append((XB, x3, t))
                return got

            def weigh(i, built):
                got = []
                lo, hi = 128 * i, 128 * i + 128
                v = lambda a, h: a.rearrange("p (n t h) -> p n t h", t=2, h=h)
                for (XB, x3, t), (k, lg, rev, order) in zip(built, dirs):
                    mul = []
                    for l in range(7):
                        h = 64 >> l
                        x4, k4, q4 = v(x3[:, l, :], h), v(k[:, lo:hi], h), v(q[:, lo:hi], h)
                        kk, qq = (1, 0) if rev else (0, 1)
                        mul.append(pool.do(lambda e: e.tensor_tensor(x4[:, :, kk, :], x4[:, :, kk, :], k4[:, :, kk, :], ALU.mult), t))
                        mul.append(dve.do(lambda e: e.tensor_tensor(x4[:, :, qq, :], x4[:, :, qq, :], q4[:, :, qq, :], ALU.mult), t))
                    got.append((XB, x3, [mul[-2], mul[-1]]))
                return got

            def levels(i, built):
                out_ = []
                for (XB, x3, ready_), (k, lg, rev, order) in zip(built, dirs):
                    S = psA.next()
                    sv = S.ap.rearrange("p b n -> p (b n)").rearrange("p (l n) -> p l n", l=8)

                    def go(e):
                        for l in range(7):
                            e.matmul(sv[:, l, :], x3[:, l, :], x3[:, l, :], start=True, stop=True, skip_group_check=True)
                        return e.matmul(sv[:, 7, :], k[:, 128 * i:128 * i + 128], q[:, 128 * i:128 * i + 128],
                                        start=True, stop=True, skip_group_check=True)
                    tl = pe.do(go, ready_, S.freed)
                    XB.freed = tl
                    out_.append((S, sv, rev, tl))
                return out_

            def reduce_(lv, at_):
                for n_, (S, sv, rev, tl) in enumerate(lv):
                    if n_:
                        yield
                    M, Am = bufs["M"].next(), bufs["A"].next()
                    mk = bufs["mask"][:, 1024 * rev:1024 * rev + 1024].rearrange("p (l n) -> p l n", l=8)
                    m3 = M.ap.rearrange("p (l n) -> p l n", l=8)
                    tm = dve.do(lambda e: e.tensor_tensor(m3, sv, mk, ALU.mult), tl, M.freed, bufs["mslot"].ready)
                    S.freed = tm
                    ta = dve.do(lambda e: e.tensor_reduce(Am.ap, M.ap.rearrange("p (l n) -> p n l", l=8), AX, ALU.add), tm, Am.freed)
                    M.freed = ta
                    at_.append((Am, ta))

            def output(i, at_):
                bk = psO.next()
                pairs, need = [(Am.ap, vtile(i)) for Am, _ in at_], [ta for _, ta in at_]
                for d in range(nd):
                    if i in state[d]:
                        s3 = bufs["SP"][d].ap[0:K, 0:nt * V].rearrange("p (i n) -> p i n", n=V)
                        pairs.append((bufs["QH"][d].ap[0:K, 128 * i:128 * i + 128], s3[:, i, :]))
                        need += [state[d][i], tq[d]]
                to = mm_group(bk.ap[:, 0:V], pairs, need, bk.freed)
                for Am, _ in at_:
                    Am.freed = to
                last = finish(i, bk.ap[:, 0:V], to)

                def end():
                    bk.freed = last()
                return to, end

            def prepare():
                steps = []
                for d, (k, lg, rev, order) in enumerate(dirs):
                    KH, KT_, SP, QH, DEC = (bufs[n_][d] for n_ in ("KH", "KT", "SP", "QH", "DEC"))
                    o_, i_ = (lg[:, ::-1], lg[:, ::-1]) if rev else (lg, lg)
                    cum[d] = dve.do(lambda e: e.tensor_tensor_scan(o_, rst, i_, 0.0, ALU.mult, ALU.add), after())
                    b3 = lg.rearrange("p (i n) -> p i n", n=128)
                    end = b3[:, :, 0:1] if rev else b3[:, :, 127:128]
                    e3 = KH.ap[0:K, 0:TT].rearrange("p (i n) -> p i n", n=128)
                    te = dve.do(lambda e: e.tensor_tensor(e3, end.broadcast_to([K, nt, 128]), b3, ALU.subtract), cum[d], KH.freed)
                    te = act.do(lambda e: e.activation(KH.ap[0:K, 0:TT], KH.ap[0:K, 0:TT], ACT.Exp), te)
                    td[d] = act.do(lambda e: e.activation(DEC.ap[0:K, 0:nt], end.rearrange("p i o -> p (i o)"), ACT.Exp), cum[d], DEC.freed)
                    tq[d] = act.do(lambda e: e.activation(QH.ap[0:K, 0:TT], lg, ACT.Exp), cum[d], QH.freed)
                    yield
                    tk = dve.do(lambda e: e.tensor_tensor(KH.ap[0:K, 0:TT], k, KH.ap[0:K, 0:TT], ALU.mult), te)
                    tq[d] = pool.do(lambda e: e.tensor_tensor(QH.ap[0:K, 0:TT], q, QH.ap[0:K, 0:TT], ALU.mult), tq[d])
                    yield
                    tks[d] = []
                    for a in range(0, nt, 4):
                        b = min(nt, a + 4)
                        bk = psT.next()
                        tt = transposes(bk.ap, [KH.ap[0:K, 128 * i:128 * i + 128] for i in range(a, b)], tk, bk.freed)
                        o = KT_.ap[:, K * a:K * b].rearrange("p (i n) -> p i n", n=K)
                        i3 = bk.ap[:, 0:128 * (b - a)].rearrange("p (i n) -> p i n", n=128)[:, :, 0:K]
                        bk.freed = evac(1, o, i3, tt, KT_.freed)
                        tks[d].append(bk.freed)
                        yield
                    KH.freed = tt
                    state[d] = {}
                    steps += [(a, d) for a in range(nt - 1)]
                built_ = build(outs[0])
                steps.sort()
                per = 512 // V
                for g0 in range(0, len(steps), per):
                    some = steps[g0:g0 + per]
                    bk = psT.next()

                    def products(e):
                        for j, (a, d) in enumerate(some):
                            i = dirs[d][3][a]
                            m = e.matmul(bk.ap[0:K, V * j:V * j + V], bufs["KT"][d].ap[:, K * i:K * i + K], vtile(i),
                                         start=True, stop=True, skip_group_check=True)
                        return m
                    tm = pe.do(products, [tks[d] for _, d in some], vready(), bk.freed)
                    yield
                    for j, (a, d) in enumerate(some):
                        SP, DEC = bufs["SP"][d], bufs["DEC"][d]
                        s3 = SP.ap[0:K, 0:nt * V].rearrange("p (i n) -> p i n", n=V)
                        i, nx = dirs[d][3][a], dirs[d][3][a + 1]
                        r_ = bk.ap[0:K, V * j:V * j + V]
                        if a == 0:
                            ts = dve.do(lambda e: e.tensor_copy(s3[:, nx, :], r_), tm, SP.freed)
                        else:
                            ts = dve.do(lambda e: e.scalar_tensor_tensor(s3[:, nx, :], s3[:, i, :], DEC.ap[0:K, i:i + 1], r_,
                                                                         ALU.mult, ALU.add), tm, td[d], prev[d])
                        bk.freed = prev[d] = state[d][nx] = ts
                        bufs["KT"][d].freed, DEC.freed = tm, ts
                first["built"] = weigh(outs[0], built_)
                yield

            def run():
                built = first["built"]
                late = None
                for n, i in enumerate(outs):
                    lv = levels(i, built)
                    end = output(*late)[1] if late else None
                    if n + 1 < len(outs):
                        built = build(outs[n + 1])
                    yield
                    late = (i, [])
                    yield from reduce_(lv, late[1])
                    if end:
                        end()
                    if n + 1 < len(outs):
                        built = weigh(outs[n + 1], built)
                    yield
                to, end = output(*late)
                end()
                for d in range(nd):
                    bufs["SP"][d].freed = bufs["QH"][d].freed = to
            return prepare(), run()

        def gla_bufs(ar, K, V, nt, nd):
            TT = 128 * nt
            b = {}
            b["X"] = [Ring([Slot(ar.get(7 * 128)) for _ in range(2)]) for _ in range(nd)]
            b["KH"] = [Slot(ar.get(TT))] * nd
            b["M"] = Ring([Slot(ar.get(1024)) for _ in range(2)])
            b["A"] = Ring([Slot(ar.get(128)) for _ in range(2 * nd)])
            b["mask"] = ar.get(512 * nd).bitcast(BF16)
            b["mslot"] = mslot
            return [dict(b, **{n_: [Slot(ar.get(c)) for _ in range(nd)] for n_, c in
                               (("KT", K * nt), ("SP", nt * V), ("QH", TT), ("DEC", 8))}) for _ in range(2)]

        def project_out(BR, nb, tiles, gain, extra, wout, consume, ready_=None):
            r = bring(0, 1, 2, 3)
            W_ = [load_w(wout[:, 512 * c:512 * c + 512], 8, 512) for c in range(2)]

            def turned(i):
                pts = []
                for a in range(0, nb, 4):
                    b = min(nb, a + 4)
                    bk = r.next()
                    tt = transposes(bk.ap, [BR[:, i, 128 * k:128 * k + 128] for k in range(a, b)], bk.freed, ready_[i] if ready_ else [])
                    ev = []
                    for k in range(a, b):
                        o, s_, g_ = HT3[:, k, 128 * i:128 * i + 128], bk.ap[:, 128 * (k - a):128 * (k - a) + 128], gain(k)
                        ev.append(evac(a // 4 + i, o, s_, tt, scale=g_))
                    bk.freed = ev
                    pts += ev
                return pts
            src = lambda k: HT3[:, k, :] if k < nb else extra[:, k - nb, :]
            got = turned(tiles[0])
            for i in tiles:
                pts, got = got, turned(i + 1) if i + 1 in tiles else None
                for c, (w, wv) in enumerate(W_):
                    bk = banks[4 + (2 * i + c) % 4]
                    t = mm_group(bk.ap, [(src(k)[:, 128 * i:128 * i + 128], wv[:, k, :]) for k in range(8)], w.ready, pts, bk.freed)
                    bk.freed = consume(i, c, bk.ap, t)
                    w.freed = [t]

        def add_x(i, c, p, t):
            o = X3[:, i, 512 * c:512 * c + 512]
            return dve.do(lambda e: e.tensor_tensor(o, p, o, ALU.add), t, xready)

        def gate_job(wcols, ring):
            G3 = EX.rearrange("p (i n) -> p i n", i=4)
            for c in range(2):
                w, wv = load_w(wcols(c), 8, 512)
                for i in range(4):
                    bk = ring.next()
                    mm_group(bk.ap, [(hk(k)[:, 128 * i:128 * i + 128], wv[:, k, :]) for k in range(4)], w.ready, bk.freed, stop=False)
                    yield
                    t = mm_group(bk.ap, [(hk(k)[:, 128 * i:128 * i + 128], wv[:, k, :]) for k in range(4, 8)], start=False)
                    w.freed = t
                    bk.freed = act.do(lambda e: e.activation(G3[:, i, 512 * c:512 * c + 512], bk.ap, ACT.Copy), t)
                    yield

        def gate_apply(BR_):
            G3 = EX.rearrange("p (i n) -> p i n", i=4)
            return [dve.do(lambda e: e.tensor_tensor(BR_[:, i, :], BR_[:, i, :], G3[:, i, :], ALU.mult),
                           act.do(lambda e: e.activation(G3[:, i, :], G3[:, i, :], ACT.Silu))) for i in range(4)]

        ar = Arena()
        ar.at = first_base
        BR = ar.get(4096).rearrange("p (i n) -> p i n", i=4)
        QM = ar.get(1024).rearrange("p (f n) -> p f n", f=2)
        qkf = ar.get(8 * 512).rearrange("p (f n) -> p f n", f=8)
        VG = ar.get(4 * 768).rearrange("p (i n) -> p i n", i=4)
        LGA = ar.get(4 * 512).rearrange("p (f n) -> p f n", f=4)
        at0 = ar.at
        GL = ar.get(512)
        WGU = ar.get(384)
        TMP = ar.get(2 * 512).rearrange("p (f n) -> p f n", f=2)
        PBs = Ring([Slot(ar.get(256)) for _ in range(4)])
        PTs = Ring([Slot(ar.get(256)) for _ in range(4)])
        ar.at = at0
        gb = gla_bufs(ar, 96, 192, 4, 1)
        pts = barrier()
        mslot.ready = sp.dma(mslot, gb[0]["mask"].bitcast(mybir.dt.uint16), A["k_mask"][:, 0:1024], pts)
        wgs = Slot(None, sem("s_wgu"))
        wgready = sp.dma(wgs, WGU[0:16, :], A["w_gate_up"].rearrange("o a n -> (o a) n"), pts)
        g = VEC[:, VO["norm"]:VO["norm"] + 8]
        th = [norm_T(X3[:, i, :], HT3, 128 * i, g, None, bring(0, 1, 2, 3), xready) for i in range(4)]
        r = bring(0, 1, 2, 3, 4, 5, 6, 7)
        wa = A["w_in_a"][0]
        for j in range(2):
            w, wv = load_w(wa[:, 384 * j:384 * j + 384], 8, 384)
            for h in range(4):
                lin_feat(hk, [(0, 512)], w, wv, 96 * h, 96, r,
                         lambda lo, hi, p, t, j=j, h=h: evac(h, qkf[0:96, 4 * j + h, :], p, t, scale=96.0 ** -0.5 if j == 0 else None), th)
        w, wv = load_w(wa[:, 1536:1808], 8, 272)
        lin_feat(hk, [(0, 512)], w, wv, 0, 16, r, lambda lo, hi, p, t: evac(0, GL[0:16, :], p, t), th)
        tgl = (dve.sem, dve.n)
        for f in range(2):
            lin_feat(hk, [(0, 512)], w, wv, 16 + 128 * f, 128, r, lambda lo, hi, p, t, f=f: evac(f, QM[:, f, :], p, t), th)
        tlg = []
        for h in range(4):
            bk = r.next()
            p = bk.ap[0:96, :]
            t = mm_group(p, [(WGU[0:16, 96 * h:96 * h + 96], GL[0:16, :])], wgready, tgl, bk.freed)
            z, m_, n_ = LGA[0:96, h, :], TMP[0:96, 0, :], TMP[0:96, 1, :]
            t = dve.do(lambda e, z=z, p=p, h=h: e.tensor_scalar(z, p, NBG[:, h:h + 1], None, ALU.add), t)
            bk.freed = t
            ta = act.do(lambda e, m_=m_, z=z: e.activation(m_, z, ACT.Abs), t, [(dve.sem, dve.n)])
            ta = act.do(lambda e, m_=m_: e.activation(m_, m_, ACT.Exp, scale=-1.0), ta)
            ta = act.do(lambda e, m_=m_: e.activation(m_, m_, ACT.Ln, bias=con("eps")[0:96, 1:2]), ta)
            tb = dve.do(lambda e, z=z: e.tensor_scalar(z, z, 0.0, 1.0 / 16.0, ALU.min, ALU.mult), ta)
            tlg.append(dve.do(lambda e, z=z, m_=m_: e.scalar_tensor_tensor(z, m_, -1.0 / 16.0, z, ALU.mult, ALU.add), tb))
        for c0, n in ((768, 512), (1280, 256)):
            w, wv = load_w(wa[:, c0:c0 + n], 8, n)
            lin_tok(hk, range(4), w, wv, 0, n, r, lambda i, p, t, c0=c0, n=n: evac(i, VG[:, i, c0 - 768:c0 - 768 + n], p, t), th)
        barrier()

        def gla_jobs():
            for h in range(4):
                def fin(i, p, t, h=h):
                    st = stats.next()
                    s = hns.next()
                    t2 = act.do(lambda e: e.activation(s.ap[:, 0:192], p, ACT.Square, accum_out=st.ap[:, 0:1]), t, st.freed, s.freed)
                    s.freed = t2
                    t2 = rstd_of(st.ap, 1, 192, t2)

                    def end():
                        st.freed = dve.do(lambda e: e.tensor_scalar(BR[:, i, 192 * h:192 * h + 192], p, st.ap[:, 1:2], None, ALU.mult), t2)
                        return st.freed
                    return end
                yield decayed(96, 192, 4, qkf[0:96, h, :], [(qkf[0:96, 4 + h, :], LGA[0:96, h, :], 0, [0, 1, 2, 3])],
                              lambda i, h=h: VG[:, i, 192 * h:192 * h + 192], [0, 1, 2, 3], gb[h % 2],
                              gpsA, gpsT, gpsO, fin, lambda: tlg)
        gpsA, gpsT, gpsO = Ring([pair(0)]), bring(2, 3), bring(4, 5)
        mod_halves = EX
        mod_job = modulation([0], Ring([Slot(mod_halves[0:2, 512 * i:512 * i + 512]) for i in range(2)]), banks[6], banks[7])

        def gla_all():
            heads = list(gla_jobs())
            yield from heads[0][0]
            for h in range(4):
                nxt = heads[h + 1][0] if h < 3 else iter(())
                for _ in heads[h][1]:
                    next(nxt, None)
                    yield
                    next(nxt, None)
                yield from nxt
        together(gla_all(), mod_job, 1)
        barrier()
        mj = list(mem_jobs(0, QM, BR, PBs, PTs, bring(0, 1), bring(4, 5), bring(6, 7), []))
        gates = gate_job(lambda c: wa[:, 1808 + 512 * c:1808 + 512 * c + 512], Ring([banks[2], banks[3]]))
        interleave([gates] + mj, 5)

        barrier()
        gated_ = gate_apply(BR)
        project_out(BR, 8, range(4), lambda k: GNW[:, k % 3:k % 3 + 1] if k < 6 else None, None, A["w_out"][0], add_x, gated_)
        barrier()
        dump_now("x1", X)

        ar = Arena()
        ar.at = first_base
        BR = ar.get(4096).rearrange("p (i n) -> p i n", i=4)
        QM = ar.get(1024).rearrange("p (f n) -> p f n", f=2)
        DM = ar.get(1280)
        qkT = [Slot(ar.get(6 * 512).rearrange("p (f n) -> p f n", f=6)) for _ in range(2)]
        VV = [Slot(ar.get(4 * 384).rearrange("p (i n) -> p i n", i=4)) for _ in range(2)]
        SG = Ring([Slot(ar.get(384)) for _ in range(2)])
        RT = Ring([Slot(ar.get(192)) for _ in range(2)])
        SB = Ring([Slot(ar.get(1280)) for _ in range(2)])
        PTb = Ring([Slot(ar.get(1280)) for _ in range(2)])
        pts = barrier()
        dms = Slot(None, sem("s_dm"))
        dmr = sp.dma(dms, DM, A["k_const"][:, CW["dil"][0]:CW["dil"][1]], pts)
        g = VEC[:, VO["norm"] + 8:VO["norm"] + 16]
        th = [norm_T(X3[:, i, :], HT3, 128 * i, g, None, bring(0, 1, 2, 3), []) for i in range(4)]
        wb = A["w_in_b"][0]
        w, wv = load_w(wb[:, 6912:7168], 8, 256)
        for f in range(2):
            lin_feat(hk, [(0, 512)], w, wv, 128 * f, 128, bring(6, 7), lambda lo, hi, p, t, f=f: evac(f, QM[:, f, :], p, t), th)
        cs = con("drope").rearrange("p (c i n) -> p c i n", c=2, i=4)
        lring, tring, oring = bring(3, 4), bring(5, 6), bring(7)
        sall = Slot(PS[:, 0:3, :])

        def head_project(h):
            QK, V_ = qkT[h % 2], VV[h % 2]
            pts = []
            late = None
            for s_ in range(3):
                w, wv = load_w([(128 * gg, 128, wb[:, 2304 * gg + 768 * s_ + 128 * h:2304 * gg + 768 * s_ + 128 * h + 128])
                                for gg in range(3)], 8, 384)
                for i in range(4):
                    bk = lring.next()
                    mm_group(bk.ap[:, 0:384], [(hk(k)[:, 128 * i:128 * i + 128], wv[:, k, :]) for k in range(4)], w.ready, th, bk.freed, stop=False)
                    yield
                    t = mm_group(bk.ap[:, 0:384], [(hk(k)[:, 128 * i:128 * i + 128], wv[:, k, :]) for k in range(4, 8)], start=False)
                    w.freed = [t]
                    if late:
                        late()
                        late = None
                    if s_ == 2:
                        t = evac(1, V_.ap[:, i, :], bk.ap[:, 0:384], t, V_.freed)
                        bk.freed = t
                        pts.append(t)
                        yield
                        continue
                    S_, R_ = SG.next(), RT.next()
                    t = evac(1, S_.ap, bk.ap[:, 0:384], t, S_.freed)
                    bk.freed = t
                    v = S_.ap.rearrange("p (g n) -> p g n", g=3)
                    x1, x2 = v[:, :, 0:16], v[:, :, 16:32]
                    cc = cs[:, 0, i, :].unsqueeze(1).broadcast_to([128, 3, 16])
                    ss = cs[:, 1, i, :].unsqueeze(1).broadcast_to([128, 3, 16])
                    r4 = R_.ap.rearrange("p (a g n) -> p a g n", a=4, g=3)
                    ts = [dve.do(lambda e: e.tensor_tensor(o, x, y, ALU.mult), t, R_.freed)
                          for o, x, y in ((r4[:, 0], x1, cc), (r4[:, 1], x2, ss), (r4[:, 2], x1, ss), (r4[:, 3], x2, cc))]
                    tr = [dve.do(lambda e: e.tensor_tensor(x1, r4[:, 0], r4[:, 1], ALU.subtract), ts),
                          dve.do(lambda e: e.tensor_tensor(x2, r4[:, 2], r4[:, 3], ALU.add), ts)]
                    R_.freed = tr

                    def late(S_=S_, tr=tr, s_=s_, i=i):
                        bk = tring.next()
                        tt = transposes(bk.ap, [S_.ap[:, 128 * gg:128 * gg + 128] for gg in range(3)], tr, bk.freed)
                        S_.freed = tt
                        o = QK.ap[:, 3 * s_:3 * s_ + 3, 128 * i:128 * i + 128]
                        t = evac(i, o, bk.ap[:, 0:384].rearrange("p (g n) -> p g n", g=3), tt, QK.freed)
                        bk.freed = t
                        pts.append(t)
                    yield
            QK.ready = pts

        def head_attend(h):
            QK, V_ = qkT[h % 2], VV[h % 2]
            for i in range(4):
                n0 = 1 if i == 0 else 2
                n1 = i + 1
                while SB.full() or PTb.full():
                    yield
                st, P, pt = stats.next(), SB.next(), PTb.next()
                def scores(e, i=i, n0=n0, n1=n1):
                    e.matmul(sall.ap[:, 0, 0:128 * n0], QK.ap[:, 0, 128 * i:128 * i + 128], QK.ap[:, 3, 128 * (i + 1 - n0):128 * (i + 1)], start=True, stop=True)
                    e.matmul(sall.ap[:, 1, 0:128 * n1], QK.ap[:, 1, 128 * i:128 * i + 128], QK.ap[:, 4, 0:128 * n1], start=True, stop=True)
                    return e.matmul(sall.ap[:, 2, 0:128 * n1], QK.ap[:, 2, 128 * i:128 * i + 128], QK.ap[:, 5, 0:128 * n1], start=True, stop=True)
                t = pe.do(scores, QK.ready, sall.freed)
                yield
                ns = [n0, n1, n1]
                offs = [0, n0, n0 + n1]
                mends = [256, 768, 1280]
                ta = []
                for gg in range(3):
                    c0, wd = 128 * offs[gg], 128 * ns[gg]
                    ta.append(dve.do(lambda e, gg=gg, c0=c0, wd=wd, P=P: e.scalar_tensor_tensor(
                        P.ap[:, c0:c0 + wd], sall.ap[:, gg, 0:wd], 128.0 ** -0.5, DM[:, mends[gg] - wd:mends[gg]], ALU.mult, ALU.add), t, dmr, P.freed))
                sall.freed = ta
                nk = n0 + 2 * n1
                t1 = dve.do(lambda e, P=P, st=st, nk=nk: e.tensor_reduce(st.ap[:, 0:1], P.ap[:, 0:128 * nk], AX, ALU.max), ta, st.freed)
                t1 = dve.do(lambda e, st=st: e.tensor_scalar(st.ap[:, 1:2], st.ap[:, 0:1], -1.0, None, ALU.mult), t1)
                t2 = act.do(lambda e, P=P, st=st, nk=nk: e.activation(P.ap[:, 0:128 * nk], P.ap[:, 0:128 * nk], ACT.Exp, bias=st.ap[:, 1:2],
                                                              accum_out=st.ap[:, 2:3]), t1)
                yield
                yield
                t3 = dve.do(lambda e, st=st: e.reciprocal(st.ap[:, 3:4], st.ap[:, 2:3]), t2)
                te = []
                for a in range(0, nk, 4):
                    b = min(nk, a + 4)
                    bk = tring.next()
                    tt = transposes(bk.ap, [P.ap[:, 128 * j:128 * j + 128] for j in range(a, b)], t2, bk.freed)
                    te.append(evac(a // 4, pt.ap[:, 128 * a:128 * b], bk.ap[:, 0:128 * (b - a)], tt, pt.freed))
                    bk.freed = te[-1]
                P.freed = tt
                yield
                vt = []
                for gg in range(3):
                    first = i + 1 - ns[gg]
                    vt += [V_.ap[:, first + j, 128 * gg:128 * gg + 128] for j in range(ns[gg])]
                ob = oring.next()
                to = mm_group(ob.ap[:, 0:128], [(pt.ap[:, 128 * j:128 * j + 128], vt[j]) for j in range(nk)], te, QK.ready, ob.freed)
                pt.freed = to
                ob.freed = dve.do(lambda e, ob=ob, st=st, i=i: e.tensor_scalar(BR[:, i, 128 * h:128 * h + 128], ob.ap[:, 0:128], st.ap[:, 3:4], None, ALU.mult), to, t3)
                st.freed = ob.freed
            QK.freed = to
            V_.freed = to

        gates = gate_job(lambda c: wb[:, 7168 + 512 * c:7168 + 512 * c + 512], lring)
        interleave([head_project(0)], 1)
        for h in range(6):
            if h < 5:
                together(head_attend(h), head_project(h + 1), 1)
            else:
                for _ in head_attend(h):
                    next(gates, None)
        barrier()
        PBs = Ring([Slot(SB.slots[i].ap[:, 256 * j:256 * j + 256]) for i in range(2) for j in range(2)])
        PTs = Ring([Slot(PTb.slots[i].ap[:, 256 * j:256 * j + 256]) for i in range(2) for j in range(2)])
        interleave([gates] + list(mem_jobs(1, QM, BR, PBs, PTs, bring(0, 1, 2), bring(5, 6), bring(7), [])), 5)
        barrier()
        gated_ = gate_apply(BR)
        project_out(BR, 8, range(4), lambda k: None, None, A["w_out"][1], add_x, gated_)
        barrier()
        dump_now("x2", X)
        ar = Arena()
        FW = ar.get(1024)
        pts = barrier()
        fws = Slot(None, sem("s_fw"))
        fwr = sp.dma(fws, FW, A["final_norm_w"].rearrange("(o n) -> o n", o=1).broadcast_to([128, 1024]), pts)
        for i in range(4):
            s, st = hns.next(), stats.next()
            t = act.do(lambda e, i=i, s=s, st=st: e.activation(s.ap, X3[:, i, :], ACT.Square, accum_out=st.ap[:, 0:1]), s.freed, st.freed)
            s.freed = t
            t = rstd_of(st.ap, 1, D, t)
            t = dve.do(lambda e, i=i, st=st: e.scalar_tensor_tensor(X3[:, i, :], X3[:, i, :], st.ap[:, 1:2], FW, ALU.mult, ALU.mult), t, fwr)
            st.freed = t
        barrier()
        dump_now("x3", X)

        def residual_rows(ar, l, j, gcol, after=()):
            GV = ar.get(2048).rearrange("p (c n) -> p c n", c=2)
            cl = ar.get(16)
            dg = Ring([Slot(ar.get(128)) for _ in range(2)])
            rr = bring(0, 1)
            tdone = []
            for who in range(2):
                tcol = dve.do(lambda e, who=who: e.tensor_tensor(cl[:, 8 * who:8 * who + 8], modcol(l, j, who), gcol, ALU.mult), after)
                for half in range(2):
                    bk = rr.next()
                    for k in range(4):
                        s = dg.next()
                        kk = 4 * half + k
                        t = dve.do(lambda e, s=s, kk=kk, who=who: e.tensor_scalar(s.ap, ident, cl[:, 8 * who + kk:8 * who + kk + 1], None, ALU.mult), tcol, s.freed)
                        t = mm_group(bk.ap[:, 128 * k:128 * k + 128], [(ones, s.ap)], t, bk.freed if k == 0 else [])
                        s.freed = t
                    bk.freed = evac(half, GV[:, who, 512 * half:512 * half + 512], bk.ap, t)
                    tdone.append(bk.freed)
            return GV, tdone

        def scale_cols(ar, l, j, gcol, who):
            a = ar.get(8)
            t = dve.do(lambda e: e.scalar_tensor_tensor(a, modcol(l, j, who), 1.0, gcol, ALU.add, ALU.mult))
            return a, t

        def xt(i):
            return X3[:, i, :] if i < 4 else XC3[:, i - 4, :]

        def add_normed(Y, i, GV, pts):
            s, st = hns.next(), stats.next()
            y = Y[:, i, :]
            t = act.do(lambda e: e.activation(s.ap, y, ACT.Square, accum_out=st.ap[:, 0:1]), pts, s.freed, st.freed)
            s.freed = t
            t = rstd_of(st.ap, 1, D, t)
            gv = GV[:, 0 if i < 4 else 1, :]
            t = dve.do(lambda e: e.scalar_tensor_tensor(y, y, st.ap[:, 1:2], gv, ALU.mult, ALU.mult), t, pts)
            st.freed = t
            return dve.do(lambda e: e.tensor_tensor(xt(i), xt(i), y, ALU.add), t)

        for l in range(2):
            both = l == 0
            nt = 6 if both else 4
            w2 = A["w_in_2"][l]
            gcol = lambda j: VEC[:, VO["norm_g"] + 32 * l + 8 * j:VO["norm_g"] + 32 * l + 8 * j + 8]
            ar = Arena()
            BR = ar.get(6 * 768).rearrange("p (i n) -> p i n", i=6)
            FTT = ar.get(2 * 768).rearrange("p (f n) -> p f n", f=2)
            base = ar.at
            pts = barrier()
            cols = [scale_cols(ar, l, 1, gcol(0), who) for who in range(2)]
            th = [norm_T(xt(i), HT3, 128 * i, cols[i // 4][0], modcol(l, 0, i // 4), bring(0, 1, 2, 3), [cols[i // 4][1], xcready])
                  for i in range(6)]
            U = ar.get(6 * 256).rearrange("p (i n) -> p i n", i=6)
            QKT = ar.get(4 * 768).rearrange("p (f n) -> p f n", f=4)
            DV = ar.get(6 * 256).rearrange("p (i n) -> p i n", i=6)
            SG = Ring([Slot(ar.get(512)) for _ in range(2)])
            RT = Ring([Slot(ar.get(1024)) for _ in range(2)])
            PA = Ring([Slot(ar.get(1536)) for _ in range(3)])
            PTb = Ring([Slot(ar.get(768)) for _ in range(3)])
            PQ = ar.get(2 * 2 * 512).rearrange("p (c f n) -> p c f n", c=2, f=2)
            lring = bring(0, 1, 2, 3)
            tring = bring(4, 5)
            w, wv = load_w(w2[:, 2560:3072], 8, 512)
            arp = con("arope").rearrange("p (c i a n) -> p c i a n", c=2, i=4, a=2)
            qpts = []

            def qk_cons(i, p, t):
                S_ = SG.next()
                t = evac(1, S_.ap, p, t, S_.freed)
                ret = t
                if i < 4:
                    R_ = RT.next()
                    v = S_.ap.rearrange("p (g a c n) -> p g a c n", g=16, a=2, c=2)
                    x1, x2 = v[:, :, :, 0, :], v[:, :, :, 1, :]
                    cc = arp[:, 0, i].unsqueeze(1).broadcast_to([128, 16, 2, 8])
                    ss = arp[:, 1, i].unsqueeze(1).broadcast_to([128, 16, 2, 8])
                    r4 = R_.ap.rearrange("p (q g a n) -> p q g a n", q=4, g=16, a=2)
                    ts = [dve.do(lambda e, o=r4[:, a], x=x, y=y: e.tensor_tensor(o, x, y, ALU.mult), t, R_.freed)
                          for a, (x, y) in enumerate(((x1, cc), (x2, ss), (x1, ss), (x2, cc)))]
                    t = [dve.do(lambda e: e.tensor_tensor(x1, r4[:, 0], r4[:, 1], ALU.subtract), ts),
                         dve.do(lambda e: e.tensor_tensor(x2, r4[:, 2], r4[:, 3], ALU.add), ts)]
                    R_.freed = t
                bk = tring.next()
                tt = transposes(bk.ap, [S_.ap[:, 128 * f:128 * f + 128] for f in range(4)], t, bk.freed)
                S_.freed = tt
                bk.freed = evac(i, QKT[:, :, 128 * i:128 * i + 128], bk.ap.rearrange("p (f n) -> p f n", f=4), tt)
                qpts.append(bk.freed)
                return ret
            lin_tok(hk, range(6), w, wv, 0, 512, lring, qk_cons, th)
            w, wv = load_w(w2[:, 3072:3584], 8, 512)
            lin_tok(hk, range(6), w, wv, 0, 256, lring, lambda i, p, t: evac(i, DV[:, i, :], p, t), th)
            lin_tok(hk, range(nt), w, wv, 256, 256, lring, lambda i, p, t: evac(i, U[:, i, :], p, t), th)
            barrier()
            cs64 = con("cs64")
            for who, (n, name, tiles0, off) in enumerate(((T, "k_dft", 0, 0), (TC, "k_dftc", 4, 512))):
                if who and not both:
                    continue
                kt = n // 128
                tabs = []
                for c in range(2):
                    s = wring.next()
                    v = s.ap[:, 0:kt * n].rearrange("p (k n) -> p k n", k=kt)
                    s.ready = sp.dma(s, s.ap[:, 0:kt * n], A[name][:, c * kt * n:(c + 1) * kt * n])
                    tabs.append((s, v))
                ev = []
                for c in range(2):
                    s, v = tabs[c]
                    for f in range(2):
                        bk = lring.next()
                        t = mm_group(bk.ap[:, 0:n], [(U[:, tiles0 + k, 128 * f:128 * f + 128], v[:, k, :]) for k in range(kt)], s.ready, bk.freed)
                        s.freed = [t]
                        bk.freed = evac(f, PQ[:, c, f, 0:n], bk.ap[:, 0:n], t, [(pe.sem, pe.n)] if who else [])
                        ev.append(bk.freed)
                for f in range(2):
                    bk = tring.next()
                    t = mm_group(bk.ap[:, 0:n], [(cs64[:, 128 * c:128 * c + 128], PQ[:, c, f, 0:n]) for c in range(2)], ev, bk.freed)
                    bk.freed = evac(f, FTT[:, f, off:off + n], bk.ap[:, 0:n], t)
            barrier()
            sring = Ring([pair(0), pair(2)])
            tring = oring = bring(4, 5)

            def da_job(i, h):
                lat = i < 4
                keys = [(0, 512), (512, 768)] if lat else [(512, 768)]
                nk = 6 if lat else 2
                while PA.full() or PTb.full():
                    yield
                P, pt, st = PA.next(), PTb.next(), stats.next()
                te = []
                for m_ in range(2):
                    while sring.full():
                        yield
                    S = sring.next()
                    f, o = h // 2, (h % 2) * 64 + 32 * m_
                    sv = S.ap.rearrange("p b n -> p (b n)")

                    def sc(e, sv=sv, f=f, o=o):
                        c = 0
                        for lo, hi in keys:
                            r_ = e.matmul(sv[:, c:c + hi - lo], QKT[o:o + 32, f, 128 * i:128 * i + 128], QKT[o:o + 32, 2 + f, lo:hi], start=True, stop=True)
                            c += hi - lo
                        return r_
                    t = pe.do(sc, S.freed)
                    yield
                    t1 = dve.do(lambda e, sv=sv, m_=m_: e.tensor_reduce(st.ap[:, m_:m_ + 1], sv[:, 0:128 * nk], AX, ALU.max), t, st.freed)
                    t1 = dve.do(lambda e, m_=m_: e.tensor_scalar(st.ap[:, m_:m_ + 1], st.ap[:, m_:m_ + 1], -(32.0 ** -0.5), None, ALU.mult), t1)
                    t2 = act.do(lambda e, sv=sv, m_=m_: e.activation(P.ap[:, 768 * m_:768 * m_ + 128 * nk], sv[:, 0:128 * nk], ACT.Exp, bias=st.ap[:, m_:m_ + 1],
                                                                     scale=32.0 ** -0.5, accum_out=st.ap[:, 2 + m_:3 + m_]), t1, P.freed)
                    S.freed = t2
                    te.append(t2)
                yield
                t = dve.do(lambda e: e.reciprocal(st.ap[:, 4:6], st.ap[:, 2:4]), te)
                t = dve.do(lambda e: e.tensor_scalar(st.ap[:, 5:6], st.ap[:, 5:6], LB[:, l:l + 1], None, ALU.mult), t)
                p0, p1 = P.ap[:, 0:128 * nk], P.ap[:, 768:768 + 128 * nk]
                t = dve.do(lambda e: e.tensor_scalar(p1, p1, st.ap[:, 5:6], None, ALU.mult), t)
                t = dve.do(lambda e: e.scalar_tensor_tensor(p0, p0, st.ap[:, 4:5], p1, ALU.mult, ALU.subtract), t)
                st.freed = t
                yield
                tv = []
                for a in range(0, nk, 4):
                    b = min(nk, a + 4)
                    bk = tring.next()
                    tt = transposes(bk.ap, [P.ap[:, 128 * j:128 * j + 128] for j in range(a, b)], t, bk.freed)
                    tv.append(evac(1, pt.ap[:, 128 * a:128 * b], bk.ap[:, 0:128 * (b - a)], tt, pt.freed))
                    bk.freed = tv[-1]
                yield
                ob = oring.next()
                k0 = 0 if lat else 4
                to = mm_group(ob.ap[:, 0:64], [(pt.ap[:, 128 * j:128 * j + 128], DV[:, k0 + j, 64 * h:64 * h + 64]) for j in range(nk)], tv, ob.freed)
                pt.freed = to
                s2 = stats.next()
                o_, sq = P.ap[:, 0:64], P.ap[:, 64:128]
                ob.freed = dve.do(lambda e: e.tensor_copy(o_, ob.ap[:, 0:64]), to)
                yield
                t = act.do(lambda e: e.activation(sq, o_, ACT.Square, accum_out=s2.ap[:, 0:1]), ob.freed, s2.freed)
                t = rstd_of(s2.ap, 1, 64, t)
                yield
                t = dve.do(lambda e: e.tensor_scalar(BR[:, i, 512 + 64 * h:576 + 64 * h], o_, s2.ap[:, 1:2], None, ALU.mult), t)
                s2.freed = P.freed = t

            ar.at = base
            sets = []
            for b_ in range(2):
                get = (lambda n, b_=b_: X[:, 768 * n:768 * n + 768] if n < 5 else XC[:, 768 * (n - 5):768 * (n - 4)]) if b_ \
                    else (lambda n: EX[:, 768 * n:768 * n + 768] if n < 5 else ar.get(768))
                t6 = [get(n) for n in range(7)]
                sets.append((t6[0], t6[1:3], t6[3:5], t6[5].rearrange("p (i n) -> p i n", i=6), t6[6].rearrange("p (i n) -> p i n", i=6)))
            set_free = [[], []]
            hb = gla_bufs(ar, 128, 128, 6, 2)
            spans = [(0, 512), (512, 768)]
            ready, vals = {}, {}

            def project(h):
                QF, KF, LG, VH, GH = sets[h % 2]
                fr = set_free[h % 2]
                rr = bring(6, 7)
                w, wv = load_w([(0, 128, w2[:, 128 * h:128 * h + 128]), (128, 128, w2[:, 1536 + 128 * h:1536 + 128 * h + 128]),
                                (256, 128, w2[:, 2048 + 128 * h:2048 + 128 * h + 128])], 8, 384)
                hp = [] if both else [dve.do(lambda e: e.memset(QF[:, 512:768], 0.0), fr)]
                qn = 768 if both else 512

                def feat(c0, sp1, o, ev):
                    lo, hi = sp1
                    bk = rr.next()
                    p_ = bk.ap[:, 0:hi - lo]
                    pairs = [(wv[:, k, c0:c0 + 128], hk(k)[:, lo:hi]) for k in range(8)]
                    mm_group(p_, pairs[:4], w.ready, bk.freed, stop=False)
                    if hi - lo == 512:
                        yield
                    t = mm_group(p_, pairs[4:], start=False)
                    ev.append(act.do(lambda e: e.activation(o[:, lo:hi], p_, ACT.Copy), t, fr))
                    bk.freed = ev[-1]
                    w.freed = t
                    yield
                evs, lns = [[], []], []
                for d in range(2):
                    for sp1 in spans:
                        yield from feat(128 + 128 * d, sp1, LG[d], evs[d])
                for sp1 in spans if both else spans[:1]:
                    yield from feat(0, sp1, QF, hp)
                for d in range(2):
                    lb, om = LOW[:, d, l, h:h + 1], ONEM[:, d, l, h:h + 1]
                    tk = act.do(lambda e: e.activation(KF[d], LG[d], ACT.Sigmoid, scale=-1.0), evs[d])
                    ta = act.do(lambda e: e.activation(LG[d], LG[d], ACT.Sigmoid))
                    hp.append(dve.do(lambda e: e.tensor_scalar(KF[d], KF[d], om, None, ALU.mult), tk))
                    tb = dve.do(lambda e: e.tensor_scalar(LG[d], LG[d], om, lb, ALU.mult, ALU.add), ta)
                    lns.append(dve.do(lambda e: e.tensor_scalar(LG[d], LG[d], 1e-19, None, ALU.max), tb))
                hp.append(act.do(lambda e: e.activation(QF[:, 0:qn], QF[:, 0:qn], ACT.Silu), hp))
                w, wv = load_w([(0, 128, w2[:, 512 + 128 * h:512 + 128 * h + 128]), (128, 128, w2[:, 1024 + 128 * h:1024 + 128 * h + 128])], 8, 256)
                yield
                for d in range(2):
                    hp.append(act.do(lambda e: e.activation(LG[d], LG[d], ACT.Ln), lns[d]))
                ready[h] = hp
                vp = []

                def vcons(i_, p, t):
                    vp.append(act.do(lambda e: e.activation(VH[:, i_, :], p[:, 0:128], ACT.Copy), t, fr))
                    vp.append(act.do(lambda e: e.activation(GH[:, i_, :], p[:, 128:256], ACT.Copy), t, fr))
                    return vp[-1]
                prep = heads[h][0]
                for i in range(6):
                    lin_tok(hk, [i], w, wv, 0, 256, rr, vcons, [])
                    if h:
                        next(prep)
                        if i % 3 == 2:
                            next(prep)
                    yield
                gh = GH.rearrange("p i n -> p (i n)")
                vp.append(act.do(lambda e: e.activation(gh, gh, ACT.Silu), vp))
                vals[h] = vp
                if h == 0:
                    yield
                yield from prep

            def recur(h):
                QF, KF, LG, VH, GH = sets[h % 2]

                def fin(i, p, t):
                    st = stats.next()
                    s = hns.next()
                    t2 = act.do(lambda e: e.activation(s.ap[:, 0:128], p, ACT.Square, accum_out=st.ap[:, 0:1]), t, st.freed, s.freed)
                    s.freed = t2
                    t2 = rstd_of(st.ap, 1, 128, t2)

                    def end():
                        st.freed = dve.do(lambda e: e.scalar_tensor_tensor(BR[:, i, 128 * h:128 * h + 128], p, st.ap[:, 1:2], GH[:, i, :],
                                                                           ALU.mult, ALU.mult), t2)
                        return st.freed
                    return end
                return decayed(128, 128, 6, QF, [(KF[0], LG[0], 0, [4, 5, 0, 1, 2, 3]), (KF[1], LG[1], 1, [5, 4, 3, 2, 1, 0])],
                                   lambda i: VH[:, i, :], list(range(nt)), hb[h % 2], hpsA,
                               bring(4), bring(5), fin, lambda: ready[h], lambda: vals[h])

            RATE = (1.05, 1.35)

            def main(h):
                yield from heads[h][1]
                set_free[h % 2] = [(q_.sem, q_.n) for q_ in compute]

            def later_mod():
                hv = Ring([Slot(EX[0:2, 512 * i:512 * i + 512]) for i in range(2)])
                for s_ in hv.slots:
                    s_.freed = set_free[0]
                return modulation([1], hv, banks[6], banks[7])
            hpsA = Ring([pair(0), pair(2)])
            heads = [recur(h) for h in range(4)]
            first = project(0)

            def ahead():
                while 0 not in vals:
                    next(first)
                    yield
            da = [da_job(i, h) for i in range(nt) for h in range(4)]
            interleave(da[:3] + [ahead()] + da[3:], 4)
            pts = barrier()
            mslot.ready = sp.dma(mslot, hb[0]["mask"].bitcast(mybir.dt.uint16), A["k_mask"], pts)
            spill.dma_out(sp, X, XSP[:, 0:4096], pts)
            xsp = spill.dma_out(sp, XC, XSP[:, 4096:6144], pts)
            set_free[1] = [xsp]
            interleave([first], 1)
            for h in range(4):
                together(main(h), project(h + 1) if h < 3 else later_mod() if both else iter(()), RATE[l], 1)
            pts = barrier()
            spill.dma_in(sp, X, XSP[:, 0:4096], pts, xsp)
            xready = spill.dma_in(sp, XC, XSP[:, 4096:6144])
            ar.at = base
            Y = ar.get(6 * 1024).rearrange("p (i n) -> p i n", i=6)
            GV, gpt = residual_rows(ar, l, 2, gcol(1))
            ON = VEC[:, VO["hg_onorm"] + l:VO["hg_onorm"] + l + 1]
            ypts = {}

            def take(i, c, p, t):
                ypts[i, c] = evac(i + c, Y[:, i, 512 * c:512 * c + 512], p, t)
                if c == 1 and i:
                    add_normed(Y, i - 1, GV, [gpt, xready, ypts[i - 1, 0], ypts[i - 1, 1]])
                return ypts[i, c]
            project_out(BR, 6, range(nt), lambda k: ON if k < 4 else SUBC[:, l:l + 1], FTT, A["w_out_2"][l], take)
            add_normed(Y, nt - 1, GV, [gpt, xready, ypts[nt - 1, 0], ypts[nt - 1, 1]])
            barrier()
            dump_now(f"y{l}", X)
            TT = 128 * nt
            HR, WC, AC = claim(("HR", 2 * 8 * TT, F32R), ("WC", 3 * 2048, F32R), ("AC", 2 * 4 * TT, F32R))
            xar = Arena(EX, 4096)
            HH = [HR[:, 8 * TT * p_:8 * TT * (p_ + 1)].rearrange("p (k n) -> p k n", k=8) for p_ in range(2)]
            cols = [scale_cols(xar, l, 4, gcol(2), who) for who in range(2)]
            tmps = Ring([Slot(xar.get(512)) for _ in range(2)])
            th = []
            norms = [norm_split(xt(i), HH, 128 * i, cols[i // 4][0], modcol(l, 3, i // 4), bring(0, 1, 2, 3), tmps, cols[i // 4][1], th)
                     for i in range(nt)]
            next(norms[0])
            for i in range(nt):
                if i + 1 < nt:
                    next(norms[i + 1])
                next(norms[i], None)
            xar.at = 16
            GV, gpt = residual_rows(xar, l, 5, gcol(3), barrier())
            pr = Ring([Slot(xar.get(512)) for _ in range(3)])
            wi, wo = A["w_ffn_in_2"][l], A["w_ffn_out_2"][l]
            wcr = Ring([Slot(WC[:, 2048 * i:2048 * i + 2048]) for i in range(3)])
            acs = [Slot(AC[:, 4 * TT * i:4 * TT * (i + 1)].rearrange("p (s j n) -> p s j n", s=2, j=2)) for i in range(2)]
            spans = [(0, 512), (512, 768)] if both else [(0, 512)]
            Y = HT[:, 0:nt * 1024].rearrange("p (i n) -> p i n", i=nt)
            sched = []
            for b in range(12):
                if b < 11:
                    sched += [("up", b, kp) for kp in range(4)] + [("act", b, 0)]
                if b >= 1:
                    sched += [("down", b - 1, c) for c in range(2)]
            work = [x for x in sched if x[0] != "act"]
            staged, conv = {}, {}

            wup, wdn = (Ring([s]) for s in wring.slots)

            def stage(kind, b):
                if kind == "up":
                    staged["up"] = load_w([(0, 256, wi[:, 256 * b:256 * b + 256]), (256, 256, wi[:, FF + 256 * b:FF + 256 * b + 256])], 8, 512, wup)
                else:
                    staged["down"] = load_w(wo[256 * b:256 * b + 256, :], 2, 1024, wdn)

            def convert(kind, b, c):
                w, wv = staged[kind]
                src = wv[:, 2 * c:2 * c + 2, :] if kind == "up" else wv[:, :, 512 * c:512 * c + 512]
                s = wcr.next()
                o = s.ap.rearrange("p (s k n) -> p s k n", s=2, k=2)
                t1, t2 = split(o[:, 0], o[:, 1], src, w.ready, s.freed)
                if c == (3 if kind == "up" else 1):
                    w.freed = t2
                    if b < 10:
                        stage(kind, b + 1)
                conv[kind, b, c] = (s, o, [t1, t2])

            stage("up", 0)
            stage("down", 0)

            ubank = {}
            for q_ in range(4):
                ubank[q_, 0] = (q_, PS[:, q_, 0:512])
                ubank[q_, 1] = (4 + q_ // 2, PS[:, 4 + q_ // 2, 256 * (q_ % 2):256 * (q_ % 2) + 256])
            drn = Ring([banks[6], banks[7]] if both else [banks[i] for i in (4, 5, 6, 7)])
            updone = {}
            yprev = {}

            def gated(b):
                a = acs[b % 2]
                pts, fr, late = [], {}, None
                for j2 in range(2):
                    for sp_, (lo, hi) in enumerate(spans):
                        (bg, pg), (bu, pu) = ubank[j2, sp_], ubank[2 + j2, sp_]
                        h = pr.next()
                        v = h.ap[:, 0:hi - lo]
                        ts = act.do(lambda e: e.activation(v, pg, ACT.Silu), updone[b], h.freed)
                        fr.setdefault(bg, []).append(ts)
                        if late:
                            late()
                        tm = dve.do(lambda e: e.tensor_tensor(v, v, pu, ALU.mult), ts)
                        fr.setdefault(bu, []).append(tm)

                        def late(h=h, v=v, tm=tm, j2=j2, lo=lo, hi=hi):
                            t1, t2 = split(a.ap[:, 0, j2, lo:hi], a.ap[:, 1, j2, lo:hi], v, tm, a.freed)
                            h.freed = t2
                            pts.extend([t1, t2])
                        yield
                late()
                for bi, t in fr.items():
                    banks[bi].freed = t
                a.ready = pts

            gating = iter(())
            for n_, x in enumerate(work[:2]):
                convert(*x)
            at = 2
            for kind, b, c in sched:
                if kind != "act" and at < len(work):
                    convert(*work[at])
                    at += 1
                if kind == "up":
                    s, o, rdy = conv.pop((kind, b, c))
                    need = [banks[i].freed for i in range(6)] if c == 0 else []

                    def up(e):
                        for q_ in range(4):
                            for sp_, (lo, hi) in enumerate(spans):
                                bi, p = ubank[q_, sp_]
                                for kk in range(2):
                                    k = 2 * c + kk
                                    st = c == 0 and kk == 0 and not (sp_ == 1 and q_ % 2 == 1)
                                    wh, wl = o[:, 0, kk, 128 * q_:128 * q_ + 128], o[:, 1, kk, 128 * q_:128 * q_ + 128]
                                    e.matmul(p, wh, HH[0][:, k, lo:hi], start=st, stop=False, skip_group_check=True)
                                    e.matmul(p, wh, HH[1][:, k, lo:hi], start=False, stop=False, skip_group_check=True)
                                    m = e.matmul(p, wl, HH[0][:, k, lo:hi], start=False, stop=c == 3 and kk == 1, skip_group_check=True)
                        return m
                    s.freed = updone[b] = pe.do(up, rdy, th, need)
                elif kind == "act":
                    gating = gated(b)
                    for _ in gating:
                        if b:
                            break
                else:
                    s, o, rdy = conv.pop((kind, b, c))
                    a = acs[b % 2]
                    for i in range(nt):
                        bk = drn.next()
                        tk = slice(128 * i, 128 * i + 128)

                        def down(e):
                            for kk in range(2):
                                ah, al = a.ap[:, 0, kk, tk], a.ap[:, 1, kk, tk]
                                e.matmul(bk.ap, ah, o[:, 0, kk, :], start=kk == 0, stop=False, skip_group_check=True)
                                e.matmul(bk.ap, ah, o[:, 1, kk, :], start=False, stop=False, skip_group_check=True)
                                m = e.matmul(bk.ap, al, o[:, 0, kk, :], start=False, stop=kk == 1, skip_group_check=True)
                            return m
                        t = pe.do(down, rdy, a.ready, bk.freed)
                        y = Y[:, i, 512 * c:512 * c + 512]
                        if b == 0:
                            bk.freed = dve.do(lambda e: e.tensor_copy(y, bk.ap), t)
                        else:
                            bk.freed = dve.do(lambda e: e.tensor_tensor(y, y, bk.ap, ALU.add), t, yprev[i, c])
                        yprev[i, c] = bk.freed
                        next(gating, None)
                        if b == 10 and c == 1:
                            add_normed(Y, i, GV, [gpt, yprev[i, 0], yprev[i, 1]])
                    s.freed = t
                    if c == 1:
                        a.freed = t
            barrier()
            dump_now(f"z{l}", X)
            AR, = claim(("AR", ARN, F32))

        outs = Slot(None, sem("s_out"))
        ot = sp.dma(outs, out.rearrange("o (i p) n -> p (o i) n", p=128), X3, barrier())
        sp.wait(ot, dumps)


_INS = ["x", "mem", "mem_norm_w", "norm_w", "w_memkv", "w_out", "w_in_a", "w_gate_up", "b_gate", "gla_norm_w",
        "w_in_b", "final_norm_w", "c_2", "ctx_2", "c_ctx_2", "w_mod_2", "b_mod_2", "norm_g_2", "w_in_2", "w_out_2",
        "hg_lb_logits_2", "hg_onorm_2", "da_lambda_2", "da_subln_2", "w_ffn_in_2", "w_ffn_out_2"]


def kernel(**inputs):
    import numpy as _np
    import concourse.bacc as _bacc
    from concourse import mybir as _mybir
    from concourse.bass_utils import run_bass_kernel_spmd as _run

    nc = _bacc.Bacc("TRN2", target_bir_lowering=False, num_devices=1)
    arrays, A = {}, {}
    for name in _INS:
        a = _np.ascontiguousarray(inputs[name])
        arrays[f"in_{name}"] = a
        A[name] = nc.dram_tensor(f"in_{name}", a.shape, _mybir.dt.from_np(a.dtype), kind="ExternalInput").ap()
    for name, a in zip(("k_const", "k_dft", "k_dftc", "k_mask"), shape_tables()):
        arrays[name] = a
        A[name] = nc.dram_tensor(name, a.shape, _mybir.dt.from_np(a.dtype), kind="ExternalInput").ap()
    out = nc.dram_tensor("out_0", (1, 512, 1024), _mybir.dt.float32, kind="ExternalOutput").ap()
    build(nc, A, out)
    r = _run(nc, [arrays], core_ids=[0])
    return r.results[0]["out_0"]
```
